# Optimizing a Trainium2 kernel written in Bass

```python
import jax
import jax.numpy as jnp
from jax import lax
import numpy as np

D_MODEL = 2048
BATCH = 1
SEQ = 256
DEPTH = 2

GRID_W = 64
CTX_LEN = 256

HEAD_DIM = 128
N_HEADS = D_MODEL // HEAD_DIM
N_KV_HEADS = N_HEADS // 4
GQA_GROUP = N_HEADS // N_KV_HEADS
ATTN_DIM = N_HEADS * HEAD_DIM
KV_DIM = N_KV_HEADS * HEAD_DIM
Q_BLOCK = 128
ATTN_SCALE = HEAD_DIM ** -0.5
ROPE_THETA = 10000.0
AXIS_DIM = HEAD_DIM // 2
ODD_IN = 2 * ATTN_DIM + 2 * KV_DIM

WIDTH_A = D_MODEL
WIDTH_B = D_MODEL
CONV_A_WIDTH = 31
CONV_B_WIDTH = 3
EVEN_IN = 3 * WIDTH_A + 4 * WIDTH_B
EVEN_SPLITS = [WIDTH_A, 2 * WIDTH_A, 3 * WIDTH_A, 3 * WIDTH_A + WIDTH_B,
               3 * WIDTH_A + 2 * WIDTH_B, 3 * WIDTH_A + 3 * WIDTH_B]

N_EVEN = (DEPTH + 1) // 2
N_ODD = DEPTH // 2
DEEPNORM_ALPHA = (2.0 * DEPTH) ** 0.25
DEEPNORM_BETA = (8.0 * DEPTH) ** -0.25
LN_EPS = 1e-5
RMS_EPS = 1e-6

kernel_name = 'hybrid_conv_gqa_prefix_dit_block'

def layer_norm(x, g, b):
    xf = x.astype(jnp.float32)
    mu = jnp.mean(xf, axis=-1, keepdims=True)
    var = jnp.mean(jnp.square(xf - mu), axis=-1, keepdims=True)
    return ((xf - mu) * lax.rsqrt(var + LN_EPS)).astype(x.dtype) * g + b

def rms_norm(x, g):
    xf = x.astype(jnp.float32)
    inv = lax.rsqrt(jnp.mean(jnp.square(xf), axis=-1, keepdims=True) + RMS_EPS)
    return (xf * inv).astype(x.dtype) * g

def adaln(cond, w, b):
    m = jax.nn.silu(cond) @ w + b
    return jnp.split(m, 3, axis=-1)

def depthwise_conv(u, w):
    pad = w.shape[0] // 2
    return lax.conv_general_dilated(u, w[:, None, :].astype(u.dtype), (1,), [(pad, pad)],
                                    dimension_numbers=('NWC', 'WIO', 'NWC'),
                                    feature_group_count=u.shape[-1])

def rope_tables(n_tokens, dtype):
    rows_n = n_tokens // GRID_W
    row = jnp.repeat(jnp.arange(rows_n, dtype=jnp.float32), GRID_W)
    col = jnp.tile(jnp.arange(GRID_W, dtype=jnp.float32), rows_n)
    inv_freq = ROPE_THETA ** (-jnp.arange(0, AXIS_DIM, 2, dtype=jnp.float32) / AXIS_DIM)
    ang_r = row[:, None] * inv_freq[None, :]
    ang_c = col[:, None] * inv_freq[None, :]
    return (jnp.cos(ang_r).astype(dtype), jnp.sin(ang_r).astype(dtype),
            jnp.cos(ang_c).astype(dtype), jnp.sin(ang_c).astype(dtype))

def rotate(xh, cos, sin):
    x1, x2 = jnp.split(xh, 2, axis=-1)
    cos = cos[None, :, None, :]
    sin = sin[None, :, None, :]
    return jnp.concatenate([x1 * cos - x2 * sin, x1 * sin + x2 * cos], axis=-1)

def apply_rope_2d(x, tabs):
    cos_r, sin_r, cos_c, sin_c = tabs
    x_row, x_col = jnp.split(x, 2, axis=-1)
    return jnp.concatenate([rotate(x_row, cos_r, sin_r), rotate(x_col, cos_c, sin_c)], axis=-1)

def gqa(q, k, v):
    b, nq = q.shape[:2]
    qg = q.reshape(b, nq, N_KV_HEADS, GQA_GROUP, HEAD_DIM)
    s = jnp.einsum('bqkgd,bnkd->bkgqn', qg, k, preferred_element_type=jnp.float32) * ATTN_SCALE
    p = jax.nn.softmax(s, axis=-1).astype(v.dtype)
    o = jnp.einsum('bkgqn,bnkd->bqkgd', p, v)
    return o.reshape(b, nq, ATTN_DIM)

def q_gate_proj(h, w_qg, qg):
    q, g = jnp.split(h @ w_qg, 2, axis=-1)
    q = rms_norm(q.reshape(h.shape[0], h.shape[1], N_HEADS, HEAD_DIM), qg)
    return q, g

def kv_proj(h, w_kv, kg):
    k, v = jnp.split(h @ w_kv, 2, axis=-1)
    k = rms_norm(k.reshape(h.shape[0], h.shape[1], N_KV_HEADS, HEAD_DIM), kg)
    v = v.reshape(h.shape[0], h.shape[1], N_KV_HEADS, HEAD_DIM)
    return k, v

def attn_mixer(h_lat, h_ctx, w_in, qg, kg, w_out, tabs, ctx_out):
    w_qg = w_in[:, :2 * ATTN_DIM]
    w_kv = w_in[:, 2 * ATTN_DIM:]
    b, s = h_lat.shape[:2]
    k_c, v_c = kv_proj(h_ctx, w_kv, kg)
    q_l, g_l = q_gate_proj(h_lat, w_qg, qg)
    k_l, v_l = kv_proj(h_lat, w_kv, kg)
    q_l = apply_rope_2d(q_l, tabs)
    k_l = apply_rope_2d(k_l, tabs)
    k_all = jnp.concatenate([k_c, k_l], axis=1)
    v_all = jnp.concatenate([v_c, v_l], axis=1)
    n_blocks = s // Q_BLOCK
    q_blocks = q_l.reshape(b, n_blocks, Q_BLOCK, N_HEADS, HEAD_DIM).swapaxes(0, 1)
    o = lax.map(lambda qb: gqa(qb, k_all, v_all), q_blocks)
    o = o.swapaxes(0, 1).reshape(b, s, ATTN_DIM)
    y_lat = (o * jax.nn.silu(g_l)) @ w_out
    if not ctx_out:
        return y_lat, None
    q_c, g_c = q_gate_proj(h_ctx, w_qg, qg)
    o_c = gqa(q_c, k_c, v_c)
    y_ctx = (o_c * jax.nn.silu(g_c)) @ w_out
    return y_lat, y_ctx

def conv_mixer(h, w_in, ca_w, ca_b, na_g, na_b, cb_w, w_out):
    a_val, a_glu, a_gate, b_x, b_b, b_c, b_gate = jnp.split(h @ w_in, EVEN_SPLITS, axis=-1)
    u = a_val * jax.nn.sigmoid(a_glu)
    u = depthwise_conv(u, ca_w) + ca_b
    u = jax.nn.silu(layer_norm(u, na_g, na_b))
    a_out = u * jax.nn.silu(a_gate)
    v = depthwise_conv(b_c * b_x, cb_w)
    b_out = b_b * v * jax.nn.silu(b_gate)
    return jnp.concatenate([a_out, b_out], axis=-1) @ w_out

def setup_inputs(seed: int = 0) -> dict:
    key = jax.random.key(seed)
    ks = jax.random.split(key, 19)

    def nrm(k, shape, s):
        return jax.random.normal(k, shape, jnp.float32) * s

    return {
        'x': nrm(ks[0], (BATCH, SEQ, D_MODEL), 1.0),
        'c': nrm(ks[1], (BATCH, D_MODEL), 1.0),
        'ctx': nrm(ks[2], (BATCH, CTX_LEN, D_MODEL), 1.0),
        'c_ctx': nrm(ks[3], (D_MODEL,), 1.0),
        'w_mod': nrm(ks[4], (DEPTH, D_MODEL, 3 * D_MODEL), D_MODEL ** -0.5),
        'b_mod': nrm(ks[5], (DEPTH, 3 * D_MODEL), 0.01),
        'post_ln_g': 1.0 + nrm(ks[6], (DEPTH, D_MODEL), 0.02),
        'post_ln_b': nrm(ks[7], (DEPTH, D_MODEL), 0.02),
        'w_in_e': nrm(ks[8], (N_EVEN, D_MODEL, EVEN_IN), D_MODEL ** -0.5),
        'conv_a_w': nrm(ks[9], (N_EVEN, CONV_A_WIDTH, WIDTH_A), CONV_A_WIDTH ** -0.5),
        'conv_a_b': nrm(ks[10], (N_EVEN, WIDTH_A), 0.02),
        'norm_a_g': 1.0 + nrm(ks[11], (N_EVEN, WIDTH_A), 0.02),
        'norm_a_b': nrm(ks[12], (N_EVEN, WIDTH_A), 0.02),
        'conv_b_w': nrm(ks[13], (N_EVEN, CONV_B_WIDTH, WIDTH_B), CONV_B_WIDTH ** -0.5),
        'w_out_e': nrm(ks[14], (N_EVEN, WIDTH_A + WIDTH_B, D_MODEL),
                       DEEPNORM_BETA * (WIDTH_A + WIDTH_B) ** -0.5),
        'w_in_o': nrm(ks[15], (N_ODD, D_MODEL, ODD_IN), D_MODEL ** -0.5),
        'q_norm_g': 1.0 + nrm(ks[16], (N_ODD, HEAD_DIM), 0.02),
        'k_norm_g': 1.0 + nrm(ks[17], (N_ODD, HEAD_DIM), 0.02),
        'w_out_o': nrm(ks[18], (N_ODD, ATTN_DIM, D_MODEL), DEEPNORM_BETA * ATTN_DIM ** -0.5),
    }

def reference(x, c, ctx, c_ctx, w_mod, b_mod, post_ln_g, post_ln_b, w_in_e, conv_a_w, conv_a_b,
              norm_a_g, norm_a_b, conv_b_w, w_out_e, w_in_o, q_norm_g, k_norm_g, w_out_o):
    tabs = rope_tables(x.shape[1], x.dtype)
    for layer in range(DEPTH):
        last = layer == DEPTH - 1
        is_attn = layer % 2 == 1
        i = layer // 2
        need_ctx = (not last) or is_attn
        shift, scale, gate = adaln(c, w_mod[layer], b_mod[layer])
        h_lat = x * (1 + scale[:, None, :]) + shift[:, None, :]
        if need_ctx:
            shift_c, scale_c, gate_c = adaln(c_ctx, w_mod[layer], b_mod[layer])
            h_ctx = ctx * (1 + scale_c) + shift_c
        if is_attn:
            y_lat, y_ctx = attn_mixer(h_lat, h_ctx, w_in_o[i], q_norm_g[i], k_norm_g[i],
                                      w_out_o[i], tabs, not last)
        else:
            y_lat = conv_mixer(h_lat, w_in_e[i], conv_a_w[i], conv_a_b[i], norm_a_g[i],
                               norm_a_b[i], conv_b_w[i], w_out_e[i])
            if not last:
                y_ctx = conv_mixer(h_ctx, w_in_e[i], conv_a_w[i], conv_a_b[i], norm_a_g[i],
                                   norm_a_b[i], conv_b_w[i], w_out_e[i])
        x = layer_norm(DEEPNORM_ALPHA * x + gate[:, None, :] * y_lat,
                       post_ln_g[layer], post_ln_b[layer])
        if not last:
            ctx = layer_norm(DEEPNORM_ALPHA * ctx + gate_c * y_ctx,
                             post_ln_g[layer], post_ln_b[layer])
    return x


_drawn_inputs = setup_inputs


def setup_inputs(seed=0):
    import zlib

    import numpy as np

    out = dict(_drawn_inputs(seed))
    spreads = {}
    factors = {'ctx': 5.81,
     'b_mod': 6.985,
     'conv_a_b': 8.0,
     'norm_a_g': 21.401,
     'norm_a_b': 36.65,
     'q_norm_g': 8.0,
     'k_norm_g': 8.0}
    for name, (base, spread) in spreads.items():
        noise = np.random.default_rng([zlib.crc32(name.encode()), seed]).standard_normal(out[name].shape)
        drawn = base * np.exp(spread * noise) if base else spread * noise
        out[name] = jnp.asarray(drawn.astype(out[name].dtype))
    for name, factor in factors.items():
        out[name] = (out[name] * factor).astype(out[name].dtype)
    return out
```

```python
from contextlib import ExitStack

import numpy as np

import concourse.bass as bass
from concourse import mybir

F32 = mybir.dt.float32
F32R = mybir.dt.float32r
ALU = mybir.AluOpType
ACT = mybir.ActivationFunctionType
AX_X = mybir.AxisListType.X

P = 128
D = 2048
KC = D // P
LAT = 256
TOK = 512
HEADS, KV, HD = 16, 4, 128
GROUP = HEADS // KV
TAPS_A, TAPS_B = 31, 3
PAD_A, PAD_B = TAPS_A // 2, TAPS_B // 2
ALPHA = (2.0 * 2) ** 0.25
LN_EPS, RMS_EPS = 1e-5, 1e-6
SCALE = HD ** -0.5
GRID_W = 64
ROPE_THETA = 10000.0

RING = 4
AHEAD = RING - 1

MOD_PAIR = 2 * KC
S_MOD0 = 0
MIX = 6 * 4 + KC
S_MIX = S_MOD0 + 4 * MOD_PAIR
S_AGATE = S_MIX + KC * MIX
S_OUT0 = S_AGATE + KC * 4
S_K = S_OUT0 + KC * 8
S_V = S_K + KC
S_Q0 = S_V + KC
S_ATT = S_Q0 + KC
ATT = KC + GROUP * 4
S_ATTL = S_ATT + (KV - 1) * ATT
S_OUT1 = S_ATTL + GROUP * 4
SLABS = S_OUT1 + KC * 4

_sizes = [("conv_a_w", KC * TAPS_A), ("conv_a_b", KC), ("norm_a_g", KC), ("norm_a_b", KC),
          ("conv_b_w", KC * TAPS_B), ("ln_g", 2 * KC), ("ln_b", 2 * KC), ("b_mod", 96), ("cond", 2 * KC)]
COL, _at = {}, 0
for _n, _s in _sizes:
    COL[_n] = (_at, _at + _s)
    _at += _s
PARAMS = _at
CONSTS = P + P + 2
ROPE = 2 * 2 * HD + 2 * HD


def lin(c, per=0, i=None):
    return c if i is None else i * per + c


def build(nc, weights, x_t, params, consts, rope, out_t):
    ctx = ExitStack()
    with ctx:
        def sb(name, shape, dt=F32):
            return ctx.enter_context(nc.sbuf_tensor(name, shape, dt))

        def sem(name):
            return ctx.enter_context(nc.semaphore(name))

        arena_at = -(-nc.sbuf_base // 32) * 32
        sb("arena", [P, KC * 2 * TOK])
        b_act = nc.alloc_sbuf_tensor_at("b_act", [P, KC, 2, TOK], F32R, offset=arena_at)
        att_at = arena_at + KC * TOK * 4
        k_t = nc.alloc_sbuf_tensor_at("k_t", [P, KV, TOK], F32, offset=att_at)
        v_tok = nc.alloc_sbuf_tensor_at("v_tok", [P, 4, KV * HD], F32, offset=att_at + 8192)
        q_tok = nc.alloc_sbuf_tensor_at("q_tok", [P, 2, GROUP * HD], F32, offset=att_at + 16384)
        q_t = nc.alloc_sbuf_tensor_at("q_t", [P, GROUP, LAT], F32, offset=att_at + 20480)
        prob = nc.alloc_sbuf_tensor_at("prob", [P, 2, TOK], F32, offset=att_at + 24576)
        prob_t = nc.alloc_sbuf_tensor_at("prob_t", [P, 4, LAT], F32, offset=att_at + 28672)
        k_tok = nc.alloc_sbuf_tensor_at("k_tok", [P, 4, KV * HD], F32, offset=att_at + 24576)
        b_flat = b_act[:, :, :, :].rearrange("p k s t -> p (k s t)")
        o_act = b_flat[:, 0:KC * 2 * LAT].rearrange("p (k s t) -> p k s t", k=KC, s=2)

        h = sb("h", [P, KC, 2, TOK], F32R)
        u = sb("u", [P, KC, TOK])
        w_raw = sb("w_raw", [P, RING, TOK])
        w_hi = sb("w_hi", [P, RING, TOK], F32R)
        w_lo = sb("w_lo", [P, RING, TOK], F32R)
        tmp = sb("tmp", [P, 4, TOK])
        x_in = sb("x_in", [P, 2, TOK])
        pads = sb("pads", [P, 2 * (LAT + 2 * PAD_A) + 2 * (LAT + 2 * PAD_B)])
        par = sb("par", [P, PARAMS])
        con = sb("con", [P, CONSTS])
        mod = sb("mod", [P, 96, 2])
        c4 = sb("c4", [P, 4 * KC + P], F32R)
        small = sb("small", [P, 64])
        v_stage = par[:, 0:4 * HD].rearrange("p (t d) -> p t d", t=4)

        t1, t2, t3, t4 = (tmp[:, n, :] for n in range(4))
        mod_row = t4
        n_pad_a = 2 * (LAT + 2 * PAD_A)
        pad_a = pads[:, 0:n_pad_a].rearrange("p (s t) -> p s t", s=2)
        pad_b = pads[:, n_pad_a:n_pad_a + 2 * (LAT + 2 * PAD_B)].rearrange("p (s t) -> p s t", s=2)
        rope_cos = pads[:, 0:2 * HD].rearrange("p (t d) -> p t d", t=2)
        rope_sin = pads[:, 2 * HD:4 * HD].rearrange("p (t d) -> p t d", t=2)
        gains = pads[:, 4 * HD:6 * HD].rearrange("p (q d) -> p q d", q=2)

        def column(name, inner=1):
            a, b = COL[name]
            return par[:, a:b]

        conv_a_w, conv_a_b = column("conv_a_w"), column("conv_a_b")
        norm_a_g, norm_a_b = column("norm_a_g"), column("norm_a_b")
        conv_b_w, ln_g, ln_b = column("conv_b_w"), column("ln_g"), column("ln_b")
        b_mod = column("b_mod")
        cond = column("cond").rearrange("p (k c) -> p k c", c=2)
        ones, ident, sel = con[:, 0:P], con[:, P:2 * P], con[0:4, 2 * P:2 * P + 2]
        cond_s = small[:, 0:2 * KC].rearrange("p (k c) -> p k c", c=2)
        neg_half = small[:, 32:40]
        sumsq = small[:, 40:48]
        negmax = small[:, 48:50]
        rowsum = small[:, 50:52]
        rowinv = small[:, 52:54]

        banks = ctx.enter_context(nc.psum_tensor("banks", [P, 8, TOK], F32))
        VAL, GLU, BX, BC, BB, MOD, SUM, SQS = range(8)
        BG = BX
        G, Q, S, PT, PV = 0, 1, 3, 5, 7

        params_in = sem("params_in")
        consts_in = sem("consts_in")
        rope_in = sem("rope_in")
        xall_in = sem("xall_in")
        slab_landed = [sem(f"slab_landed{s}") for s in range(RING)]
        x_landed = [sem(f"x_landed{s}") for s in range(2)]
        hi_ready = sem("hi_ready")
        lo_ready = sem("lo_ready")
        slab_used = sem("slab_used")
        cleared = sem("cleared")
        cond_sig = sem("cond_sig")
        cond_mul = sem("cond_mul")
        cond_hi = sem("cond_hi")
        cond_lo = sem("cond_lo")
        mod_row_ready = sem("mod_row_ready")
        mod_cols_ready = sem("mod_cols_ready")
        mod_ready = sem("mod_ready")
        h_mod = sem("h_mod")
        h_hi = sem("h_hi")
        h_lo = sem("h_lo")
        glu_sig = sem("glu_sig")
        a_gated = sem("a_gated")
        bx_copied = sem("bx_copied")
        b_gated = sem("b_gated")
        conv_tap = sem("conv_tap")
        b_tap = sem("b_tap")
        b_mix = sem("b_mix")
        b_hi = sem("b_hi")
        conv_sq = sem("conv_sq")
        a_stats = sem("a_stats")
        ln_copy = sem("ln_copy")
        ln_sums = sem("ln_sums")
        ln_step = sem("ln_step")
        ln_sqrt = sem("ln_sqrt")
        an_step = sem("an_step")
        an_affine = sem("an_affine")
        ag_sig = sem("ag_sig")
        ag_mul = sem("ag_mul")
        act_hi = sem("act_hi")
        act_lo = sem("act_lo")
        x_scaled = sem("x_scaled")
        res_step = sem("res_step")
        res_sq = sem("res_sq")
        res_stats = sem("res_stats")
        n1_step = sem("n1_step")
        n1_affine = sem("n1_affine")
        h1_mod = sem("h1_mod")
        h1_hi = sem("h1_hi")
        h1_lo = sem("h1_lo")
        scale1 = sem("scale1")
        k_copied = sem("k_copied")
        v_copied = sem("v_copied")
        q_copied = sem("q_copied")
        prep = sem("prep")
        prep_pow = sem("prep_pow")
        k_transposed = sem("k_transposed")
        kt_ready = sem("kt_ready")
        q_transposed = sem("q_transposed")
        qt_ready = sem("qt_ready")
        v_staged = sem("v_staged")
        qk_done = sem("qk_done")
        max_step = sem("max_step")
        p_exp = sem("p_exp")
        p_norm_inv = sem("p_norm_inv")
        p_norm = sem("p_norm")
        pt_done = sem("pt_done")
        pt_copied = sem("pt_copied")
        pv_done = sem("pv_done")
        g_part = sem("g_part")
        g_sum = sem("g_sum")
        g_exp = sem("g_exp")
        g_inv = sem("g_inv")
        o_mul = sem("o_mul")
        o_hi = sem("o_hi")
        o_lo = sem("o_lo")
        y_part = sem("y_part")
        y_step = sem("y_step")
        y_sq = sem("y_sq")
        y_stats = sem("y_stats")
        fin_step = sem("fin_step")
        fin_ready = sem("fin_ready")
        out_sem = sem("out_sem")

        PREP = 12

        def chunk(buf, j, jn):
            if j is None:
                return buf[:, jn, :]
            return buf[:, bass.ds(j[1] * j[0] + jn, 1), :].rearrange("p o t -> p (o t)")

        def per_chunk(col, j, jn):
            return col[:, jn:jn + 1] if j is None else col[:, bass.ds(j[1] * j[0] + jn, 1)]

        def rms_power(pool, n):
            pool.wait_ge(prep, PREP * n + 3)
            nc.gpsimd.tensor_tensor(sumsq, sumsq, neg_half, ALU.pow).then_inc(prep_pow, 1)

        def stage_v(pool, n):
            if n == 0:
                pool.wait_ge(v_copied, 4)
            else:
                pool.wait_ge(pv_done, GROUP * n)
            nc.gpsimd.tensor_copy(v_stage[:, :, :], v_tok[:, :, n * HD:(n + 1) * HD]).then_inc(v_staged, 1)

        block = ctx.enter_context(nc.Block())

        @block.sync
        def _(sp):
            def load_slab(base, k, per=0, i=None):
                p, slot = base + k, (base + k) % RING
                if p >= RING:
                    sp.wait_ge(lo_ready, lin(p - RING + 1, per, i))
                src = weights[p] if i is None else weights[bass.ds(i * per + p, 1)].rearrange("o p n -> p (o n)")
                sp.dma_start(w_raw[:, slot, :], src).then_inc(slab_landed[slot], 16)

            sp.dma_start(par[:, :], params).then_inc(params_in, 16)
            sp.dma_start(con[:, :], consts).then_inc(consts_in, 16)
            for k in range(RING):
                load_slab(0, k)
            sp.dma_start(u[:, :, :], x_t).then_inc(xall_in, 16)
            with sp.Fori(0, (S_OUT0 - RING) // RING) as i:
                for k in range(RING):
                    load_slab(RING, k, RING, i)

            def load_x(j_slot, pair, i=None):
                if i is not None:
                    sp.wait_ge(x_scaled, i * 2 + j_slot - 1)
                    src = x_t[:, bass.ds(i * 2 + j_slot, 1), :].rearrange("p o n -> p (o n)")
                else:
                    src = x_t[:, 2 * pair + j_slot, :]
                sp.dma_start(x_in[:, j_slot, :], src).then_inc(x_landed[j_slot], 16)

            def out0_pair(pair, i=None):
                for s in range(2):
                    load_x(s, pair, i)
                    for k in range(8):
                        load_slab(S_OUT0 + (16 * pair if i is None else 0), 8 * s + k, 16, i)

            out0_pair(0)
            with sp.Fori(1, KC // 2) as i:
                out0_pair(0, i)
            sp.wait_ge(b_tap, TAPS_B * KC)
            sp.wait_ge(conv_tap, (TAPS_A + 1) * KC)
            sp.dma_start(pads[:, 0:ROPE], rope).then_inc(rope_in, 16)
            with sp.Fori(0, (SLABS - S_K) // RING) as i:
                for k in range(RING):
                    load_slab(S_K, k, RING, i)
            for j in range(KC):
                sp.wait_ge(fin_ready, j + 1)
                sp.dma_start(out_t[:, j, :], u[:, j, 0:LAT]).then_inc(out_sem, 16)
            sp.wait_ge(out_sem, 16 * KC)

        @block.gpsimd
        def _(pool):
            for n in range(2):
                rms_power(pool, n)
            rms_power(pool, 2)
            stage_v(pool, 0)
            for n in range(1, KV):
                rms_power(pool, 2 + n)
                stage_v(pool, n)

        @block.tensor
        def _(pe):
            def slab(base, k, per=0, i=None):
                pe.wait_ge(lo_ready, lin(base + k + 1, per, i))
                return (base + k) % RING

            def job_slab(base, k, bank, act, first, last, per=0, i=None):
                s = slab(base, k, per, i)
                for kk in range(4):
                    blk = slice(kk * P, (kk + 1) * P)
                    for n, (w, half) in enumerate(((w_hi, 0), (w_hi, 1), (w_lo, 0))):
                        mm = nc.tensor.matmul(banks[:, bank, :], w[:, s, blk], act(kk, half),
                                              start=first and kk == 0 and n == 0,
                                              stop=last and kk == 3 and n == 2)
                mm.then_inc(slab_used, 1)

            def job(base, bank, per=0, i=None, before=None):
                for k in range(4):
                    job_slab(base, k, bank, lambda kk, half: h[:, 4 * k + kk, half, :], k == 0, k == 3, per, i)

            def mod_slab(base, k, kc, bank, per=0, i=None):
                s = slab(base, k, per, i)
                for n, w in enumerate((w_hi, w_lo)):
                    mm = nc.tensor.matmul(banks[:, bank, :], c4[:, 4 * kc:4 * kc + P], w[:, s, :],
                                          start=kc == 0 and n == 0, stop=kc == KC - 1 and n == 1)
                mm.then_inc(slab_used, 1)

            def mod_columns(bank, n):
                pe.wait_ge(mod_row_ready, n)
                for q in range(4):
                    mm = nc.tensor.matmul(banks[:, bank, 2 * q:2 * q + 2], mod_row[0:4, q * P:(q + 1) * P], sel,
                                          start=True, stop=True)
                mm.then_inc(mod_cols_ready, 1)

            def ln_totals(r, width):
                pe.wait_ge(ln_copy, 2 * r + 2)
                for t, bank in ((t1, SUM), (t2, SQS)):
                    mm = nc.tensor.matmul(banks[:, bank, 0:width], ones, t[:, 0:width], start=True, stop=True)
                mm.then_inc(ln_sums, 1)

            pe.wait_ge(consts_in, 16)
            pe.wait_ge(cond_lo, 1)
            with pe.Fori(0, 4) as i:
                pe.wait_ge(mod_ready, i * 2 + 2)
                for k in range(KC):
                    mod_slab(S_MOD0, k, k, VAL, MOD_PAIR, i)
                for k in range(KC):
                    mod_slab(S_MOD0 + KC, k, k, GLU, MOD_PAIR, i)
                    if k == 4:
                        mod_columns(VAL, i * 2 + 1)
                mod_columns(GLU, i * 2 + 2)
            pe.wait_ge(h_lo, KC)
            pe.wait_ge(mod_ready, 2 + 8)
            with pe.Fori(0, KC) as i:
                def part(n, bank, mods):
                    for k in range(4):
                        at = 8 * n + 2 * k if mods else 32 + 4 * (n - 4) + k
                        job_slab(S_MIX + at, 0, bank, lambda kk, half: h[:, 4 * k + kk, half, :],
                                 k == 0, k == 3, MIX, i)
                        if mods:
                            mod_slab(S_MIX + at + 1, 0, 4 * n + k, MOD, MIX, i)
                pe.wait_ge(a_gated, i + 1)
                pe.wait_ge(mod_ready, i + 2 + 8)
                part(0, VAL, True)
                part(1, GLU, True)
                pe.wait_ge(b_mix, i * 4 + 2)
                part(2, BX, True)
                pe.wait_ge(b_gated, i + 1)
                part(3, BC, True)
                pe.wait_ge(b_mix, i * 4 + 1)
                part(4, BB, False)
                mod_columns(MOD, i + 9)
                pe.wait_ge(bx_copied, i + 1)
                part(5, BG, False)

            def agate_pair(base, per=0, i=None):
                for s in range(2):
                    if i is not None:
                        pe.wait_ge(ag_mul, i * 4 + 2 * s - 3)
                    elif s == 0:
                        pe.wait_ge(a_gated, KC + 1)
                    for k in range(4):
                        job_slab(base + 4 * s, k, s, lambda kk, half: h[:, 4 * k + kk, half, :],
                                 k == 0, k == 3, per, i)
                        if i is None and s == 0 and k == 0:
                            ln_totals(0, TOK)
            agate_pair(S_AGATE)
            with pe.Fori(1, KC // 2) as i:
                agate_pair(S_AGATE, 8, i)

            def out0_pair(base, per=0, i=None):
                for s in range(2):
                    if i is not None:
                        pe.wait_ge(res_step, i * 4 + 2 * s - 2)
                    elif s == 0:
                        pe.wait_ge(b_hi, KC)
                        pe.wait_ge(b_mix, 4 * KC + 4)
                        pe.wait_ge(b_gated, KC + 1)
                    for k in range(8):
                        act = (lambda kk, half: b_act[:, 4 * k + kk, half, :]) if k < 4 else \
                              (lambda kk, half: h[:, 4 * (k - 4) + kk, half, :])
                        if i is None and s == 0 and k >= 4:
                            pe.wait_ge(act_lo, 4 * (k - 3))
                        job_slab(base + 8 * s, k, BX + s, act, k == 0, k == 7, per, i)
            out0_pair(S_OUT0)
            with pe.Fori(1, KC // 2) as i:
                out0_pair(S_OUT0, 16, i)
            ln_totals(1, TOK)

            def token_slab(base, k, kc, bank0, tiles, per=0, i=None):
                s = slab(base, k, per, i)
                for t in range(tiles):
                    tok = slice(t * P, (t + 1) * P)
                    for n, (half, w) in enumerate(((0, w_hi), (0, w_lo), (1, w_hi))):
                        mm = nc.tensor.matmul(banks[:, bank0 + t, :], h[:, kc, half, tok], w[:, s, :],
                                              start=kc == 0 and n == 0, stop=kc == KC - 1 and n == 2)
                mm.then_inc(slab_used, 1)

            pe.wait_ge(res_step, 2 * KC)
            for kc in range(KC):
                pe.wait_ge(h1_lo, kc + 1)
                token_slab(S_K, kc, kc, 0, 4)
            pe.wait_ge(n1_step, 1)
            for kc in range(KC):
                token_slab(S_V, kc, kc, 4, 4)
            for n in range(2):
                pe.wait_ge(prep, PREP * (n + 1))
                if n == 0:
                    pe.wait_ge(k_copied, 4)
                for t in range(2):
                    for kv in range(KV):
                        mm = nc.tensor.transpose(banks[:, 2 * n + t, kv * P:(kv + 1) * P],
                                                 k_tok[:, 2 * n + t, kv * HD:(kv + 1) * HD], ident)
                mm.then_inc(k_transposed, 1)
            pe.wait_ge(v_copied, 4)
            for kc in range(KC):
                token_slab(S_Q0, kc, kc, 4, 2)

            def transpose_q(n_expr_prep, bank0):
                pe.wait_ge(prep, n_expr_prep)
                for t in range(2):
                    for g in range(GROUP):
                        mm = nc.tensor.transpose(banks[:, bank0 + t, g * P:(g + 1) * P],
                                                 q_tok[:, t, g * HD:(g + 1) * HD], ident)
                mm.then_inc(q_transposed, 1)

            pe.wait_ge(kt_ready, 4)
            transpose_q(PREP * 3, Q)

            def scores(n, g):
                keys = k_t[:, n, :] if isinstance(n, int) else k_t[:, bass.ds(n, 1), :].rearrange("p o t -> p (o t)")
                for t in range(2):
                    mm = nc.tensor.matmul(banks[:, S + t, :], q_t[:, g, t * P:(t + 1) * P], keys,
                                          start=True, stop=True)
                mm.then_inc(qk_done, 1)

            def gate_slab(base, k, kk0, per, i):
                s = slab(base, k, per, i)
                for kk in range(4):
                    kc, blk = kk0 + kk, slice(kk * P, (kk + 1) * P)
                    nc.tensor.matmul(banks[:, G, :], w_hi[:, s, blk], h[:, kc, :, 0:LAT],
                                     start=kc == 0, stop=False)
                    mm = nc.tensor.matmul(banks[:, G, 0:LAT], w_lo[:, s, blk], h[:, kc, 0, 0:LAT],
                                          start=False, stop=kc == KC - 1)
                mm.then_inc(slab_used, 1)

            def attend(base, n, last, per=0, i=None):
                head = lambda c, k=1: lin(c, GROUP * k, i)
                pe.wait_ge(qt_ready, lin(2 if i is not None else 2 * KV, 2, i))
                scores(n, 0)
                k = 0
                for g in range(GROUP):
                    hd = g if i is not None else g + GROUP * (KV - 1)
                    if not last and g < 2:
                        for q in range(8):
                            token_slab(base, k, 8 * g + q, Q, 2, per, i)
                            k += 1
                    pe.wait_ge(g_sum, head(hd + 1))
                    for q in range(4):
                        gate_slab(base, k, 4 * q, per, i)
                        k += 1
                    pe.wait_ge(p_norm, head(2 * hd + 2, 2))
                    for t in range(2):
                        for c in range(4):
                            mm = nc.tensor.transpose(banks[:, PT + t, c * P:(c + 1) * P],
                                                     prob[:, t, c * P:(c + 1) * P], ident)
                    mm.then_inc(pt_done, 1)
                    if g + 1 < GROUP:
                        scores(n, g + 1)
                    elif not last:
                        transpose_q(lin(PREP * 4, PREP, i), Q)
                    pe.wait_ge(pt_copied, head(2 * hd + 2, 2))
                    pe.wait_ge(o_mul, head(hd + 1))
                    if g == 0:
                        pe.wait_ge(v_staged, lin(1 if i is not None else KV, 1, i))
                    for c in range(4):
                        mm = nc.tensor.matmul(banks[:, PV, 0:LAT], v_stage[:, c, :], prob_t[:, c, :],
                                              start=c == 0, stop=c == 3)
                    mm.then_inc(pv_done, 1)

            with pe.Fori(0, KV - 1) as i:
                attend(S_ATT, i, False, ATT, i)
            attend(S_ATTL, KV - 1, True)

            def out1_pair(base, per=0, i=None, first=False):
                for s in range(2):
                    if first and s == 0:
                        pe.wait_ge(o_lo, HEADS + 1)
                        pe.wait_ge(g_sum, HEADS + 1)
                    elif not first:
                        pe.wait_ge(y_step, i * 4 + 2 * s - 3 if not isinstance(i, int) else 4 * i + 2 * s - 3)
                    for k in range(4):
                        sl = slab(base + 4 * s, k, per, None if isinstance(i, int) else i)
                        for kk in range(4):
                            kc, blk = 4 * k + kk, slice(kk * P, (kk + 1) * P)
                            nc.tensor.matmul(banks[:, s, :], w_hi[:, sl, blk], o_act[:, kc, :, :],
                                             start=kc == 0, stop=False)
                            mm = nc.tensor.matmul(banks[:, s, 0:LAT], w_lo[:, sl, blk], o_act[:, kc, 0, :],
                                                  start=False, stop=kc == KC - 1)
                        mm.then_inc(slab_used, 1)
            out1_pair(S_OUT1, first=True)
            with pe.Fori(1, KC // 2 - 1) as i:
                out1_pair(S_OUT1, 8, i)
            out1_pair(S_OUT1 + 8 * (KC // 2 - 1), 0, KC // 2 - 1)
            ln_totals(2, LAT)

        @block.scalar
        def _(act):
            def head_of(base, k, per=0, i=None):
                p = base + k + AHEAD
                if p >= SLABS:
                    return
                slot = p % RING
                act.wait_ge(slab_landed[slot], lin(16 * (p // RING + 1), 16 * per // RING, i))
                if p >= RING:
                    act.wait_ge(slab_used, lin(p - RING + 1, per, i))
                nc.scalar.activation(w_hi[:, slot, :], w_raw[:, slot, :], ACT.Copy).then_inc(hi_ready, 1)

            def copy_mod_row(bank, used, n):
                act.wait_ge(slab_used, used)
                act.wait_ge(mod_cols_ready, n)
                nc.scalar.activation(mod_row[0:4, :], banks[0:4, bank, :], ACT.Copy).then_inc(mod_row_ready, 1)

            def ln_root(r, width):
                act.wait_ge(ln_step, 5 * r + 4)
                nc.scalar.activation(t2[:, 0:width], t2[:, 0:width], ACT.Sqrt).then_inc(ln_sqrt, 1)

            act.wait_ge(params_in, 16)
            nc.scalar.activation(cond_s, cond, ACT.Sigmoid).then_inc(cond_sig, 1)
            act.wait_ge(cond_mul, 1)
            c4v = c4[:, 0:4 * KC].rearrange("p (k c s) -> p k c s", c=2, s=2)
            nc.scalar.activation(c4v[:, :, :, 0], cond_s, ACT.Copy).then_inc(cond_hi, 1)
            for k in range(-AHEAD, 0):
                head_of(0, k)
            with act.Fori(0, 4) as i:
                for k in range(MOD_PAIR):
                    head_of(S_MOD0, k, MOD_PAIR, i)
                    if k == KC:
                        copy_mod_row(VAL, i * MOD_PAIR + KC, i * 2 + 1)
                copy_mod_row(GLU, i * MOD_PAIR + MOD_PAIR, i * 2 + 2)
                for q in range(4):
                    act.wait_ge(h_mod, i * 8 + 2 * q + 2)
                    nc.scalar.activation(h[:, bass.ds(i * 4 + q, 1), 0, :].rearrange("p o t -> p (o t)"),
                                         tmp[:, q % 2, :], ACT.Copy).then_inc(h_hi, 1)

            with act.Fori(0, KC) as i:
                row = lambda buf: buf[:, bass.ds(i, 1), :].rearrange("p o t -> p (o t)")
                for k in range(MIX):
                    head_of(S_MIX, k, MIX, i)
                    if k == 14:
                        act.wait_ge(slab_used, i * MIX + S_MIX + 15)
                        act.wait_ge(b_mix, i * 4 + 3)
                        nc.scalar.activation(t2, banks[:, GLU, :], ACT.Sigmoid).then_inc(glu_sig, 1)
                    if k == 22:
                        act.wait_ge(slab_used, i * MIX + S_MIX + 23)
                        act.wait_ge(b_mix, i * 4 + 4)
                        nc.scalar.activation(t1, banks[:, BX, :], ACT.Copy).then_inc(bx_copied, 1)
                    if k == 31:
                        copy_mod_row(MOD, i * MIX + S_MIX + 32, i + 9)
                act.wait_ge(slab_used, i * MIX + S_MIX + MIX)
                act.wait_ge(a_gated, i + 2)
                nc.scalar.activation(t2, banks[:, BG, :], ACT.Sigmoid).then_inc(glu_sig, 1)
                act.wait_ge(conv_tap, i * (TAPS_A + 1) + TAPS_A + 1)
                nc.scalar.activation(t3, row(u), ACT.Square).then_inc(conv_sq, 1)
                act.wait_ge(b_mix, i * 4 + 4 + 3)
                nc.scalar.activation(b_act[:, bass.ds(i, 1), 0, :].rearrange("p o t -> p (o t)"), t1,
                                     ACT.Copy).then_inc(b_hi, 1)

            def norm_a_affine(j, jn):
                act.wait_ge(an_step, lin(3 * jn + 2, 6, None if j is None else j[1]))
                uj = chunk(u, j, jn)
                g = per_chunk(norm_a_g, j, jn)
                b = per_chunk(norm_a_b, j, jn)
                nc.scalar.activation(t3, uj, ACT.Sigmoid, scale=g, bias=b).then_inc(an_affine, 1)
                nc.scalar.activation(uj, uj, ACT.Identity, scale=g, bias=b).then_inc(an_affine, 1)

            def agate_act(base, per=0, i=None):
                for s in range(2):
                    for k in range(4):
                        head_of(base + 4 * s, k, per, i)
                        if i is None and s == 0 and k == 0:
                            ln_root(0, TOK)
                        if k == 0:
                            norm_a_affine(None if i is None else (2, i), s)
                    act.wait_ge(slab_used, lin(base + 4 * s + 4, per, i))
                    if i is not None or s:
                        act.wait_ge(ag_mul, lin(2 * s, 4, i))
                    else:
                        act.wait_ge(mod_cols_ready, 25)
                    nc.scalar.activation(t4, banks[:, s, :], ACT.Sigmoid).then_inc(ag_sig, 1)

            agate_act(S_AGATE)
            with act.Fori(1, KC // 2) as i:
                agate_act(S_AGATE, 8, i)

            def out0_act(base, per=0, i=None):
                for s in range(2):
                    for k in range(8):
                        head_of(base + 8 * s, k, per, i)
                        if i is None and s == 0 and k < 4:
                            if k == 0:
                                act.wait_ge(slab_used, S_OUT0)
                                act.wait_ge(ag_mul, 2 * KC)
                            for c in range(4 * k, 4 * k + 4):
                                nc.scalar.activation(h[:, c, 0, :], u[:, c, :], ACT.Copy).then_inc(act_hi, 1)
                    act.wait_ge(x_landed[s], lin(16, 16, i))
                    if i is not None or s:
                        act.wait_ge(res_step, lin(2 * s, 4, i))
                    nc.scalar.activation(t3, x_in[:, s, :], ACT.Copy, scale=ALPHA).then_inc(x_scaled, 1)
                    act.wait_ge(res_step, lin(2 * s + 2, 4, i))
                    if i is not None or s:
                        act.wait_ge(res_stats, lin(2 * s, 4, i))
                    nc.scalar.activation(t4, chunk(u, None if i is None else (2, i), s),
                                         ACT.Square).then_inc(res_sq, 1)

            out0_act(S_OUT0)
            with act.Fori(1, KC // 2) as i:
                out0_act(S_OUT0, 16, i)
            ln_root(1, TOK)
            for c in range(KC + 1):
                if c < KC:
                    act.wait_ge(n1_step, 2 * c + 3)
                    nc.scalar.activation(u[:, c, :], u[:, c, :], ACT.Identity, scale=ln_g[:, c:c + 1],
                                         bias=ln_b[:, c:c + 1]).then_inc(n1_affine, 1)
                if c:
                    act.wait_ge(h1_mod, 2 * c)
                    nc.scalar.activation(h[:, c - 1, 0, :], tmp[:, 2 + (c - 1) % 2, :], ACT.Copy).then_inc(h1_hi, 1)
                    head_of(S_K, c - 1)
            for kc in range(KC):
                head_of(S_V, kc)
                if kc == 0:
                    act.wait_ge(slab_used, S_V)
                if kc < 4:
                    nc.scalar.activation(k_tok[:, kc, :], banks[:, kc, :], ACT.Copy).then_inc(k_copied, 1)
            act.wait_ge(slab_used, S_Q0)
            for t in range(4):
                nc.scalar.activation(v_tok[:, t, :], banks[:, 4 + t, :], ACT.Copy).then_inc(v_copied, 1)

            def copy_transposed(dst, bank0, tile0, ready):
                for t in range(2):
                    tok = slice((tile0 + t) * P, (tile0 + t + 1) * P)
                    nc.scalar.activation(dst[:, :, tok], banks[:, bank0 + t, :].rearrange("p (g t) -> p g t", g=4),
                                         ACT.Copy).then_inc(ready, 1)

            for kc in range(KC):
                head_of(S_Q0, kc)
                if kc in (0, 1):
                    act.wait_ge(k_transposed, kc + 1)
                    copy_transposed(k_t, 2 * kc, 2 * kc, kt_ready)
            act.wait_ge(slab_used, S_ATT)
            for t in range(2):
                nc.scalar.activation(q_tok[:, t, :], banks[:, 4 + t, :], ACT.Copy).then_inc(q_copied, 1)
            act.wait_ge(q_transposed, 1)
            copy_transposed(q_t, Q, 0, qt_ready)

            def attend_act(base, last, per=0, i=None):
                head = lambda c, k=1: lin(c, GROUP * k, i)
                k = 0
                for g in range(GROUP):
                    hd = g if i is not None else g + GROUP * (KV - 1)
                    slabs = 12 if not last and g < 2 else 4
                    for m in range(slabs):
                        head_of(base, k, per, i)
                        k += 1
                        if m == 0:
                            for t in range(2):
                                if t == 0:
                                    act.wait_ge(max_step, head(2 * hd + 2, 2))
                                nc.scalar.activation(prob[:, t, :], banks[:, S + t, :], ACT.Exp, scale=SCALE,
                                                     bias=negmax[:, t:t + 1],
                                                     accum_out=rowsum[:, t:t + 1]).then_inc(p_exp, 1)
                            if hd or i is not None:
                                if g:
                                    o_head(hd - 1, i)
                        if not last and g == 1 and m == 8:
                            act.wait_ge(slab_used, lin(base + 20, per, i))
                            for t in range(2):
                                nc.scalar.activation(q_tok[:, t, :], banks[:, Q + t, :],
                                                     ACT.Copy).then_inc(q_copied, 1)
                    act.wait_ge(pt_done, head(hd + 1))
                    for t in range(2):
                        nc.scalar.activation(prob_t[:, :, t * P:(t + 1) * P],
                                             banks[:, PT + t, :].rearrange("p (c t) -> p c t", c=4),
                                             ACT.Copy).then_inc(pt_copied, 1)
                    act.wait_ge(slab_used, lin(base + k, per, i))
                    act.wait_ge(o_lo, head(hd + 1))
                    nc.scalar.activation(t1[:, 0:LAT], banks[:, G, LAT:TOK], ACT.Copy).then_inc(g_part, 1)
                    act.wait_ge(g_sum, head(hd + 2))
                    nc.scalar.activation(t2[:, 0:LAT], t1[:, 0:LAT], ACT.Exp, scale=-1.0).then_inc(g_exp, 1)
                if not last:
                    act.wait_ge(q_transposed, lin(2, 1, i))
                    copy_transposed(q_t, Q, 0, qt_ready)
                o_head(GROUP - 1 if i is not None else HEADS - 1, i)

            def o_head(hd, i):
                act.wait_ge(o_mul, lin(hd + 2, GROUP, i))
                at = bass.ds(i * GROUP + hd, 1) if i is not None else slice(hd, hd + 1)
                nc.scalar.activation(o_act[:, at, 0, :].rearrange("p o t -> p (o t)"), t1[:, 0:LAT],
                                     ACT.Copy).then_inc(o_hi, 1)

            with act.Fori(0, KV - 1) as i:
                attend_act(S_ATT, False, ATT, i)
            attend_act(S_ATTL, True)

            def out1_act(base, pair, per=0, i=None):
                j = None if i is None else (2, i)
                for s in range(2):
                    for k in range(4):
                        head_of(base + 4 * s, k, per, i)
                    act.wait_ge(slab_used, lin(base + 4 * s + 4, per, i))
                    jn = 2 * pair + s
                    if i is not None or jn:
                        act.wait_ge(y_step, lin(2 * jn - 1 if i is None else 2 * s - 1, 4, i))
                    gate = mod[:, bass.ds(i * 2 + 80 + s, 1), 0] if i is not None else mod[:, 80 + jn:81 + jn, 0]
                    nc.scalar.activation(t1[:, 0:LAT], banks[:, s, LAT:TOK], ACT.Identity,
                                         scale=gate).then_inc(y_part, 1)
                    act.wait_ge(y_step, lin(2 * jn + 2 if i is None else 2 * s + 2, 4, i))
                    if i is not None or jn:
                        act.wait_ge(y_stats, lin(2 * jn if i is None else 2 * s, 4, i))
                    nc.scalar.activation(t4[:, 0:LAT], chunk(u, j, s if i is not None else jn)[:, 0:LAT],
                                         ACT.Square).then_inc(y_sq, 1)
            out1_act(S_OUT1, 0)
            with act.Fori(1, KC // 2 - 1) as i:
                out1_act(S_OUT1, 0, 8, i)
            out1_act(S_OUT1 + 8 * (KC // 2 - 1), KC // 2 - 1)
            ln_root(2, LAT)
            for c in range(KC):
                act.wait_ge(fin_step, 2 * c + 2)
                nc.scalar.activation(u[:, c, 0:LAT], u[:, c, 0:LAT], ACT.Identity, scale=ln_g[:, KC + c:KC + c + 1],
                                     bias=ln_b[:, KC + c:KC + c + 1]).then_inc(fin_ready, 1)

        @block.vector
        def _(dve):
            V = nc.vector

            def tail_of(base, k, per=0, i=None):
                p = base + k + AHEAD
                if p >= SLABS:
                    return
                slot = p % RING
                dve.wait_ge(hi_ready, lin(p + 1, per, i))
                V.tensor_tensor(w_lo[:, slot, :], w_raw[:, slot, :], w_hi[:, slot, :].bitcast(F32),
                                ALU.subtract).then_inc(lo_ready, 1)

            def mod_bias(bank, n, col, i_per=0, i=None):
                dve.wait_ge(mod_cols_ready, n)
                at = bass.ds(i * i_per + col, 4) if i is not None else slice(col, col + 4)
                V.tensor_tensor(mod[:, at, :], banks[:, bank, 0:8].rearrange("p (q c) -> p q c", c=2),
                                b_mod[:, at].unsqueeze(2).to_broadcast([P, 4, 2]), ALU.add).then_inc(mod_ready, 1)

            def clear_stats():
                V.memset(banks[:, SUM, :], 0.0).then_inc(cleared, 1)
                V.memset(banks[:, SQS, :], 0.0).then_inc(cleared, 1)

            def ln_copies(r, width, stats_done):
                stats_done()
                V.tensor_copy(t1[:, 0:width], banks[:, SUM, 0:width]).then_inc(ln_copy, 1)
                V.tensor_copy(t2[:, 0:width], banks[:, SQS, 0:width]).then_inc(ln_copy, 1)

            def ln_moments(r, width):
                a, b, c = t1[:, 0:width], t2[:, 0:width], t3[:, 0:width]
                dve.wait_ge(ln_sums, r + 1)
                V.tensor_scalar(a, banks[:, SUM, 0:width], 1.0 / D, None, ALU.mult).then_inc(ln_step, 1)
                dve.wait_ge(ln_step, 5 * r + 1)
                V.tensor_tensor(c, a, a, ALU.mult).then_inc(ln_step, 1)
                dve.wait_ge(ln_step, 5 * r + 2)
                V.scalar_tensor_tensor(out=b, in0=banks[:, SQS, 0:width], scalar=1.0 / D, in1=c,
                                       op0=ALU.mult, op1=ALU.subtract).then_inc(ln_step, 1)
                dve.wait_ge(ln_step, 5 * r + 3)
                V.tensor_scalar(b, b, 0.0, LN_EPS, ALU.max, ALU.add).then_inc(ln_step, 1)
                if r < 2:
                    V.memset(banks[:, SUM, :], 0.0).then_inc(cleared, 1)
                    V.memset(banks[:, SQS, :], 0.0).then_inc(cleared, 1)
                dve.wait_ge(ln_sqrt, r + 1)
                V.reciprocal(b, b).then_inc(ln_step, 1)
                dve.wait_ge(ln_step, 5 * r + 5)

            dve.sem_inc(mod_ready, 2)
            dve.sem_inc(a_gated, 1)
            dve.sem_inc(b_gated, 1)
            dve.sem_inc(b_mix, 4)
            dve.sem_inc(g_sum, 1)
            dve.sem_inc(o_mul, 1)
            dve.sem_inc(o_lo, 1)
            dve.sem_inc(mod_cols_ready, 1)
            V.memset(pads[:, :], 0.0).then_inc(cleared, 1)
            V.memset(c4[:, 4 * KC:].bitcast(F32), 0.0).then_inc(cleared, 1)
            V.memset(neg_half, -0.5).then_inc(cleared, 1)
            clear_stats()
            dve.wait_ge(params_in, 16)
            dve.wait_ge(cond_sig, 1)
            V.tensor_tensor(cond_s, cond_s, cond, ALU.mult).then_inc(cond_mul, 1)
            dve.wait_ge(cond_hi, 1)
            dve.wait_ge(cleared, 5)
            c4v = c4[:, 0:4 * KC].rearrange("p (k c s) -> p k c s", c=2, s=2)
            V.tensor_tensor(c4v[:, :, :, 1], cond_s, c4v[:, :, :, 0].bitcast(F32), ALU.subtract).then_inc(cond_lo, 1)
            for k in range(-AHEAD, 0):
                tail_of(0, k)
            with dve.Fori(0, 4) as i:
                for k in range(MOD_PAIR):
                    tail_of(S_MOD0, k, MOD_PAIR, i)
                    if k == KC + 6:
                        mod_bias(VAL, i * 2 + 2, 0, 4, i)
                mod_bias(GLU, i * 2 + 3, KC, 4, i)
                dve.wait_ge(mod_ready, i * 2 + 4)
                sc = mod[:, bass.ds(i * 4 + KC, 4), :]
                V.tensor_scalar(sc, sc, 1.0, None, ALU.add).then_inc(scale1, 1)
                dve.wait_ge(scale1, i + 1)
                dve.wait_ge(xall_in, 16)
                for q in range(4):
                    t = tmp[:, q % 2, :]
                    for half in range(2):
                        tok = slice(half * LAT, (half + 1) * LAT)
                        V.tensor_scalar(t[:, tok], u[:, bass.ds(i * 4 + q, 1), tok].rearrange("p o t -> p (o t)"),
                                        mod[:, bass.ds(i * 4 + KC + q, 1), half],
                                        mod[:, bass.ds(i * 4 + q, 1), half],
                                        ALU.mult, ALU.add).then_inc(h_mod, 1)
                    dve.wait_ge(h_hi, i * 4 + q + 1)
                    hq = lambda s: h[:, bass.ds(i * 4 + q, 1), s, :].rearrange("p o t -> p (o t)")
                    V.tensor_tensor(hq(1), t, hq(0).bitcast(F32), ALU.subtract).then_inc(h_lo, 1)

            with dve.Fori(0, KC) as i:
                ui = u[:, bass.ds(i, 1), :].rearrange("p o t -> p (o t)")
                u3 = u[:, bass.ds(i, 1), :].rearrange("p o (s t) -> p (o s) t", s=2)
                t33 = t3.rearrange("p (s t) -> p s t", s=2)
                t13 = t1.rearrange("p (s t) -> p s t", s=2)
                taps = iter(range(TAPS_A))

                def conv_a_tap():
                    n = next(taps, None)
                    if n is None:
                        return
                    src, w = pad_a[:, :, n:n + LAT], conv_a_w[:, bass.ds(i * TAPS_A + n, 1)]
                    acc = (u3, t33)[n % 2]
                    if n == 0:
                        dve.wait_ge(a_gated, i + 2)
                        V.tensor_scalar(acc, src, w, conv_a_b[:, bass.ds(i, 1)], ALU.mult,
                                        ALU.add).then_inc(conv_tap, 1)
                    elif n == 1:
                        V.tensor_scalar(acc, src, w, None, ALU.mult).then_inc(conv_tap, 1)
                    else:
                        dve.wait_ge(conv_tap, i * (TAPS_A + 1) + n - 1)
                        V.scalar_tensor_tensor(out=acc, in0=src, scalar=w, in1=acc, op0=ALU.mult,
                                               op1=ALU.add).then_inc(conv_tap, 1)

                for k in range(MIX):
                    tail_of(S_MIX, k, MIX, i)
                    if k == 15:
                        dve.wait_ge(glu_sig, i * 2 + 1)
                        V.tensor_tensor(pad_a[:, :, PAD_A:PAD_A + LAT],
                                        banks[:, VAL, :].rearrange("p (s t) -> p s t", s=2),
                                        t2.rearrange("p (s t) -> p s t", s=2), ALU.mult).then_inc(a_gated, 1)
                    if k > 15 and (k >= 32 or k % 2 == 0):
                        conv_a_tap()
                        conv_a_tap()
                    if k == 31:
                        dve.wait_ge(slab_used, i * MIX + S_MIX + 31)
                        dve.wait_ge(bx_copied, i + 1)
                        V.tensor_tensor(pad_b[:, :, PAD_B:PAD_B + LAT],
                                        banks[:, BC, :].rearrange("p (s t) -> p s t", s=2), t13,
                                        ALU.mult).then_inc(b_gated, 1)
                    if k in (33, 34, 35):
                        n = k - 33
                        src, w = pad_b[:, :, n:n + LAT], conv_b_w[:, bass.ds(i * TAPS_B + n, 1)]
                        if n == 0:
                            dve.wait_ge(b_gated, i + 2)
                            V.tensor_scalar(t13, src, w, None, ALU.mult).then_inc(b_tap, 1)
                        else:
                            dve.wait_ge(b_tap, i * TAPS_B + n)
                            V.scalar_tensor_tensor(out=t13, in0=src, scalar=w, in1=t13, op0=ALU.mult,
                                                   op1=ALU.add).then_inc(b_tap, 1)
                    if k == 36:
                        dve.wait_ge(slab_used, i * MIX + S_MIX + 36)
                        dve.wait_ge(b_tap, i * TAPS_B + TAPS_B)
                        V.tensor_tensor(t1, banks[:, BB, :], t1, ALU.mult).then_inc(b_mix, 1)
                for _ in range(TAPS_A):
                    conv_a_tap()
                dve.wait_ge(conv_tap, i * (TAPS_A + 1) + TAPS_A)
                V.tensor_tensor(ui, ui, t3, ALU.add).then_inc(conv_tap, 1)
                dve.wait_ge(glu_sig, i * 2 + 2)
                V.tensor_tensor(t2, banks[:, BG, :], t2, ALU.mult).then_inc(b_mix, 1)
                dve.wait_ge(conv_tap, i * (TAPS_A + 1) + TAPS_A + 1)
                V.tensor_tensor(banks[:, SUM, :], banks[:, SUM, :], ui, ALU.add).then_inc(a_stats, 1)
                dve.wait_ge(b_mix, i * 4 + 4 + 2)
                V.tensor_tensor(t1, t1, t2, ALU.mult).then_inc(b_mix, 1)
                dve.wait_ge(conv_sq, i + 1)
                V.tensor_tensor(banks[:, SQS, :], banks[:, SQS, :], t3, ALU.add).then_inc(a_stats, 1)
                mod_bias(MOD, i + 10, 32, 4, i)
                dve.wait_ge(b_hi, i + 1)
                bi = lambda s: b_act[:, bass.ds(i, 1), s, :].rearrange("p o t -> p (o t)")
                V.tensor_tensor(bi(1), t1, bi(0).bitcast(F32), ALU.subtract).then_inc(b_mix, 1)

            def agate_dve(base, per=0, i=None):
                j = None if i is None else (2, i)
                for s in range(2):
                    uj = chunk(u, j, s)
                    if i is None and s == 0:
                        dve.wait_ge(b_hi, KC)
                        dve.wait_ge(b_mix, 4 * KC + 4)
                        ln_copies(0, TOK, lambda: dve.wait_ge(a_stats, 2 * KC))
                    for k in range(4):
                        tail_of(base + 4 * s, k, per, i)
                        if k == 0:
                            if i is None and s == 0:
                                ln_moments(0, TOK)
                            V.tensor_tensor(uj, uj, t1, ALU.subtract).then_inc(an_step, 1)
                            dve.wait_ge(an_step, lin(3 * s + 1, 6, i))
                            V.tensor_tensor(uj, uj, t2, ALU.mult).then_inc(an_step, 1)
                        if k == 2:
                            dve.wait_ge(an_affine, lin(2 * s + 2, 4, i))
                            V.tensor_tensor(uj, uj, t3, ALU.mult).then_inc(an_step, 1)
                    dve.wait_ge(ag_sig, lin(s + 1, 2, i))
                    V.tensor_tensor(t4, banks[:, s, :], t4, ALU.mult).then_inc(ag_mul, 1)
                    dve.wait_ge(ag_mul, lin(2 * s + 1, 4, i))
                    dve.wait_ge(an_step, lin(3 * s + 3, 6, i))
                    V.tensor_tensor(uj, uj, t4, ALU.mult).then_inc(ag_mul, 1)

            agate_dve(S_AGATE)
            with dve.Fori(1, KC // 2) as i:
                agate_dve(S_AGATE, 8, i)

            def out0_dve(base, per=0, i=None):
                j = None if i is None else (2, i)
                for s in range(2):
                    uj = chunk(u, j, s)
                    for k in range(8):
                        tail_of(base + 8 * s, k, per, i)
                        if i is None and s == 0 and k < 4:
                            for c in range(4 * k, 4 * k + 4):
                                dve.wait_ge(act_hi, c + 1)
                                V.tensor_tensor(h[:, c, 1, :], u[:, c, :], h[:, c, 0, :].bitcast(F32),
                                                ALU.subtract).then_inc(act_lo, 1)
                    dve.wait_ge(slab_used, lin(base + 8 * s + 8, per, i))
                    dve.wait_ge(x_scaled, lin(s + 1, 2, i))
                    for half in range(2):
                        tok = slice(half * LAT, (half + 1) * LAT)
                        gate = mod[:, 32 + s:33 + s, half] if i is None else mod[:, bass.ds(i * 2 + 32 + s, 1), half]
                        V.scalar_tensor_tensor(out=uj[:, tok], in0=banks[:, BX + s, tok], scalar=gate,
                                               in1=t3[:, tok], op0=ALU.mult, op1=ALU.add).then_inc(res_step, 1)
                    dve.wait_ge(res_step, lin(2 * s + 2, 4, i))
                    V.tensor_tensor(banks[:, SUM, :], banks[:, SUM, :], uj, ALU.add).then_inc(res_stats, 1)
                    dve.wait_ge(res_sq, lin(s + 1, 2, i))
                    V.tensor_tensor(banks[:, SQS, :], banks[:, SQS, :], t4, ALU.add).then_inc(res_stats, 1)

            out0_dve(S_OUT0)
            with dve.Fori(1, KC // 2) as i:
                out0_dve(S_OUT0, 16, i)
            sc1 = mod[:, 48 + KC:48 + 2 * KC, :]
            dve.wait_ge(mod_ready, 2 + 24)
            V.tensor_scalar(sc1, sc1, 1.0, None, ALU.add).then_inc(scale1, 1)
            ln_copies(1, TOK, lambda: dve.wait_ge(res_stats, 2 * KC))
            ln_moments(1, TOK)
            dve.wait_ge(scale1, 5)
            dve.sem_inc(n1_step, 1)
            for c in range(KC + 2):
                if c < KC:
                    V.tensor_tensor(u[:, c, :], u[:, c, :], t1, ALU.subtract).then_inc(n1_step, 1)
                if 1 <= c <= KC:
                    m = c - 1
                    dve.wait_ge(n1_affine, m + 1)
                    if m >= 2:
                        dve.wait_ge(h1_lo, m - 1)
                    for half in range(2):
                        tok = slice(half * LAT, (half + 1) * LAT)
                        V.tensor_scalar(tmp[:, 2 + m % 2, tok], u[:, m, tok], mod[:, 48 + KC + m:49 + KC + m, half],
                                        mod[:, 48 + m:49 + m, half], ALU.mult, ALU.add).then_inc(h1_mod, 1)
                if c < KC:
                    dve.wait_ge(n1_step, 2 * c + 2)
                    V.tensor_tensor(u[:, c, :], u[:, c, :], t2, ALU.mult).then_inc(n1_step, 1)
                if c >= 2:
                    m = c - 2
                    dve.wait_ge(h1_hi, m + 1)
                    V.tensor_tensor(h[:, m, 1, :], tmp[:, 2 + m % 2, :], h[:, m, 0, :].bitcast(F32),
                                    ALU.subtract).then_inc(h1_lo, 1)
                    tail_of(S_K, m)

            def prepare(x, n, gain, rotate, n_expr=None, powers=None):
                at = (lambda c: PREP * n + c) if n_expr is None else (lambda c: n_expr + c)
                heads = lambda a: a.rearrange("p t (g d) -> p (t g) d", d=HD)
                big, big2 = tmp[:, 2:4, :], x_in[:, :, :]
                V.tensor_tensor(big, x, x, ALU.mult).then_inc(prep, 1)
                dve.wait_ge(prep, at(1))
                V.tensor_reduce(out=sumsq, in_=heads(big), axis=AX_X, op=ALU.add).then_inc(prep, 1)
                dve.wait_ge(prep, at(2))
                V.tensor_scalar(sumsq, sumsq, 1.0 / HD, RMS_EPS, ALU.mult, ALU.add).then_inc(prep, 1)
                dve.wait_ge(prep_pow, n + 1 if powers is None else powers)
                V.tensor_tensor(heads(x), heads(x), sumsq.unsqueeze(2).to_broadcast([P, 8, HD]),
                                ALU.mult).then_inc(prep, 1)
                dve.wait_ge(prep, at(4))
                V.tensor_tensor(heads(x), heads(x), gains[:, gain, :].unsqueeze(1).to_broadcast([P, 8, HD]),
                                ALU.mult).then_inc(prep, 1)
                dve.wait_ge(prep, at(5))
                if not rotate:
                    dve.sem_inc(prep, PREP - 5)
                    return
                per_tile = lambda a, t: a[:, t, :].rearrange("p (g d) -> p g d", d=HD)
                for t in range(2):
                    V.tensor_tensor(per_tile(big, t), per_tile(x, t),
                                    rope_cos[:, t, :].unsqueeze(1).to_broadcast([P, GROUP, HD]),
                                    ALU.mult).then_inc(prep, 1)
                for t in range(2):
                    for f in range(2):
                        o, a, b = (z.rearrange("p (g r f e) -> p g r f e", g=GROUP, r=2, f=2)
                                   for z in (big2[:, t, :], x[:, t, :], x[:, t, :]))
                        sn = rope_sin[:, t, :].rearrange("p (r f e) -> p r f e", r=2, f=2)[:, :, f, :]
                        V.tensor_tensor(o[:, :, :, f, :], a[:, :, :, 1 - f, :],
                                        sn.unsqueeze(1).to_broadcast([P, GROUP, 2, 32]), ALU.mult).then_inc(prep, 1)
                dve.wait_ge(prep, at(11))
                V.tensor_tensor(x, big, big2, ALU.add).then_inc(prep, 1)

            dve.wait_ge(rope_in, 16)
            for kc in range(KC):
                tail_of(S_V, kc)
                if kc == 5:
                    dve.wait_ge(k_copied, 4)
                    prepare(k_tok[:, 0:2, :], 0, 1, True)
                if kc == 10:
                    prepare(k_tok[:, 2:4, :], 1, 1, False)
            for kc in range(KC):
                tail_of(S_Q0, kc)
            dve.wait_ge(q_copied, 2)
            prepare(q_tok[:, :, :], 2, 0, True)

            def attend_dve(base, last, per=0, i=None):
                head = lambda c, k=1: lin(c, GROUP * k, i)
                k = 0
                for g in range(GROUP):
                    hd = g if i is not None else g + GROUP * (KV - 1)
                    slabs = 12 if not last and g < 2 else 4
                    for m in range(slabs):
                        tail_of(base, k, per, i)
                        k += 1
                        if m == 0:
                            dve.wait_ge(qk_done, head(hd + 1))
                            V.tensor_reduce(out=rowinv, in_=banks[:, S:S + 2, :], axis=AX_X,
                                            op=ALU.max).then_inc(max_step, 1)
                            dve.wait_ge(max_step, head(2 * hd + 1, 2))
                            V.tensor_scalar(negmax, rowinv, -SCALE, None, ALU.mult).then_inc(max_step, 1)
                            if g:
                                output(hd - 1, i)
                        if m == 2:
                            dve.wait_ge(p_exp, head(2 * hd + 2, 2))
                            V.reciprocal(rowinv, rowsum).then_inc(p_norm_inv, 1)
                            dve.wait_ge(p_norm_inv, head(hd + 1))
                            for t in range(2):
                                V.tensor_scalar(prob[:, t, :], prob[:, t, :], rowinv[:, t:t + 1], None,
                                                ALU.mult).then_inc(p_norm, 1)
                        if not last and g == 2 and m == 3:
                            dve.wait_ge(q_copied, lin(4, 2, i))
                            prepare(q_tok[:, :, :], 0, 0, True, lin(PREP * 3, PREP, i), lin(4, 1, i))
                    dve.wait_ge(g_part, head(hd + 1))
                    V.tensor_tensor(t1[:, 0:LAT], banks[:, G, 0:LAT], t1[:, 0:LAT], ALU.add).then_inc(g_sum, 1)
                    dve.wait_ge(g_exp, head(hd + 1))
                    V.tensor_scalar(t2[:, 0:LAT], t2[:, 0:LAT], 1.0, None, ALU.add).then_inc(g_inv, 1)
                    dve.wait_ge(g_inv, head(3 * hd + 1, 3))
                    V.reciprocal(t2[:, 0:LAT], t2[:, 0:LAT]).then_inc(g_inv, 1)
                    dve.wait_ge(g_inv, head(3 * hd + 2, 3))
                    V.tensor_tensor(t1[:, 0:LAT], t1[:, 0:LAT], t2[:, 0:LAT], ALU.mult).then_inc(g_inv, 1)
                output(GROUP - 1 if i is not None else HEADS - 1, i)

            def output(hd, i):
                dve.wait_ge(pv_done, lin(hd + 1, GROUP, i))
                dve.wait_ge(g_inv, lin(3 * hd + 3, 3 * GROUP, i))
                V.tensor_tensor(t1[:, 0:LAT], banks[:, PV, 0:LAT], t1[:, 0:LAT], ALU.mult).then_inc(o_mul, 1)
                dve.wait_ge(o_hi, lin(hd + 1, GROUP, i))
                at = bass.ds(i * GROUP + hd, 1) if i is not None else slice(hd, hd + 1)
                part = lambda s: o_act[:, at, s, :].rearrange("p o t -> p (o t)")
                V.tensor_tensor(part(1), t1[:, 0:LAT], part(0).bitcast(F32), ALU.subtract).then_inc(o_lo, 1)

            with dve.Fori(0, KV - 1) as i:
                attend_dve(S_ATT, False, ATT, i)
            attend_dve(S_ATTL, True)

            def out1_dve(base, pair, per=0, i=None):
                j = None if i is None else (2, i)
                for s in range(2):
                    jn = 2 * pair + s
                    n = (lambda c, m: lin(m * s + c, 2 * m, i)) if i is not None else (lambda c, m: m * jn + c)
                    for k in range(4):
                        tail_of(base + 4 * s, k, per, i)
                    uj = chunk(u, j, s if i is not None else jn)[:, 0:LAT]
                    gate = mod[:, bass.ds(i * 2 + 80 + s, 1), 0] if i is not None else mod[:, 80 + jn:81 + jn, 0]
                    dve.wait_ge(y_part, n(1, 1))
                    V.scalar_tensor_tensor(out=t2[:, 0:LAT], in0=banks[:, s, 0:LAT], scalar=gate,
                                           in1=t1[:, 0:LAT], op0=ALU.mult, op1=ALU.add).then_inc(y_step, 1)
                    dve.wait_ge(y_step, n(1, 2))
                    V.scalar_tensor_tensor(out=uj, in0=uj, scalar=ALPHA, in1=t2[:, 0:LAT], op0=ALU.mult,
                                           op1=ALU.add).then_inc(y_step, 1)
                    dve.wait_ge(y_step, n(2, 2))
                    V.tensor_tensor(banks[:, SUM, 0:LAT], banks[:, SUM, 0:LAT], uj, ALU.add).then_inc(y_stats, 1)
                    dve.wait_ge(y_sq, n(1, 1))
                    V.tensor_tensor(banks[:, SQS, 0:LAT], banks[:, SQS, 0:LAT], t4[:, 0:LAT],
                                    ALU.add).then_inc(y_stats, 1)

            dve.wait_ge(v_copied, 4)
            clear_stats()
            out1_dve(S_OUT1, 0)
            with dve.Fori(1, KC // 2 - 1) as i:
                out1_dve(S_OUT1, 0, 8, i)
            out1_dve(S_OUT1 + 8 * (KC // 2 - 1), KC // 2 - 1)
            ln_copies(2, LAT, lambda: dve.wait_ge(y_stats, 2 * KC))
            ln_moments(2, LAT)
            for c in range(KC):
                V.tensor_tensor(u[:, c, 0:LAT], u[:, c, 0:LAT], t1[:, 0:LAT], ALU.subtract).then_inc(fin_step, 1)
                dve.wait_ge(fin_step, 2 * c + 1)
                V.tensor_tensor(u[:, c, 0:LAT], u[:, c, 0:LAT], t2[:, 0:LAT], ALU.mult).then_inc(fin_step, 1)


def weight_slabs(w_mod, w_in_e, w_out_e, w_in_o, w_out_o):
    mods = np.concatenate([w_mod[0], w_mod[1]], axis=1)

    def job(w, col, chunks):
        rows = w[chunks[0] * P:(chunks[-1] + 1) * P, col:col + P]
        return rows.reshape(len(chunks) // 4, 4, P, P).transpose(0, 2, 1, 3).reshape(-1, P, 4 * P)

    def group(w, col):
        return w[:, col:col + 512].reshape(KC, P, 512)

    all_in = range(KC)
    out = []
    for q in range(4):
        out += [group(mods, q * 512), group(mods, D + q * 512)]
    for j in range(KC):
        parts = [job(w_in_e, at * D + j * P, all_in) for at in (0, 1, 3, 5, 4, 6)]
        mod_group = group(mods, 2 * D + j * 512)
        for n in range(4):
            out.append(np.stack([parts[n], mod_group[4 * n:4 * n + 4]], axis=1).reshape(8, P, 512))
        out += parts[4:]
    for j in range(KC):
        out.append(job(w_in_e, 2 * D + j * P, all_in))
    for j in range(KC):
        out += [job(w_out_e, j * P, range(KC, 2 * KC)), job(w_out_e, j * P, all_in)]
    out += [group(w_in_o, 2 * D), group(w_in_o, 2 * D + KV * HD), group(w_in_o, 0)]
    for n in range(KV):
        for g in range(GROUP):
            if n + 1 < KV and g < 2:
                out.append(group(w_in_o, (n + 1) * 512)[8 * g:8 * g + 8])
            out.append(job(w_in_o, D + (n * GROUP + g) * P, all_in))
    for j in range(KC):
        out.append(job(w_out_o, j * P, all_in))
    slabs = np.concatenate(out, axis=0)
    assert slabs.shape == (SLABS, P, 512)
    return slabs


def rope_constants():
    tok = np.arange(LAT)
    row, col = (tok // GRID_W).astype(np.float32), (tok % GRID_W).astype(np.float32)
    axis = HD // 2
    freq = (ROPE_THETA ** (-np.arange(0, axis, 2, dtype=np.float32) / axis)).astype(np.float32)
    cos, sin = np.zeros((LAT, HD), np.float32), np.zeros((LAT, HD), np.float32)
    for n, pos in enumerate((row, col)):
        ang = pos[:, None] * freq[None, :]
        at = n * axis
        cos[:, at:at + axis] = np.concatenate([np.cos(ang), np.cos(ang)], axis=1)
        sin[:, at:at + axis] = np.concatenate([-np.sin(ang), np.sin(ang)], axis=1)
    return (t.reshape(2, P, HD).transpose(1, 0, 2).reshape(P, 2 * HD) for t in (cos, sin))


def kernel(x, c, ctx, c_ctx, w_mod, b_mod, post_ln_g, post_ln_b, w_in_e, conv_a_w, conv_a_b,
           norm_a_g, norm_a_b, conv_b_w, w_out_e, w_in_o, q_norm_g, k_norm_g, w_out_o):
    import numpy as np
    import concourse.bacc as bacc
    from concourse.bass_utils import run_bass_kernel_spmd

    def channels(a):
        a = np.asarray(a)
        return a.reshape(a.shape[0], -1, P).transpose(2, 1, 0)

    f = lambda a: channels(a).reshape(P, -1)
    tokens = np.concatenate([np.asarray(x)[0], np.asarray(ctx)[0]], axis=0)
    cond = np.concatenate([np.asarray(c), np.asarray(c_ctx)[None]], axis=0)
    params = np.concatenate([
        f(conv_a_w[0]), f(conv_a_b), f(norm_a_g), f(norm_a_b), f(conv_b_w[0]),
        channels(post_ln_g).transpose(0, 2, 1).reshape(P, -1), channels(post_ln_b).transpose(0, 2, 1).reshape(P, -1),
        channels(b_mod).transpose(0, 2, 1).reshape(P, -1), f(cond)], axis=1)
    sel = np.zeros((P, 2), np.float32)
    sel[0:2, 0] = 1
    sel[2:4, 1] = 1
    consts = np.concatenate([np.ones((P, P), np.float32), np.eye(P, dtype=np.float32), sel], axis=1)
    cos, sin = rope_constants()
    gains = [np.broadcast_to(np.asarray(g), (P, HD)) for g in (q_norm_g, k_norm_g)]
    rope = np.concatenate([cos, sin] + gains, axis=1)
    arrays = {
        "weights": weight_slabs(np.asarray(w_mod), np.asarray(w_in_e)[0], np.asarray(w_out_e)[0],
                                np.asarray(w_in_o)[0], np.asarray(w_out_o)[0]),
        "x_t": channels(tokens), "params": params, "consts": consts, "rope": rope,
    }
    arrays = {n: np.ascontiguousarray(a) for n, a in arrays.items()}
    nc = bacc.Bacc("TRN2", target_bir_lowering=False, num_devices=1)
    aps = [nc.dram_tensor(n, a.shape, F32, kind="ExternalInput").ap() for n, a in arrays.items()]
    out_t = nc.dram_tensor("out_t", (P, KC, LAT), F32, kind="ExternalOutput").ap()
    build(nc, *aps, out_t)
    r = run_bass_kernel_spmd(nc, [arrays], core_ids=[0])
    return r.results[0]["out_t"].transpose(2, 1, 0).reshape(1, LAT, D)
```

```python
from contextlib import ExitStack

import numpy as np

import concourse.bass as bass
from concourse import mybir

F32 = mybir.dt.float32
F32R = mybir.dt.float32r
ALU = mybir.AluOpType
ACT = mybir.ActivationFunctionType
AX_X = mybir.AxisListType.X

P = 128
D = 2048
KC = D // P
LAT = 256
TOK = 512
HEADS, KV, HD = 16, 4, 128
GROUP = HEADS // KV
TAPS_A, TAPS_B = 31, 3
PAD_A, PAD_B = TAPS_A // 2, TAPS_B // 2
ALPHA = (2.0 * 2) ** 0.25
LN_EPS, RMS_EPS = 1e-5, 1e-6
SCALE = HD ** -0.5
GRID_W = 64
ROPE_THETA = 10000.0

RING = 4
AHEAD = RING - 1

TURN = 2 * KC
START = 4 * TURN
START_RING = 16
STEP = []
for _m in range(6 * 4):
    STEP.append((_m // 4, _m % 4))
    if 3 <= _m < 3 + KC:
        STEP.append(("mod", _m - 3))
MIX = len(STEP)
BOTH_STEPS = 12
MOD_BY_VECTOR = KC // 2
S_MIX = 0
S_AGATE = S_MIX + KC * MIX
S_OUT0 = S_AGATE + KC * 4
S_K = S_OUT0 + KC * 8
S_V = S_K + KC
S_Q0 = S_V + KC
S_ATT = S_Q0 + KC
ATT = KC + GROUP * 4
S_ATTL = S_ATT + (KV - 1) * ATT
S_OUT1 = S_ATTL + GROUP * 4
SLABS = S_OUT1 + KC * 4

_sizes = [("conv_a_w", KC * TAPS_A), ("conv_a_b", KC), ("norm_a_g", KC), ("norm_a_b", KC),
          ("conv_b_w", KC * TAPS_B), ("ln_g", 2 * KC), ("ln_b", 2 * KC), ("b_mod", 96), ("cond", 2 * KC)]
COL, _at = {}, 0
for _n, _s in _sizes:
    COL[_n] = (_at, _at + _s)
    _at += _s
PARAMS = _at
CONSTS = P + P + 2 + 3
ROPE = 2 * 2 * HD + 2 * HD


def by_vector(pos, latent_only):
    return STEP[pos][0] == "mod" and (latent_only or STEP[pos][1] < MOD_BY_VECTOR)


def counts(pos, latent_only):
    return 2 if pos + 1 < MIX and by_vector(pos + 1, latent_only) else 1


def lin(c, per=0, i=None):
    return c if i is None else i * per + c


def build(nc, weights, x_t, params, consts, rope, out_t):
    ctx = ExitStack()
    with ctx:
        def sb(name, shape, dt=F32):
            return ctx.enter_context(nc.sbuf_tensor(name, shape, dt))

        def sem(name):
            return ctx.enter_context(nc.semaphore(name))

        arena_at = -(-nc.sbuf_base // 32) * 32
        sb("arena", [P, KC * 2 * TOK])
        b_act = nc.alloc_sbuf_tensor_at("b_act", [P, KC, 2, TOK], F32R, offset=arena_at)
        att_at = arena_at + KC * TOK * 4
        k_t = nc.alloc_sbuf_tensor_at("k_t", [P, KV, TOK], F32, offset=att_at)
        v_tok = nc.alloc_sbuf_tensor_at("v_tok", [P, 4, KV * HD], F32, offset=att_at + 8192)
        q_tok = nc.alloc_sbuf_tensor_at("q_tok", [P, 2, GROUP * HD], F32, offset=att_at + 16384)
        q_t = nc.alloc_sbuf_tensor_at("q_t", [P, GROUP, LAT], F32, offset=att_at + 20480)
        prob = nc.alloc_sbuf_tensor_at("prob", [P, 2, TOK], F32, offset=att_at + 24576)
        prob_t = nc.alloc_sbuf_tensor_at("prob_t", [P, 4, LAT], F32, offset=att_at + 28672)
        k_tok = nc.alloc_sbuf_tensor_at("k_tok", [P, 4, KV * HD], F32, offset=att_at + 24576)
        start_raw = nc.alloc_sbuf_tensor_at("start_raw", [P, START_RING, TOK], F32, offset=arena_at)
        c_row = nc.alloc_sbuf_tensor_at("c_row", [P, 4 * KC + P], F32, offset=att_at)
        b_flat = b_act[:, :, :, :].rearrange("p k s t -> p (k s t)")
        o_act = b_flat[:, 0:KC * 2 * LAT].rearrange("p (k s t) -> p k s t", k=KC, s=2)

        h = sb("h", [P, KC, 2, TOK], F32R)
        u = sb("u", [P, KC, TOK])
        w_raw = sb("w_raw", [P, RING, TOK])
        w_hi = sb("w_hi", [P, RING, TOK], F32R)
        w_lo = sb("w_lo", [P, RING, TOK], F32R)
        tmp = sb("tmp", [P, 4, TOK])
        x_in = sb("x_in", [P, 2, TOK])
        pads = sb("pads", [P, 2 * (LAT + 2 * PAD_A) + 2 * (LAT + 2 * PAD_B)])
        par = sb("par", [P, PARAMS])
        con = sb("con", [P, CONSTS])
        mod = sb("mod", [P, 96, 2])
        c4 = sb("c4", [P, 4 * KC + P], F32R)
        small = sb("small", [P, 86])
        v_stage = par[:, 0:4 * HD].rearrange("p (t d) -> p t d", t=4)

        t1, t2, t3, t4 = (tmp[:, n, :] for n in range(4))
        mod_row = t4
        mod_sum = x_in
        n_pad_a = 2 * (LAT + 2 * PAD_A)
        pad_a = pads[:, 0:n_pad_a].rearrange("p (s t) -> p s t", s=2)
        pad_b = pads[:, n_pad_a:n_pad_a + 2 * (LAT + 2 * PAD_B)].rearrange("p (s t) -> p s t", s=2)
        rope_cos = pads[:, 0:2 * HD].rearrange("p (t d) -> p t d", t=2)
        rope_sin = pads[:, 2 * HD:4 * HD].rearrange("p (t d) -> p t d", t=2)
        gains = pads[:, 4 * HD:6 * HD].rearrange("p (q d) -> p q d", q=2)
        squares = pads[:, 6 * HD:8 * HD].rearrange("p (n d) -> p n d", n=2)

        def column(name, inner=1):
            a, b = COL[name]
            return par[:, a:b]

        conv_a_w, conv_a_b = column("conv_a_w"), column("conv_a_b")
        norm_a_g, norm_a_b = column("norm_a_g"), column("norm_a_b")
        conv_b_w, ln_g, ln_b = column("conv_b_w"), column("ln_g"), column("ln_b")
        b_mod = column("b_mod")
        cond = column("cond").rearrange("p (k c) -> p k c", c=2)
        ones, ident, sel = con[:, 0:P], con[:, P:2 * P], con[0:4, 2 * P:2 * P + 2]
        to_column = (con[:, 2 * P + 3:2 * P + 5], con[:, 2 * P + 2:2 * P + 4])
        cond_s = small[:, 0:2 * KC].rearrange("p (k c) -> p k c", c=2)
        neg_half = small[:, 32:40]
        alpha_g, alpha_b = small[:, 54:54 + KC], small[:, 70:70 + KC]
        sumsq = small[:, 40:48]
        negmax = small[:, 48:50]
        rowsum = small[:, 50:52]
        rowinv = small[:, 52:54]

        banks = ctx.enter_context(nc.psum_tensor("banks", [P, 8, TOK], F32))
        VAL, GLU, BX, BC, BB, MOD, SUM, SQS = range(8)
        BG = BX
        G, Q, S, PT, PV = 0, 1, 3, 5, 7

        params_in = sem("params_in")
        consts_in = sem("consts_in")
        rope_in = sem("rope_in")
        xall_in = sem("xall_in")
        slab_landed = [sem(f"slab_landed{s}") for s in range(RING)]
        x_landed = [sem(f"x_landed{s}") for s in range(2)]
        start_landed = [sem(f"start_landed{n}") for n in range(START_RING // 4)]
        start_hi = sem("start_hi")
        start_lo = sem("start_lo")
        start_used = sem("start_used")
        hi_ready = sem("hi_ready")
        lo_ready = sem("lo_ready")
        slab_used = sem("slab_used")
        cleared = sem("cleared")
        cond_sig = sem("cond_sig")
        cond_mul = sem("cond_mul")
        cond_hi = sem("cond_hi")
        cond_lo = sem("cond_lo")
        mod_row_ready = sem("mod_row_ready")
        mod_cols_ready = sem("mod_cols_ready")
        mod_ready = sem("mod_ready")
        h_mod = sem("h_mod")
        h_hi = sem("h_hi")
        h_lo = sem("h_lo")
        glu_sig = sem("glu_sig")
        a_gated = sem("a_gated")
        bx_copied = sem("bx_copied")
        b_gated = sem("b_gated")
        conv_tap = sem("conv_tap")
        b_tap = sem("b_tap")
        b_mix = sem("b_mix")
        b_hi = sem("b_hi")
        conv_sq = sem("conv_sq")
        a_stats = sem("a_stats")
        ln_copy = sem("ln_copy")
        ln_sums = sem("ln_sums")
        ln_step = sem("ln_step")
        ln_sqrt = sem("ln_sqrt")
        an_step = sem("an_step")
        an_affine = sem("an_affine")
        ag_sig = sem("ag_sig")
        ag_mul = sem("ag_mul")
        act_hi = sem("act_hi")
        act_lo = sem("act_lo")
        x_scaled = sem("x_scaled")
        res_step = sem("res_step")
        res_sq = sem("res_sq")
        res_stats = sem("res_stats")
        n1_step = sem("n1_step")
        h1_mod = sem("h1_mod")
        h1_hi = sem("h1_hi")
        h1_lo = sem("h1_lo")
        scale1 = sem("scale1")
        fold1 = sem("fold1")
        v_copied = sem("v_copied")
        head_squares = sem("head_squares")
        head_mean = sem("head_mean")
        head_power = sem("head_power")
        head_scaled = sem("head_scaled")
        rope_step = sem("rope_step")
        rope_done = sem("rope_done")
        k_transposed = sem("k_transposed")
        kt_ready = sem("kt_ready")
        q_transposed = sem("q_transposed")
        qt_ready = sem("qt_ready")
        v_staged = sem("v_staged")
        qk_done = sem("qk_done")
        max_step = sem("max_step")
        p_exp = sem("p_exp")
        p_norm_inv = sem("p_norm_inv")
        p_norm = sem("p_norm")
        pt_done = sem("pt_done")
        pt_copied = sem("pt_copied")
        pv_done = sem("pv_done")
        g_part = sem("g_part")
        g_sum = sem("g_sum")
        g_tanh = sem("g_tanh")
        g_silu = sem("g_silu")
        o_mul = sem("o_mul")
        o_hi = sem("o_hi")
        o_lo = sem("o_lo")
        y_part = sem("y_part")
        x1_scaled = sem("x1_scaled")
        y_step = sem("y_step")
        y_sq = sem("y_sq")
        y_stats = sem("y_stats")
        fin_step = sem("fin_step")
        fin_ready = sem("fin_ready")
        out_sem = sem("out_sem")

        def turn_landed(engine, k, i):
            q, slots = k // 4, START_RING // 4
            engine.wait_ge(start_landed[q % slots], lin(16 * (q // slots + 1), 16 * 8 // slots, i))

        ROPE_K, ROPE_T, ROPE_Q = 8, 3, 7
        ROPE_BASE = ROPE_K - 1 + ROPE_T

        def chunk(buf, j, jn):
            if j is None:
                return buf[:, jn, :]
            return buf[:, bass.ds(j[1] * j[0] + jn, 1), :].rearrange("p o t -> p (o t)")

        def per_chunk(col, j, jn):
            return col[:, jn:jn + 1] if j is None else col[:, bass.ds(j[1] * j[0] + jn, 1)]

        def rms_power(pool, n):
            pool.wait_ge(head_mean, n + 1)
            nc.gpsimd.tensor_tensor(sumsq, sumsq, neg_half, ALU.pow).then_inc(head_power, 1)

        def stage_v(pool, n):
            if n == 0:
                pool.wait_ge(v_copied, 4)
            else:
                pool.wait_ge(pv_done, GROUP * n)
            nc.gpsimd.tensor_copy(v_stage[:, :, :], v_tok[:, :, n * HD:(n + 1) * HD]).then_inc(v_staged, 1)

        block = ctx.enter_context(nc.Block())

        @block.sync
        def _(sp):
            def load_slab(base, k, per=0, i=None):
                p, slot = base + k, (base + k) % RING
                if p >= RING:
                    sp.wait_ge(lo_ready, lin(p - RING + 1, per, i))
                at = START + p
                src = weights[at] if i is None else weights[bass.ds(i * per + at, 1)].rearrange("o p n -> p (o n)")
                sp.dma_start(w_raw[:, slot, :], src).then_inc(slab_landed[slot], 16)

            sp.dma_start(par[:, :], params).then_inc(params_in, 16)
            sp.dma_start(con[:, :], consts).then_inc(consts_in, 16)

            def load_four(turn, q, i=None):
                if i is not None or turn or q >= 4:
                    sp.wait_ge(start_used, lin(TURN * turn + 4 * q + 4, TURN, i))
                src = weights[4 * q:4 * q + 4] if i is None else weights[bass.ds(i * TURN + 4 * q, 4)]
                slot = q % (START_RING // 4)
                sp.dma_start(start_raw[:, 4 * slot:4 * slot + 4, :],
                             src.rearrange("s p n -> p s n")).then_inc(start_landed[slot], 16)

            for q in range(8):
                load_four(0, q)
                if q == 1:
                    sp.dma_start(u[:, :, :], x_t).then_inc(xall_in, 16)
            with sp.Fori(1, 4) as i:
                for q in range(8):
                    load_four(0, q, i)
            for k in range(RING):
                load_slab(0, k)
            with sp.Fori(0, (S_OUT0 - RING) // RING) as i:
                for k in range(RING):
                    load_slab(RING, k, RING, i)

            def load_x(j_slot, pair, i=None):
                if i is not None:
                    sp.wait_ge(x_scaled, i * 2 + j_slot - 1)
                    src = x_t[:, bass.ds(i * 2 + j_slot, 1), :].rearrange("p o n -> p (o n)")
                else:
                    src = x_t[:, 2 * pair + j_slot, :]
                sp.dma_start(x_in[:, j_slot, :], src).then_inc(x_landed[j_slot], 16)

            def out0_pair(pair, i=None):
                for s in range(2):
                    load_x(s, pair, i)
                    for k in range(8):
                        load_slab(S_OUT0 + (16 * pair if i is None else 0), 8 * s + k, 16, i)

            sp.wait_ge(mod_ready, 2 + 24)
            out0_pair(0)
            with sp.Fori(1, KC // 2) as i:
                out0_pair(0, i)
            sp.wait_ge(b_tap, TAPS_B * KC)
            sp.wait_ge(conv_tap, (TAPS_A + 1) * KC)
            sp.dma_start(pads[:, 0:ROPE], rope).then_inc(rope_in, 16)
            with sp.Fori(0, (SLABS - S_K) // RING) as i:
                for k in range(RING):
                    load_slab(S_K, k, RING, i)
            for j in range(KC):
                sp.wait_ge(fin_ready, j + 1)
                sp.dma_start(out_t[:, j, :], u[:, j, 0:LAT]).then_inc(out_sem, 16)
            sp.wait_ge(out_sem, 16 * KC)

        @block.gpsimd
        def _(pool):
            for n in range(3):
                rms_power(pool, n)
            stage_v(pool, 0)
            for n in range(1, KV):
                rms_power(pool, 2 + n)
                stage_v(pool, n)

        @block.tensor
        def _(pe):
            def slab(base, k, per=0, i=None):
                pe.wait_ge(lo_ready, lin(base + k + 1, per, i))
                return (base + k) % RING

            def job_slab(base, k, bank, act, first, last, per=0, i=None, count=1):
                s = slab(base, k, per, i)
                for kk in range(4):
                    blk = slice(kk * P, (kk + 1) * P)
                    for n, (w, half) in enumerate(((w_hi, 0), (w_hi, 1), (w_lo, 0))):
                        mm = nc.tensor.matmul(banks[:, bank, :], w[:, s, blk], act(kk, half),
                                              start=first and kk == 0 and n == 0,
                                              stop=last and kk == 3 and n == 2)
                mm.then_inc(slab_used, count)

            def job(base, bank, per=0, i=None, before=None):
                for k in range(4):
                    job_slab(base, k, bank, lambda kk, half: h[:, 4 * k + kk, half, :], k == 0, k == 3, per, i)

            def start_slab(k, i):
                bank, kc = (VAL, GLU)[k // KC], k % KC
                if k % 2:
                    turn_landed(pe, k, i)
                    mm = nc.tensor.matmul(banks[:, bank, :], c_row[:, 4 * kc:4 * kc + P],
                                          start_raw[:, k % START_RING, :], start=False, stop=kc == KC - 1)
                else:
                    pe.wait_ge(start_lo, lin(k // 2 + 1, KC, i))
                    for n, w in enumerate((w_hi, w_lo)):
                        mm = nc.tensor.matmul(banks[:, bank, :], c4[:, 4 * kc:4 * kc + P],
                                              w[:, (k // 2) % RING, :], start=kc == 0 and n == 0, stop=False)
                mm.then_inc(start_used, 1)

            def start_turn(i=None):
                pe.wait_ge(mod_ready, lin(2, 2, i))
                for k in range(TURN):
                    start_slab(k, i)
                    if k == KC + 8:
                        mod_columns(VAL, lin(1, 2, i))
                mod_columns(GLU, lin(2, 2, i))

            def mod_slab(base, k, kc, first, bank, per=0, i=None):
                s = slab(base, k, per, i)
                for n, w in enumerate((w_hi, w_lo)):
                    mm = nc.tensor.matmul(banks[:, bank, :], c4[:, 4 * kc:4 * kc + P], w[:, s, :],
                                          start=kc == first and n == 0, stop=kc == KC - 1 and n == 1)
                mm.then_inc(slab_used, 1)

            def mod_columns(bank, n):
                pe.wait_ge(mod_row_ready, n)
                for q in range(4):
                    mm = nc.tensor.matmul(banks[:, bank, 2 * q:2 * q + 2], mod_row[0:4, q * P:(q + 1) * P], sel,
                                          start=True, stop=True)
                mm.then_inc(mod_cols_ready, 1)

            def ln_totals(r, width):
                pe.wait_ge(ln_copy, 2 * r + 2)
                for t, bank in ((t1, SUM), (t2, SQS)):
                    mm = nc.tensor.matmul(banks[:, bank, 0:width], ones, t[:, 0:width], start=True, stop=True)
                mm.then_inc(ln_sums, 1)

            pe.wait_ge(consts_in, 16)
            pe.wait_ge(cond_lo, 1)
            start_turn()
            with pe.Fori(1, 4) as i:
                start_turn(i)
            pe.wait_ge(h_lo, KC)
            pe.wait_ge(mod_ready, 2 + 8)
            def sum_columns(latent_only, n):
                if not latent_only:
                    pe.wait_ge(mod_row_ready, n)
                for q in range(4):
                    blk = slice(q * P, (q + 1) * P)
                    if not latent_only:
                        nc.tensor.matmul(banks[:, MOD, 2 * q:2 * q + 2], mod_row[0:4, blk], sel,
                                         start=True, stop=False)
                    last = 0 if latent_only else 1
                    for c in range(last + 1):
                        mm = nc.tensor.matmul(banks[:, MOD, 2 * q:2 * q + 2], mod_sum[:, c, blk], to_column[c],
                                              start=latent_only, stop=c == last)
                mm.then_inc(mod_cols_ready, 1)

            def mix_step(i, latent_only):
                for pos, (n, k) in enumerate(STEP):
                    if n == "mod":
                        if not by_vector(pos, latent_only):
                            mod_slab(S_MIX + pos, 0, k, MOD_BY_VECTOR, MOD, MIX, i)
                        continue
                    if pos == 0:
                        pe.wait_ge(a_gated, i + 1)
                        pe.wait_ge(mod_ready, i + 2 + 8)
                    elif k == 0 and n == 2:
                        pe.wait_ge(b_mix, i * 4 + 1)
                    elif k == 0 and n == 3:
                        pe.wait_ge(b_gated, i + 1)
                    elif k == 0 and n == 4:
                        pe.wait_ge(bx_copied, i + 1)
                    elif k == 0 and n == 5:
                        sum_columns(latent_only, i + 9)
                        pe.wait_ge(b_mix, i * 4 + 3)
                    job_slab(S_MIX + pos, 0, (VAL, GLU, BX, BC, BG, BB)[n],
                             lambda kk, half: h[:, 4 * k + kk, half, :], k == 0, k == 3, MIX, i,
                             counts(pos, latent_only))
            with pe.Fori(0, BOTH_STEPS) as i:
                mix_step(i, False)
            with pe.Fori(BOTH_STEPS, KC) as i:
                mix_step(i, True)

            def agate_pair(base, per=0, i=None):
                for s in range(2):
                    if i is not None:
                        pe.wait_ge(ag_mul, i * 4 + 2 * s - 3)
                    elif s == 0:
                        pe.wait_ge(a_gated, KC + 1)
                    for k in range(4):
                        job_slab(base + 4 * s, k, s, lambda kk, half: h[:, 4 * k + kk, half, :],
                                 k == 0, k == 3, per, i)
                        if i is None and s == 0 and k == 0:
                            ln_totals(0, TOK)
            agate_pair(S_AGATE)
            with pe.Fori(1, KC // 2) as i:
                agate_pair(S_AGATE, 8, i)

            def out0_pair(base, per=0, i=None):
                for s in range(2):
                    if i is not None:
                        pe.wait_ge(res_step, i * 4 + 2 * s - 2)
                    elif s == 0:
                        pe.wait_ge(b_hi, KC)
                        pe.wait_ge(b_mix, 4 * KC + 4)
                        pe.wait_ge(b_gated, KC + 1)
                    for k in range(8):
                        act = (lambda kk, half: b_act[:, 4 * k + kk, half, :]) if k < 4 else \
                              (lambda kk, half: h[:, 4 * (k - 4) + kk, half, :])
                        if i is None and s == 0 and k >= 4:
                            pe.wait_ge(act_lo, 4 * (k - 3))
                        job_slab(base + 8 * s, k, BX + s, act, k == 0, k == 7, per, i)
            out0_pair(S_OUT0)
            with pe.Fori(1, KC // 2) as i:
                out0_pair(S_OUT0, 16, i)
            ln_totals(1, TOK)

            def token_slab(base, k, kc, bank0, tiles, per=0, i=None):
                s = slab(base, k, per, i)
                for t in range(tiles):
                    tok = slice(t * P, (t + 1) * P)
                    for n, (half, w) in enumerate(((0, w_hi), (0, w_lo), (1, w_hi))):
                        mm = nc.tensor.matmul(banks[:, bank0 + t, :], h[:, kc, half, tok], w[:, s, :],
                                              start=kc == 0 and n == 0, stop=kc == KC - 1 and n == 2)
                mm.then_inc(slab_used, 1)

            pe.wait_ge(res_step, 2 * KC)
            for kc in range(KC):
                pe.wait_ge(h1_lo, kc + 1)
                token_slab(S_K, kc, kc, 0, 4)
            pe.wait_ge(n1_step, 1)
            for kc in range(KC):
                token_slab(S_V, kc, kc, 4, 4)
            for n in range(2):
                pe.wait_ge(rope_done, n + 1)
                for t in range(2):
                    for kv in range(KV):
                        mm = nc.tensor.transpose(banks[:, 2 * n + t, kv * P:(kv + 1) * P],
                                                 k_tok[:, 2 * n + t, kv * HD:(kv + 1) * HD], ident)
                mm.then_inc(k_transposed, 1)
            pe.wait_ge(v_copied, 4)
            for kc in range(KC):
                token_slab(S_Q0, kc, kc, 4, 2)

            def transpose_q(done, bank0):
                pe.wait_ge(rope_done, done)
                for t in range(2):
                    for g in range(GROUP):
                        mm = nc.tensor.transpose(banks[:, bank0 + t, g * P:(g + 1) * P],
                                                 q_tok[:, t, g * HD:(g + 1) * HD], ident)
                mm.then_inc(q_transposed, 1)

            pe.wait_ge(kt_ready, 4)
            transpose_q(3, Q)

            def scores(n, g):
                keys = k_t[:, n, :] if isinstance(n, int) else k_t[:, bass.ds(n, 1), :].rearrange("p o t -> p (o t)")
                for t in range(2):
                    mm = nc.tensor.matmul(banks[:, S + t, :], q_t[:, g, t * P:(t + 1) * P], keys,
                                          start=True, stop=True)
                mm.then_inc(qk_done, 1)

            def gate_slab(base, k, kk0, per, i):
                s = slab(base, k, per, i)
                for kk in range(4):
                    kc, blk = kk0 + kk, slice(kk * P, (kk + 1) * P)
                    nc.tensor.matmul(banks[:, G, :], w_hi[:, s, blk], h[:, kc, :, 0:LAT],
                                     start=kc == 0, stop=False)
                    mm = nc.tensor.matmul(banks[:, G, 0:LAT], w_lo[:, s, blk], h[:, kc, 0, 0:LAT],
                                          start=False, stop=kc == KC - 1)
                mm.then_inc(slab_used, 1)

            def attend(base, n, last, per=0, i=None):
                head = lambda c, k=1: lin(c, GROUP * k, i)
                pe.wait_ge(qt_ready, lin(2 if i is not None else 2 * KV, 2, i))
                scores(n, 0)
                k = 0
                for g in range(GROUP):
                    hd = g if i is not None else g + GROUP * (KV - 1)
                    if not last and g < 2:
                        for q in range(8):
                            token_slab(base, k, 8 * g + q, Q, 2, per, i)
                            k += 1
                    pe.wait_ge(g_sum, head(hd + 1))
                    for q in range(4):
                        gate_slab(base, k, 4 * q, per, i)
                        k += 1
                    pe.wait_ge(p_norm, head(2 * hd + 2, 2))
                    for t in range(2):
                        for c in range(4):
                            mm = nc.tensor.transpose(banks[:, PT + t, c * P:(c + 1) * P],
                                                     prob[:, t, c * P:(c + 1) * P], ident)
                    mm.then_inc(pt_done, 1)
                    if g + 1 < GROUP:
                        scores(n, g + 1)
                    elif not last:
                        transpose_q(lin(4, 1, i), Q)
                    pe.wait_ge(pt_copied, head(2 * hd + 2, 2))
                    pe.wait_ge(o_mul, head(hd + 1))
                    if g == 0:
                        pe.wait_ge(v_staged, lin(1 if i is not None else KV, 1, i))
                    for c in range(4):
                        mm = nc.tensor.matmul(banks[:, PV, 0:LAT], v_stage[:, c, :], prob_t[:, c, :],
                                              start=c == 0, stop=c == 3)
                    mm.then_inc(pv_done, 1)

            with pe.Fori(0, KV - 1) as i:
                attend(S_ATT, i, False, ATT, i)
            attend(S_ATTL, KV - 1, True)

            def out1_pair(base, per=0, i=None, first=False):
                for s in range(2):
                    if first and s == 0:
                        pe.wait_ge(o_lo, HEADS + 1)
                        pe.wait_ge(g_sum, HEADS + 1)
                    elif not first:
                        pe.wait_ge(y_step, i * 4 + 2 * s - 3 if not isinstance(i, int) else 4 * i + 2 * s - 3)
                    for k in range(4):
                        sl = slab(base + 4 * s, k, per, None if isinstance(i, int) else i)
                        for kk in range(4):
                            kc, blk = 4 * k + kk, slice(kk * P, (kk + 1) * P)
                            nc.tensor.matmul(banks[:, s, :], w_hi[:, sl, blk], o_act[:, kc, :, :],
                                             start=kc == 0, stop=False)
                            mm = nc.tensor.matmul(banks[:, s, 0:LAT], w_lo[:, sl, blk], o_act[:, kc, 0, :],
                                                  start=False, stop=kc == KC - 1)
                        mm.then_inc(slab_used, 1)
            out1_pair(S_OUT1, first=True)
            with pe.Fori(1, KC // 2 - 1) as i:
                out1_pair(S_OUT1, 8, i)
            out1_pair(S_OUT1 + 8 * (KC // 2 - 1), 0, KC // 2 - 1)
            ln_totals(2, LAT)

        @block.scalar
        def _(act):
            def head_of(base, k, per=0, i=None, count=1):
                p = base + k + AHEAD
                if p >= SLABS:
                    return
                slot = p % RING
                act.wait_ge(slab_landed[slot], lin(16 * (p // RING + 1), 16 * per // RING, i))
                if p >= RING:
                    act.wait_ge(slab_used, lin(p - RING + 1, per, i))
                nc.scalar.activation(w_hi[:, slot, :], w_raw[:, slot, :], ACT.Copy).then_inc(hi_ready, count)

            def copy_mod_row(bank, used, count, n):
                act.wait_ge(used, count)
                act.wait_ge(mod_cols_ready, n)
                nc.scalar.activation(mod_row[0:4, :], banks[0:4, bank, :], ACT.Copy).then_inc(mod_row_ready, 1)

            def ln_root(r, width):
                act.wait_ge(ln_step, 5 * r + 4)
                nc.scalar.activation(t2[:, 0:width], t2[:, 0:width], ACT.Sqrt).then_inc(ln_sqrt, 1)

            act.wait_ge(params_in, 16)
            nc.scalar.activation(cond_s, cond, ACT.Sigmoid).then_inc(cond_sig, 1)
            act.wait_ge(cond_mul, 1)
            c4v = c4[:, 0:4 * KC].rearrange("p (k c s) -> p k c s", c=2, s=2)
            nc.scalar.activation(c4v[:, :, :, 0], cond_s, ACT.Copy).then_inc(cond_hi, 1)

            def h_head(c, i=None):
                at = slice(c, c + 1) if i is None else bass.ds(i * 4 + c - 4, 1)
                sc = mod[:, KC + c:KC + c + 1, :] if i is None else mod[:, bass.ds(i * 4 + c + KC - 4, 1), :]
                sh = mod[:, at, :]
                for half in range(2):
                    tok = slice(half * LAT, (half + 1) * LAT)
                    nc.scalar.activation(h[:, at, 0, tok].rearrange("p o t -> p (o t)"),
                                         u[:, at, tok].rearrange("p o t -> p (o t)"), ACT.Identity,
                                         scale=sc[:, 0, half:half + 1], bias=sh[:, 0, half:half + 1]).then_inc(h_hi, 1)

            def start_turn(i=None):
                for m in range(KC):
                    k = 2 * m
                    turn_landed(act, k, i)
                    if i is not None or m >= RING:
                        act.wait_ge(start_used, lin(k - 2 * RING + 1 + START_RING, TURN, i))
                    nc.scalar.activation(w_hi[:, m % RING, :], start_raw[:, k % START_RING, :],
                                         ACT.Copy).then_inc(start_hi, 1)
                    if m == KC // 2 + 4:
                        copy_mod_row(VAL, start_used, lin(KC + START_RING, TURN, i), lin(1, 2, i))
                    if i is not None and m % 3 == 2 and m < 12:
                        if m == 2:
                            act.wait_ge(scale1, i)
                            act.wait_ge(xall_in, 16)
                        h_head(m // 3, i)
                copy_mod_row(GLU, start_used, lin(TURN + START_RING, TURN, i), lin(2, 2, i))

            start_turn()
            with act.Fori(1, 4) as i:
                start_turn(i)
            act.wait_ge(scale1, 4)
            for c in range(KC - 4, KC):
                h_head(c)
            for k in range(-AHEAD, 0):
                head_of(0, k)

            def mix_step(i, latent_only):
                row = lambda buf: buf[:, bass.ds(i, 1), :].rearrange("p o t -> p (o t)")
                for k in range(MIX):
                    pos = (k + AHEAD) % MIX
                    if not by_vector(pos, latent_only):
                        head_of(S_MIX, k, MIX, i, counts(pos, latent_only))
                    if k == 11:
                        act.wait_ge(slab_used, i * MIX + S_MIX + 12)
                        act.wait_ge(b_mix, i * 4 + 2)
                        nc.scalar.activation(t2, banks[:, GLU, :], ACT.Sigmoid).then_inc(glu_sig, 1)
                    if k == 19:
                        act.wait_ge(slab_used, i * MIX + S_MIX + 20)
                        act.wait_ge(b_mix, i * 4 + 4)
                        nc.scalar.activation(t1, banks[:, BX, :], ACT.Copy).then_inc(bx_copied, 1)
                    if k == 34 and not latent_only:
                        copy_mod_row(MOD, slab_used, i * MIX + S_MIX + 35, i + 9)
                    if k == 35:
                        act.wait_ge(slab_used, i * MIX + S_MIX + 36)
                        act.wait_ge(a_gated, i + 2)
                        nc.scalar.activation(t2, banks[:, BG, :], ACT.Sigmoid).then_inc(glu_sig, 1)
                act.wait_ge(conv_tap, i * (TAPS_A + 1) + TAPS_A + 1)
                nc.scalar.activation(t3, row(u), ACT.Square).then_inc(conv_sq, 1)
                act.wait_ge(b_mix, i * 4 + 4 + 3)
                nc.scalar.activation(b_act[:, bass.ds(i, 1), 0, :].rearrange("p o t -> p (o t)"), t1,
                                     ACT.Copy).then_inc(b_hi, 1)
            with act.Fori(0, BOTH_STEPS) as i:
                mix_step(i, False)
            with act.Fori(BOTH_STEPS, KC) as i:
                mix_step(i, True)

            def norm_a_affine(j, jn):
                act.wait_ge(an_step, lin(3 * jn + 2, 6, None if j is None else j[1]))
                uj = chunk(u, j, jn)
                g = per_chunk(norm_a_g, j, jn)
                b = per_chunk(norm_a_b, j, jn)
                nc.scalar.activation(t3, uj, ACT.Sigmoid, scale=g, bias=b).then_inc(an_affine, 1)
                nc.scalar.activation(uj, uj, ACT.Identity, scale=g, bias=b).then_inc(an_affine, 1)

            def agate_act(base, per=0, i=None):
                for s in range(2):
                    for k in range(4):
                        head_of(base + 4 * s, k, per, i)
                        if i is None and s == 0 and k == 0:
                            ln_root(0, TOK)
                        if k == 0:
                            norm_a_affine(None if i is None else (2, i), s)
                    act.wait_ge(slab_used, lin(base + 4 * s + 4, per, i))
                    if i is not None or s:
                        act.wait_ge(ag_mul, lin(2 * s, 4, i))
                    else:
                        act.wait_ge(mod_cols_ready, 25)
                    nc.scalar.activation(t4, banks[:, s, :], ACT.Sigmoid).then_inc(ag_sig, 1)

            agate_act(S_AGATE)
            with act.Fori(1, KC // 2) as i:
                agate_act(S_AGATE, 8, i)

            def out0_act(base, per=0, i=None):
                for s in range(2):
                    for k in range(8):
                        head_of(base + 8 * s, k, per, i)
                        if i is None and s == 0 and k < 4:
                            if k == 0:
                                act.wait_ge(slab_used, S_OUT0)
                                act.wait_ge(ag_mul, 2 * KC)
                            for c in range(4 * k, 4 * k + 4):
                                nc.scalar.activation(h[:, c, 0, :], u[:, c, :], ACT.Copy).then_inc(act_hi, 1)
                    act.wait_ge(x_landed[s], lin(16, 16, i))
                    if i is not None or s:
                        act.wait_ge(res_step, lin(2 * s, 4, i))
                    nc.scalar.activation(t3, x_in[:, s, :], ACT.Copy, scale=ALPHA).then_inc(x_scaled, 1)
                    act.wait_ge(res_step, lin(2 * s + 2, 4, i))
                    if i is not None or s:
                        act.wait_ge(res_stats, lin(2 * s, 4, i))
                    nc.scalar.activation(t4, chunk(u, None if i is None else (2, i), s),
                                         ACT.Square).then_inc(res_sq, 1)

            out0_act(S_OUT0)
            with act.Fori(1, KC // 2) as i:
                out0_act(S_OUT0, 16, i)
            ln_root(1, TOK)
            for c in range(KC):
                act.wait_ge(n1_step, 2 * c + 3)
                for half in range(2):
                    tok = slice(half * LAT, (half + 1) * LAT)
                    nc.scalar.activation(h[:, c, 0, tok], u[:, c, tok], ACT.Identity,
                                         scale=mod[:, 48 + KC + c, half:half + 1],
                                         bias=mod[:, 48 + c, half:half + 1]).then_inc(h1_hi, 1)
                head_of(S_K, c)

            def head_sums(bank0, heads, batch, i=None):
                for n in heads:
                    if batch and n == 0:
                        act.wait_ge(head_scaled, lin(8 * batch, 8, i))
                    if batch or n > 1 or i is not None:
                        act.wait_ge(head_squares, lin(8 * batch + n - 1, 8, i))
                    nc.scalar.activation(squares[:, n % 2, :], banks[:, bank0 + n // 4, (n % 4) * HD:(n % 4 + 1) * HD],
                                         ACT.Square, accum_out=sumsq[:, n:n + 1]).then_inc(head_squares, 1)

            def head_scales(dst, bank0, heads, batch=None):
                if batch is not None:
                    act.wait_ge(head_power, batch)
                for n in heads:
                    d = slice((n % 4) * HD, (n % 4 + 1) * HD)
                    nc.scalar.activation(dst[:, n // 4, d], banks[:, bank0 + n // 4, d], ACT.Identity,
                                         scale=sumsq[:, n:n + 1]).then_inc(head_scaled, 1)

            for kc in range(KC):
                head_of(S_V, kc)
                if kc == 0:
                    act.wait_ge(slab_used, S_V)
                if kc in (0, 1):
                    head_sums(0, range(4 * kc, 4 * kc + 4), 0)
                if kc in (3, 4):
                    head_scales(k_tok[:, 0:2, :], 0, range(4 * kc - 12, 4 * kc - 8), 1)
                if kc in (5, 6):
                    head_sums(2, range(4 * kc - 20, 4 * kc - 16), 1)
                if kc in (8, 9):
                    head_scales(k_tok[:, 2:4, :], 2, range(4 * kc - 32, 4 * kc - 28), 2)
            act.wait_ge(slab_used, S_Q0)
            for t in range(4):
                nc.scalar.activation(v_tok[:, t, :], banks[:, 4 + t, :], ACT.Copy).then_inc(v_copied, 1)

            def copy_transposed(dst, bank0, tile0, ready):
                for t in range(2):
                    tok = slice((tile0 + t) * P, (tile0 + t + 1) * P)
                    nc.scalar.activation(dst[:, :, tok], banks[:, bank0 + t, :].rearrange("p (g t) -> p g t", g=4),
                                         ACT.Copy).then_inc(ready, 1)

            for kc in range(KC):
                head_of(S_Q0, kc)
                if kc in (0, 1):
                    act.wait_ge(k_transposed, kc + 1)
                    copy_transposed(k_t, 2 * kc, 2 * kc, kt_ready)
            act.wait_ge(slab_used, S_ATT)
            head_sums(4, range(8), 2)
            head_scales(q_tok, 4, range(8), 3)
            act.wait_ge(q_transposed, 1)
            copy_transposed(q_t, Q, 0, qt_ready)

            def attend_act(base, last, per=0, i=None):
                head = lambda c, k=1: lin(c, GROUP * k, i)
                k = 0
                for g in range(GROUP):
                    hd = g if i is not None else g + GROUP * (KV - 1)
                    slabs = 12 if not last and g < 2 else 4
                    for m in range(slabs):
                        head_of(base, k, per, i)
                        k += 1
                        if m == 0:
                            for t in range(2):
                                if t == 0:
                                    act.wait_ge(max_step, head(2 * hd + 2, 2))
                                nc.scalar.activation(prob[:, t, :], banks[:, S + t, :], ACT.Exp, scale=SCALE,
                                                     bias=negmax[:, t:t + 1],
                                                     accum_out=rowsum[:, t:t + 1]).then_inc(p_exp, 1)
                            if hd or i is not None:
                                if g:
                                    o_head(hd - 1, i)
                        if not last and g == 1 and m == 9:
                            act.wait_ge(slab_used, lin(base + 20, per, i))
                        if not last and g == 1 and m in (9, 10):
                            head_sums(Q, range(4 * m - 36, 4 * m - 32), 3, i)
                        if not last and g == 2 and m in (1, 2):
                            head_scales(q_tok, Q, range(4 * m - 4, 4 * m), lin(4, 1, i))
                    act.wait_ge(slab_used, lin(base + k, per, i))
                    act.wait_ge(o_lo, head(hd + 1))
                    nc.scalar.activation(t1[:, 0:LAT], banks[:, G, LAT:TOK], ACT.Copy).then_inc(g_part, 1)
                    act.wait_ge(pt_done, head(hd + 1))
                    for t in range(2):
                        nc.scalar.activation(prob_t[:, :, t * P:(t + 1) * P],
                                             banks[:, PT + t, :].rearrange("p (c t) -> p c t", c=4),
                                             ACT.Copy).then_inc(pt_copied, 1)
                    act.wait_ge(g_sum, head(hd + 2))
                    nc.scalar.activation(t2[:, 0:LAT], t1[:, 0:LAT], ACT.Tanh, scale=0.5).then_inc(g_tanh, 1)
                if not last:
                    act.wait_ge(q_transposed, lin(2, 1, i))
                    copy_transposed(q_t, Q, 0, qt_ready)
                o_head(GROUP - 1 if i is not None else HEADS - 1, i)

            def o_head(hd, i):
                act.wait_ge(o_mul, lin(hd + 2, GROUP, i))
                at = bass.ds(i * GROUP + hd, 1) if i is not None else slice(hd, hd + 1)
                nc.scalar.activation(o_act[:, at, 0, :].rearrange("p o t -> p (o t)"), t1[:, 0:LAT],
                                     ACT.Copy).then_inc(o_hi, 1)

            with act.Fori(0, KV - 1) as i:
                attend_act(S_ATT, False, ATT, i)
            attend_act(S_ATTL, True)

            def out1_read(s, jn, i=None):
                j = None if i is None else (2, i)
                at = lambda c, m: lin(m * jn + c, 2 * m, i)
                first = i is None and jn == 0
                if not first:
                    act.wait_ge(y_step, at(0, 2))
                act.wait_ge(slab_used, at(S_OUT1 + 4, 4))
                gate = mod[:, bass.ds(i * 2 + 80 + jn, 1), 0] if i is not None else mod[:, 80 + jn:81 + jn, 0]
                nc.scalar.activation(t1[:, 0:LAT], banks[:, s, LAT:TOK], ACT.Identity,
                                     scale=gate).then_inc(y_part, 1)
                uj = chunk(u, j, jn)[:, 0:LAT]
                nc.scalar.activation(t3[:, 0:LAT], uj, ACT.Identity, scale=per_chunk(alpha_g, j, jn),
                                     bias=per_chunk(alpha_b, j, jn)).then_inc(x1_scaled, 1)

            def out1_act(base, per=0, i=None, pair=0):
                for s in range(2):
                    jn = 2 * pair + s - 1
                    for k in range(4):
                        head_of(base + 4 * s, k, per, i)
                        if i is None and jn < 0:
                            continue
                        if k == 0:
                            out1_read(1 - s, jn, i)

            out1_act(S_OUT1)
            with act.Fori(1, KC // 2 - 1) as i:
                out1_act(S_OUT1, 8, i)
            out1_act(S_OUT1 + 8 * (KC // 2 - 1), pair=KC // 2 - 1)
            out1_read(1, KC - 1)
            ln_root(2, LAT)
            for c in range(KC):
                act.wait_ge(fin_step, 2 * c + 2)
                nc.scalar.activation(u[:, c, 0:LAT], u[:, c, 0:LAT], ACT.Identity, scale=ln_g[:, KC + c:KC + c + 1],
                                     bias=ln_b[:, KC + c:KC + c + 1]).then_inc(fin_ready, 1)

        @block.vector
        def _(dve):
            V = nc.vector

            def tail_of(base, k, per=0, i=None):
                p = base + k + AHEAD
                if p >= SLABS:
                    return
                slot = p % RING
                dve.wait_ge(hi_ready, lin(p + 1, per, i))
                V.tensor_tensor(w_lo[:, slot, :], w_raw[:, slot, :], w_hi[:, slot, :].bitcast(F32),
                                ALU.subtract).then_inc(lo_ready, 1)

            def mod_bias(bank, n, col, i_per=0, i=None):
                dve.wait_ge(mod_cols_ready, n)
                at = bass.ds(i * i_per + col, 4) if i is not None else slice(col, col + 4)
                V.tensor_tensor(mod[:, at, :], banks[:, bank, 0:8].rearrange("p (q c) -> p q c", c=2),
                                b_mod[:, at].unsqueeze(2).to_broadcast([P, 4, 2]), ALU.add).then_inc(mod_ready, 1)

            def clear_stats():
                V.memset(banks[:, SUM, :], 0.0).then_inc(cleared, 1)
                V.memset(banks[:, SQS, :], 0.0).then_inc(cleared, 1)

            def ln_copies(r, width, stats_done):
                stats_done()
                V.tensor_copy(t1[:, 0:width], banks[:, SUM, 0:width]).then_inc(ln_copy, 1)
                V.tensor_copy(t2[:, 0:width], banks[:, SQS, 0:width]).then_inc(ln_copy, 1)

            def ln_moments(r, width):
                a, b, c = t1[:, 0:width], t2[:, 0:width], t3[:, 0:width]
                dve.wait_ge(ln_sums, r + 1)
                V.tensor_scalar(a, banks[:, SUM, 0:width], 1.0 / D, None, ALU.mult).then_inc(ln_step, 1)
                dve.wait_ge(ln_step, 5 * r + 1)
                V.tensor_tensor(c, a, a, ALU.mult).then_inc(ln_step, 1)
                dve.wait_ge(ln_step, 5 * r + 2)
                V.scalar_tensor_tensor(out=b, in0=banks[:, SQS, 0:width], scalar=1.0 / D, in1=c,
                                       op0=ALU.mult, op1=ALU.subtract).then_inc(ln_step, 1)
                dve.wait_ge(ln_step, 5 * r + 3)
                V.tensor_scalar(b, b, 0.0, LN_EPS, ALU.max, ALU.add).then_inc(ln_step, 1)
                if r < 2:
                    V.memset(banks[:, SUM, :], 0.0).then_inc(cleared, 1)
                    V.memset(banks[:, SQS, :], 0.0).then_inc(cleared, 1)
                dve.wait_ge(ln_sqrt, r + 1)
                V.reciprocal(b, b).then_inc(ln_step, 1)
                dve.wait_ge(ln_step, 5 * r + 5)

            dve.sem_inc(start_used, START_RING)
            dve.sem_inc(mod_ready, 2)
            dve.sem_inc(a_gated, 1)
            dve.sem_inc(b_gated, 1)
            dve.sem_inc(b_mix, 4)
            dve.sem_inc(g_sum, 1)
            dve.sem_inc(o_mul, 1)
            dve.sem_inc(o_lo, 1)
            dve.sem_inc(mod_cols_ready, 1)
            V.memset(pads[:, :], 0.0).then_inc(cleared, 1)
            V.memset(c4[:, 4 * KC:].bitcast(F32), 0.0).then_inc(cleared, 1)
            V.memset(neg_half, -0.5).then_inc(cleared, 1)
            clear_stats()
            V.memset(c_row[:, :], 0.0).then_inc(cleared, 1)
            dve.wait_ge(params_in, 16)
            dve.wait_ge(cond_sig, 1)
            V.tensor_tensor(cond_s, cond_s, cond, ALU.mult).then_inc(cond_mul, 1)
            dve.wait_ge(cond_mul, 1)
            dve.wait_ge(cleared, 6)
            cr = c_row[:, 0:4 * KC].rearrange("p (k c s) -> p k c s", c=2, s=2)
            V.tensor_copy(cr[:, :, :, 0], cond_s).then_inc(cond_mul, 1)
            dve.wait_ge(cond_hi, 1)
            c4v = c4[:, 0:4 * KC].rearrange("p (k c s) -> p k c s", c=2, s=2)
            V.tensor_tensor(c4v[:, :, :, 1], cond_s, c4v[:, :, :, 0].bitcast(F32), ALU.subtract).then_inc(cond_lo, 1)

            def h_tail(q, i=None):
                c = lambda n, m=1: lin(m * q + n - (0 if i is None else 4 * m), 4 * m, i)
                at = slice(q, q + 1) if i is None else bass.ds(i * 4 + q - 4, 1)
                at_sc = slice(q + KC, q + KC + 1) if i is None else bass.ds(i * 4 + q + KC - 4, 1)
                t = tmp[:, q % 2, :]
                for half in range(2):
                    tok = slice(half * LAT, (half + 1) * LAT)
                    V.tensor_scalar(t[:, tok], u[:, at, tok].rearrange("p o t -> p (o t)"),
                                    mod[:, at_sc, half], mod[:, at, half], ALU.mult, ALU.add).then_inc(h_mod, 1)
                dve.wait_ge(h_mod, c(2, 2))
                dve.wait_ge(h_hi, c(2, 2))
                hq = lambda s: h[:, at, s, :].rearrange("p o t -> p (o t)")
                V.tensor_tensor(hq(1), t, hq(0).bitcast(F32), ALU.subtract).then_inc(h_lo, 1)

            def start_turn(i=None):
                for m in range(KC):
                    dve.wait_ge(start_hi, lin(m + 1, KC, i))
                    V.tensor_tensor(w_lo[:, m % RING, :], start_raw[:, (2 * m) % START_RING, :],
                                    w_hi[:, m % RING, :].bitcast(F32), ALU.subtract).then_inc(start_lo, 1)
                    if m == KC // 2 + 7:
                        mod_bias(VAL, lin(2, 2, i), 0, 4, i)
                    if i is not None and m % 3 == 2 and m < 12:
                        if m == 2:
                            dve.wait_ge(xall_in, 16)
                        h_tail(m // 3, i)
                mod_bias(GLU, lin(3, 2, i), KC, 4, i)
                dve.wait_ge(mod_ready, lin(4, 2, i))
                sc = mod[:, KC:KC + 4, :] if i is None else mod[:, bass.ds(i * 4 + KC, 4), :]
                V.tensor_scalar(sc, sc, 1.0, None, ALU.add).then_inc(scale1, 1)
                dve.wait_ge(scale1, lin(1, 1, i))

            start_turn()
            with dve.Fori(1, 4) as i:
                start_turn(i)
            for c in range(KC - 4, KC):
                h_tail(c)
            for k in range(-AHEAD, 0):
                tail_of(0, k)

            def add_mod_slab(kc, pos, latent_only, i):
                slot = pos % RING
                dve.wait_ge(slab_landed[slot], lin(16 * (pos // RING + 1), 16 * MIX // RING, i))
                halves = 1 if latent_only else 2
                for c in range(halves):
                    if kc == 0:
                        op = V.tensor_scalar(mod_sum[:, c, :], w_raw[:, slot, :], cond_s[:, kc, c:c + 1], None, ALU.mult)
                    else:
                        if c == 0:
                            dve.wait_ge(lo_ready, lin(S_MIX + pos - 1, MIX, i))
                        op = V.scalar_tensor_tensor(out=mod_sum[:, c, :], in0=w_raw[:, slot, :],
                                                    scalar=cond_s[:, kc, c:c + 1], in1=mod_sum[:, c, :],
                                                    op0=ALU.mult, op1=ALU.add)
                op.then_inc(lo_ready, 1)

            def mix_step(i, latent_only):
                ui = u[:, bass.ds(i, 1), :].rearrange("p o t -> p (o t)")
                u3 = u[:, bass.ds(i, 1), :].rearrange("p o (s t) -> p (o s) t", s=2)
                t33 = t3.rearrange("p (s t) -> p s t", s=2)
                t13 = t1.rearrange("p (s t) -> p s t", s=2)
                taps = iter(range(TAPS_A))
                if latent_only:
                    taps_at = dict(enumerate([1, 1, 1] + [1, 1] * 6 + [0, 1, 0, 0] + [1, 1, 1, 3, 3, 2, 2, 2], 13))
                else:
                    taps_at = dict(enumerate([0, 1, 0] + [1, 2, 1, 1] * 3 + [0, 1, 1, 0] + [1, 1, 1, 2, 2, 2, 2, 2], 13))
                assert sum(taps_at.values()) == TAPS_A and max(taps_at) < MIX

                def conv_a_tap():
                    n = next(taps, None)
                    if n is None:
                        return
                    src, w = pad_a[:, :, n:n + LAT], conv_a_w[:, bass.ds(i * TAPS_A + n, 1)]
                    acc = (u3, t33)[n % 2]
                    if n == 0:
                        dve.wait_ge(a_gated, i + 2)
                        V.tensor_scalar(acc, src, w, conv_a_b[:, bass.ds(i, 1)], ALU.mult,
                                        ALU.add).then_inc(conv_tap, 1)
                    elif n == 1:
                        V.tensor_scalar(acc, src, w, None, ALU.mult).then_inc(conv_tap, 1)
                    else:
                        dve.wait_ge(conv_tap, i * (TAPS_A + 1) + n - 1)
                        V.scalar_tensor_tensor(out=acc, in0=src, scalar=w, in1=acc, op0=ALU.mult,
                                               op1=ALU.add).then_inc(conv_tap, 1)

                for k in range(MIX):
                    pos = (k + AHEAD) % MIX
                    if by_vector(pos, latent_only):
                        add_mod_slab(STEP[pos][1], pos, latent_only, i)
                    else:
                        tail_of(S_MIX, k, MIX, i)
                    if k == 12:
                        dve.wait_ge(glu_sig, i * 2 + 1)
                        V.tensor_tensor(pad_a[:, :, PAD_A:PAD_A + LAT],
                                        banks[:, VAL, :].rearrange("p (s t) -> p s t", s=2),
                                        t2.rearrange("p (s t) -> p s t", s=2), ALU.mult).then_inc(a_gated, 1)
                    for _ in range(taps_at.get(k, 0)):
                        conv_a_tap()
                    if k == 28:
                        dve.wait_ge(slab_used, i * MIX + S_MIX + 28)
                        dve.wait_ge(bx_copied, i + 1)
                        V.tensor_tensor(pad_b[:, :, PAD_B:PAD_B + LAT],
                                        banks[:, BC, :].rearrange("p (s t) -> p s t", s=2), t13,
                                        ALU.mult).then_inc(b_gated, 1)
                    if k in (29, 30, 31):
                        n = k - 29
                        src, w = pad_b[:, :, n:n + LAT], conv_b_w[:, bass.ds(i * TAPS_B + n, 1)]
                        if n == 0:
                            dve.wait_ge(b_gated, i + 2)
                            V.tensor_scalar(t13, src, w, None, ALU.mult).then_inc(b_tap, 1)
                        else:
                            dve.wait_ge(b_tap, i * TAPS_B + n)
                            V.scalar_tensor_tensor(out=t13, in0=src, scalar=w, in1=t13, op0=ALU.mult,
                                                   op1=ALU.add).then_inc(b_tap, 1)
                    if k == 37:
                        dve.wait_ge(glu_sig, i * 2 + 2)
                        V.tensor_tensor(t2, banks[:, BG, :], t2, ALU.mult).then_inc(b_mix, 1)
                    if k == 38:
                        dve.wait_ge(b_tap, i * TAPS_B + TAPS_B)
                        dve.wait_ge(b_mix, i * 4 + 4 + 1)
                        V.tensor_tensor(t1, t1, t2, ALU.mult).then_inc(b_mix, 1)
                        mod_bias(MOD, i + 10, 32, 4, i)
                dve.wait_ge(conv_tap, i * (TAPS_A + 1) + TAPS_A)
                V.tensor_tensor(ui, ui, t3, ALU.add).then_inc(conv_tap, 1)
                dve.wait_ge(slab_used, i * MIX + S_MIX + MIX)
                dve.wait_ge(b_mix, i * 4 + 4 + 2)
                V.tensor_tensor(t1, banks[:, BB, :], t1, ALU.mult).then_inc(b_mix, 1)
                dve.wait_ge(conv_tap, i * (TAPS_A + 1) + TAPS_A + 1)
                V.tensor_tensor(banks[:, SUM, :], banks[:, SUM, :], ui, ALU.add).then_inc(a_stats, 1)
                dve.wait_ge(b_hi, i + 1)
                bi = lambda s: b_act[:, bass.ds(i, 1), s, :].rearrange("p o t -> p (o t)")
                V.tensor_tensor(bi(1), t1, bi(0).bitcast(F32), ALU.subtract).then_inc(b_mix, 1)
                dve.wait_ge(conv_sq, i + 1)
                V.tensor_tensor(banks[:, SQS, :], banks[:, SQS, :], t3, ALU.add).then_inc(a_stats, 1)
            with dve.Fori(0, BOTH_STEPS) as i:
                mix_step(i, False)
            with dve.Fori(BOTH_STEPS, KC) as i:
                mix_step(i, True)

            def agate_dve(base, per=0, i=None):
                j = None if i is None else (2, i)
                for s in range(2):
                    uj = chunk(u, j, s)
                    if i is None and s == 0:
                        dve.wait_ge(b_hi, KC)
                        dve.wait_ge(b_mix, 4 * KC + 4)
                        ln_copies(0, TOK, lambda: dve.wait_ge(a_stats, 2 * KC))
                    for k in range(4):
                        tail_of(base + 4 * s, k, per, i)
                        if k == 0:
                            if i is None and s == 0:
                                ln_moments(0, TOK)
                            V.tensor_tensor(uj, uj, t1, ALU.subtract).then_inc(an_step, 1)
                            dve.wait_ge(an_step, lin(3 * s + 1, 6, i))
                            V.tensor_tensor(uj, uj, t2, ALU.mult).then_inc(an_step, 1)
                        if k == 2:
                            dve.wait_ge(an_affine, lin(2 * s + 2, 4, i))
                            V.tensor_tensor(uj, uj, t3, ALU.mult).then_inc(an_step, 1)
                    dve.wait_ge(ag_sig, lin(s + 1, 2, i))
                    V.tensor_tensor(t4, banks[:, s, :], t4, ALU.mult).then_inc(ag_mul, 1)
                    dve.wait_ge(ag_mul, lin(2 * s + 1, 4, i))
                    dve.wait_ge(an_step, lin(3 * s + 3, 6, i))
                    V.tensor_tensor(uj, uj, t4, ALU.mult).then_inc(ag_mul, 1)

            agate_dve(S_AGATE)
            with dve.Fori(1, KC // 2) as i:
                agate_dve(S_AGATE, 8, i)

            def out0_dve(base, per=0, i=None):
                j = None if i is None else (2, i)
                for s in range(2):
                    uj = chunk(u, j, s)
                    for k in range(8):
                        tail_of(base + 8 * s, k, per, i)
                        if i is None and s == 0 and k < 4:
                            for c in range(4 * k, 4 * k + 4):
                                dve.wait_ge(act_hi, c + 1)
                                V.tensor_tensor(h[:, c, 1, :], u[:, c, :], h[:, c, 0, :].bitcast(F32),
                                                ALU.subtract).then_inc(act_lo, 1)
                    dve.wait_ge(slab_used, lin(base + 8 * s + 8, per, i))
                    dve.wait_ge(x_scaled, lin(s + 1, 2, i))
                    for half in range(2):
                        tok = slice(half * LAT, (half + 1) * LAT)
                        gate = mod[:, 32 + s:33 + s, half] if i is None else mod[:, bass.ds(i * 2 + 32 + s, 1), half]
                        V.scalar_tensor_tensor(out=uj[:, tok], in0=banks[:, BX + s, tok], scalar=gate,
                                               in1=t3[:, tok], op0=ALU.mult, op1=ALU.add).then_inc(res_step, 1)
                    dve.wait_ge(res_step, lin(2 * s + 2, 4, i))
                    V.tensor_tensor(banks[:, SUM, :], banks[:, SUM, :], uj, ALU.add).then_inc(res_stats, 1)
                    dve.wait_ge(res_sq, lin(s + 1, 2, i))
                    V.tensor_tensor(banks[:, SQS, :], banks[:, SQS, :], t4, ALU.add).then_inc(res_stats, 1)

            out0_dve(S_OUT0)
            with dve.Fori(1, KC // 2) as i:
                out0_dve(S_OUT0, 16, i)
            sc1 = mod[:, 48 + KC:48 + 2 * KC, :]
            sh1 = mod[:, 48:48 + KC, :]
            dve.wait_ge(mod_ready, 2 + 24)
            V.tensor_scalar(sc1, sc1, 1.0, None, ALU.add).then_inc(scale1, 1)
            dve.wait_ge(scale1, 5)
            wide = lambda a: a.unsqueeze(2).to_broadcast([P, KC, 2])
            V.tensor_tensor(cond_s, sc1, wide(ln_b[:, 0:KC]), ALU.mult).then_inc(fold1, 1)
            V.tensor_scalar(alpha_g, ln_g[:, 0:KC], ALPHA, None, ALU.mult).then_inc(fold1, 1)
            dve.wait_ge(fold1, 2)
            V.tensor_tensor(sc1, sc1, wide(ln_g[:, 0:KC]), ALU.mult).then_inc(fold1, 1)
            V.tensor_tensor(sh1, sh1, cond_s, ALU.add).then_inc(fold1, 1)
            V.tensor_scalar(alpha_b, ln_b[:, 0:KC], ALPHA, None, ALU.mult).then_inc(fold1, 1)
            ln_copies(1, TOK, lambda: dve.wait_ge(res_stats, 2 * KC))
            ln_moments(1, TOK)
            dve.wait_ge(fold1, 5)
            dve.sem_inc(n1_step, 1)
            def h1_tail(c):
                dve.wait_ge(h1_mod, 2 * c + 2)
                dve.wait_ge(h1_hi, 2 * c + 2)
                V.tensor_tensor(h[:, c, 1, :], tmp[:, 2 + c % 2, :], h[:, c, 0, :].bitcast(F32),
                                ALU.subtract).then_inc(h1_lo, 1)

            for c in range(KC):
                V.tensor_tensor(u[:, c, :], u[:, c, :], t1, ALU.subtract).then_inc(n1_step, 1)
                if c:
                    h1_tail(c - 1)
                dve.wait_ge(n1_step, 2 * c + 2)
                V.tensor_tensor(u[:, c, :], u[:, c, :], t2, ALU.mult).then_inc(n1_step, 1)
                if c:
                    tail_of(S_K, c - 1)
                dve.wait_ge(n1_step, 2 * c + 3)
                for half in range(2):
                    tok = slice(half * LAT, (half + 1) * LAT)
                    V.tensor_scalar(tmp[:, 2 + c % 2, tok], u[:, c, tok], mod[:, 48 + KC + c, half:half + 1],
                                    mod[:, 48 + c, half:half + 1], ALU.mult, ALU.add).then_inc(h1_mod, 1)
            h1_tail(KC - 1)
            tail_of(S_K, KC - 1)

            big, big2 = tmp[:, 2:4, :], x_in[:, :, :]
            by_head = lambda a: a.rearrange("p t (g d) -> p (t g) d", d=HD)

            def head_means(done):
                dve.wait_ge(head_squares, done)
                V.tensor_scalar(sumsq, sumsq, 1.0 / HD, RMS_EPS, ALU.mult, ALU.add).then_inc(head_mean, 1)

            def gain_k(x, done, sem_done):
                dve.wait_ge(head_scaled, done)
                V.tensor_tensor(by_head(x), by_head(x), gains[:, 1, :].unsqueeze(1).to_broadcast([P, 8, HD]),
                                ALU.mult).then_inc(sem_done, 1)

            def rotate_cos(x):
                for t in range(2):
                    per_head = lambda a: a[:, t, :].rearrange("p (g d) -> p g d", d=HD)
                    V.tensor_tensor(per_head(big), per_head(x), rope_cos[:, t, :].unsqueeze(1).to_broadcast([P, GROUP, HD]),
                                    ALU.mult).then_inc(rope_step, 1)

            def halves(a, t):
                return a[:, t, :].rearrange("p (g r f e) -> p g r f e", g=GROUP, r=2, f=2)

            def rotate_sin(x):
                for t in range(2):
                    sines = rope_sin[:, t, :].rearrange("p (r f e) -> p r f e", r=2, f=2)
                    for f in range(2):
                        V.tensor_tensor(halves(big2, t)[:, :, :, f, :], halves(x, t)[:, :, :, 1 - f, :],
                                        sines[:, :, f, :].unsqueeze(1).to_broadcast([P, GROUP, 2, 32]),
                                        ALU.mult).then_inc(rope_step, 1)

            def rotate_add(x, steps):
                dve.wait_ge(rope_step, steps)
                V.tensor_tensor(x, big, big2, ALU.add).then_inc(rope_done, 1)

            k_lat, k_ctx = k_tok[:, 0:2, :], k_tok[:, 2:4, :]
            dve.wait_ge(rope_in, 16)
            dve.wait_ge(h1_lo, KC)
            for kc in range(KC):
                tail_of(S_V, kc)
                if kc == 2:
                    head_means(8)
                if kc == 5:
                    gain_k(k_lat, 8, rope_step)
                if kc == 6:
                    dve.wait_ge(rope_step, 1)
                    rotate_cos(k_lat)
                if kc == 7:
                    head_means(16)
                if kc == 8:
                    rotate_sin(k_lat)
                if kc == 9:
                    rotate_add(k_lat, ROPE_K - 1)
                if kc == 10:
                    gain_k(k_ctx, 16, rope_done)
                if kc == 12:
                    dve.wait_ge(rope_done, 2)
                    V.tensor_tensor(rope_cos, rope_cos, gains[:, 0, :].unsqueeze(1).to_broadcast([P, 2, HD]),
                                    ALU.mult).then_inc(rope_step, 1)
                    quarters = lambda a: a.rearrange("p t (r f e) -> p t r f e", r=2, f=2)
                    g4 = gains[:, 0, :].rearrange("p (r f e) -> p r f e", r=2, f=2)
                    for f in range(2):
                        sn = quarters(rope_sin)[:, :, :, f, :]
                        V.tensor_tensor(sn, sn, g4[:, :, 1 - f, :].unsqueeze(1).to_broadcast([P, 2, 2, 32]),
                                        ALU.mult).then_inc(rope_step, 1)
            for kc in range(KC):
                tail_of(S_Q0, kc)
            head_means(24)
            dve.wait_ge(head_scaled, 24)
            dve.wait_ge(rope_step, ROPE_BASE)
            rotate_cos(q_tok)
            rotate_sin(q_tok)
            rotate_add(q_tok[:, :, :], ROPE_BASE + ROPE_Q - 1)

            def attend_dve(base, last, per=0, i=None):
                head = lambda c, k=1: lin(c, GROUP * k, i)
                k = 0
                for g in range(GROUP):
                    hd = g if i is not None else g + GROUP * (KV - 1)
                    slabs = 12 if not last and g < 2 else 4
                    for m in range(slabs):
                        tail_of(base, k, per, i)
                        k += 1
                        if m == 0:
                            dve.wait_ge(qk_done, head(hd + 1))
                            V.tensor_reduce(out=rowinv, in_=banks[:, S:S + 2, :], axis=AX_X,
                                            op=ALU.max).then_inc(max_step, 1)
                            dve.wait_ge(max_step, head(2 * hd + 1, 2))
                            V.tensor_scalar(negmax, rowinv, -SCALE, None, ALU.mult).then_inc(max_step, 1)
                            if g:
                                output(hd - 1, i)
                        if m == 2:
                            dve.wait_ge(p_exp, head(2 * hd + 2, 2))
                            V.reciprocal(rowinv, rowsum).then_inc(p_norm_inv, 1)
                            dve.wait_ge(p_norm_inv, head(hd + 1))
                            for t in range(2):
                                V.tensor_scalar(prob[:, t, :], prob[:, t, :], rowinv[:, t:t + 1], None,
                                                ALU.mult).then_inc(p_norm, 1)
                        if not last:
                            if g == 1 and m == 11:
                                head_means(lin(32, 8, i))
                            if g == 2 and m == 3:
                                dve.wait_ge(head_scaled, lin(32, 8, i))
                                rotate_cos(q_tok)
                            if g == 3 and m == 1:
                                rotate_sin(q_tok)
                            if g == 3 and m == 3:
                                rotate_add(q_tok[:, :, :], lin(ROPE_BASE + 2 * (ROPE_Q - 1), ROPE_Q - 1, i))
                    dve.wait_ge(g_part, head(hd + 1))
                    V.tensor_tensor(t1[:, 0:LAT], banks[:, G, 0:LAT], t1[:, 0:LAT], ALU.add).then_inc(g_sum, 1)
                output(GROUP - 1 if i is not None else HEADS - 1, i)

            def output(hd, i):
                dve.wait_ge(g_tanh, lin(hd + 1, GROUP, i))
                dve.wait_ge(g_sum, lin(hd + 2, GROUP, i))
                V.scalar_tensor_tensor(out=t1[:, 0:LAT], in0=t2[:, 0:LAT], scalar=1.0, in1=t1[:, 0:LAT],
                                       op0=ALU.add, op1=ALU.mult).then_inc(g_silu, 1)
                dve.wait_ge(pv_done, lin(hd + 1, GROUP, i))
                dve.wait_ge(g_silu, lin(hd + 1, GROUP, i))
                V.scalar_tensor_tensor(out=t1[:, 0:LAT], in0=banks[:, PV, 0:LAT], scalar=0.5, in1=t1[:, 0:LAT],
                                       op0=ALU.mult, op1=ALU.mult).then_inc(o_mul, 1)
                dve.wait_ge(o_hi, lin(hd + 1, GROUP, i))
                at = bass.ds(i * GROUP + hd, 1) if i is not None else slice(hd, hd + 1)
                part = lambda s: o_act[:, at, s, :].rearrange("p o t -> p (o t)")
                V.tensor_tensor(part(1), t1[:, 0:LAT], part(0).bitcast(F32), ALU.subtract).then_inc(o_lo, 1)

            with dve.Fori(0, KV - 1) as i:
                attend_dve(S_ATT, False, ATT, i)
            attend_dve(S_ATTL, True)

            def out1_residual(s, jn, i=None):
                j = None if i is None else (2, i)
                at = lambda c, m: lin(m * jn + c, 2 * m, i)
                gate = mod[:, bass.ds(i * 2 + 80 + jn, 1), 0] if i is not None else mod[:, 80 + jn:81 + jn, 0]
                dve.wait_ge(y_part, at(1, 1))
                V.scalar_tensor_tensor(out=t2[:, 0:LAT], in0=banks[:, s, 0:LAT], scalar=gate,
                                       in1=t1[:, 0:LAT], op0=ALU.mult, op1=ALU.add).then_inc(y_step, 1)
                dve.wait_ge(y_step, at(1, 2))
                dve.wait_ge(x1_scaled, at(1, 1))
                V.tensor_tensor(chunk(u, j, jn)[:, 0:LAT], t2[:, 0:LAT], t3[:, 0:LAT], ALU.add).then_inc(y_step, 1)

            def out1_square(jn, i=None):
                at = lambda c, m: lin(m * jn + c, 2 * m, i)
                uj = chunk(u, None if i is None else (2, i), jn)[:, 0:LAT]
                dve.wait_ge(y_step, at(2, 2))
                if i is not None or jn:
                    dve.wait_ge(y_stats, at(0, 2))
                V.tensor_tensor(t4[:, 0:LAT], uj, uj, ALU.mult).then_inc(y_sq, 1)

            def out1_stats(jn, i=None):
                at = lambda c, m: lin(m * jn + c, 2 * m, i)
                uj = chunk(u, None if i is None else (2, i), jn)[:, 0:LAT]
                V.tensor_tensor(banks[:, SUM, 0:LAT], banks[:, SUM, 0:LAT], uj, ALU.add).then_inc(y_stats, 1)
                dve.wait_ge(y_sq, at(1, 1))
                V.tensor_tensor(banks[:, SQS, 0:LAT], banks[:, SQS, 0:LAT], t4[:, 0:LAT],
                                ALU.add).then_inc(y_stats, 1)

            def out1_dve(base, per=0, i=None, pair=0):
                for s in range(2):
                    jn = 2 * pair + s - 1
                    for k in range(4):
                        tail_of(base + 4 * s, k, per, i)
                        if i is None and jn < 0:
                            continue
                        if k == 1:
                            out1_residual(1 - s, jn, i)
                        if k == 2:
                            out1_square(jn, i)
                        if k == 3:
                            out1_stats(jn, i)

            dve.wait_ge(v_copied, 4)
            clear_stats()
            out1_dve(S_OUT1)
            with dve.Fori(1, KC // 2 - 1) as i:
                out1_dve(S_OUT1, 8, i)
            out1_dve(S_OUT1 + 8 * (KC // 2 - 1), pair=KC // 2 - 1)
            out1_residual(1, KC - 1)
            out1_square(KC - 1)
            out1_stats(KC - 1)
            ln_copies(2, LAT, lambda: dve.wait_ge(y_stats, 2 * KC))
            ln_moments(2, LAT)
            for c in range(KC):
                V.tensor_tensor(u[:, c, 0:LAT], u[:, c, 0:LAT], t1[:, 0:LAT], ALU.subtract).then_inc(fin_step, 1)
                dve.wait_ge(fin_step, 2 * c + 1)
                V.tensor_tensor(u[:, c, 0:LAT], u[:, c, 0:LAT], t2[:, 0:LAT], ALU.mult).then_inc(fin_step, 1)


def weight_slabs(w_mod, w_in_e, w_out_e, w_in_o, w_out_o):
    mods = np.concatenate([w_mod[0], w_mod[1]], axis=1)

    def job(w, col, chunks):
        rows = w[chunks[0] * P:(chunks[-1] + 1) * P, col:col + P]
        return rows.reshape(len(chunks) // 4, 4, P, P).transpose(0, 2, 1, 3).reshape(-1, P, 4 * P)

    def group(w, col):
        return w[:, col:col + 512].reshape(KC, P, 512)

    all_in = range(KC)
    out = []
    for q in range(4):
        out += [group(mods, q * 512), group(mods, D + q * 512)]
    for j in range(KC):
        parts = [job(w_in_e, at * D + j * P, all_in) for at in (0, 1, 3, 5, 6, 4)]
        mod_group = group(mods, 2 * D + j * 512)
        out.append(np.stack([mod_group[k] if n == "mod" else parts[n][k] for n, k in STEP]))
    for j in range(KC):
        out.append(job(w_in_e, 2 * D + j * P, all_in))
    for j in range(KC):
        out += [job(w_out_e, j * P, range(KC, 2 * KC)), job(w_out_e, j * P, all_in)]
    out += [group(w_in_o, 2 * D), group(w_in_o, 2 * D + KV * HD), group(w_in_o, 0)]
    for n in range(KV):
        for g in range(GROUP):
            if n + 1 < KV and g < 2:
                out.append(group(w_in_o, (n + 1) * 512)[8 * g:8 * g + 8])
            out.append(job(w_in_o, D + (n * GROUP + g) * P, all_in))
    for j in range(KC):
        out.append(job(w_out_o, j * P, all_in))
    slabs = np.concatenate(out, axis=0)
    assert slabs.shape == (START + SLABS, P, 512)
    return slabs


def rope_constants():
    tok = np.arange(LAT)
    row, col = (tok // GRID_W).astype(np.float32), (tok % GRID_W).astype(np.float32)
    axis = HD // 2
    freq = (ROPE_THETA ** (-np.arange(0, axis, 2, dtype=np.float32) / axis)).astype(np.float32)
    cos, sin = np.zeros((LAT, HD), np.float32), np.zeros((LAT, HD), np.float32)
    for n, pos in enumerate((row, col)):
        ang = pos[:, None] * freq[None, :]
        at = n * axis
        cos[:, at:at + axis] = np.concatenate([np.cos(ang), np.cos(ang)], axis=1)
        sin[:, at:at + axis] = np.concatenate([-np.sin(ang), np.sin(ang)], axis=1)
    return (t.reshape(2, P, HD).transpose(1, 0, 2).reshape(P, 2 * HD) for t in (cos, sin))


def kernel(x, c, ctx, c_ctx, w_mod, b_mod, post_ln_g, post_ln_b, w_in_e, conv_a_w, conv_a_b,
           norm_a_g, norm_a_b, conv_b_w, w_out_e, w_in_o, q_norm_g, k_norm_g, w_out_o):
    import numpy as np
    import concourse.bacc as bacc
    from concourse.bass_utils import run_bass_kernel_spmd

    def channels(a):
        a = np.asarray(a)
        return a.reshape(a.shape[0], -1, P).transpose(2, 1, 0)

    f = lambda a: channels(a).reshape(P, -1)
    tokens = np.concatenate([np.asarray(x)[0], np.asarray(ctx)[0]], axis=0)
    cond = np.concatenate([np.asarray(c), np.asarray(c_ctx)[None]], axis=0)
    params = np.concatenate([
        f(conv_a_w[0]), f(conv_a_b), f(norm_a_g), f(norm_a_b), f(conv_b_w[0]),
        channels(post_ln_g).transpose(0, 2, 1).reshape(P, -1), channels(post_ln_b).transpose(0, 2, 1).reshape(P, -1),
        channels(b_mod).transpose(0, 2, 1).reshape(P, -1), f(cond)], axis=1)
    sel = np.zeros((P, 2), np.float32)
    sel[0:2, 0] = 1
    sel[2:4, 1] = 1
    columns = np.broadcast_to(np.array([0, 1, 0], np.float32), (P, 3))
    consts = np.concatenate([np.ones((P, P), np.float32), np.eye(P, dtype=np.float32), sel, columns], axis=1)
    cos, sin = rope_constants()
    gains = [np.broadcast_to(np.asarray(g), (P, HD)) for g in (q_norm_g, k_norm_g)]
    rope = np.concatenate([cos, sin] + gains, axis=1)
    arrays = {
        "weights": weight_slabs(np.asarray(w_mod), np.asarray(w_in_e)[0], np.asarray(w_out_e)[0],
                                np.asarray(w_in_o)[0], np.asarray(w_out_o)[0]),
        "x_t": channels(tokens), "params": params, "consts": consts, "rope": rope,
    }
    arrays = {n: np.ascontiguousarray(a) for n, a in arrays.items()}
    nc = bacc.Bacc("TRN2", target_bir_lowering=False, num_devices=1)
    aps = [nc.dram_tensor(n, a.shape, F32, kind="ExternalInput").ap() for n, a in arrays.items()]
    out_t = nc.dram_tensor("out_t", (P, KC, LAT), F32, kind="ExternalOutput").ap()
    build(nc, *aps, out_t)
    r = run_bass_kernel_spmd(nc, [arrays], core_ids=[0])
    return r.results[0]["out_t"].transpose(2, 1, 0).reshape(1, LAT, D)
```

```python
from contextlib import ExitStack

import numpy as np

import concourse.bass as bass
from concourse import mybir

F32 = mybir.dt.float32
F32R = mybir.dt.float32r
ALU = mybir.AluOpType
ACT = mybir.ActivationFunctionType
AX_X = mybir.AxisListType.X

P = 128
D = 2048
KC = D // P
LAT = 256
TOK = 512
HEADS, KV, HD = 16, 4, 128
GROUP = HEADS // KV
TAPS_A, TAPS_B = 31, 3
PAD_A, PAD_B = TAPS_A // 2, TAPS_B // 2
ALPHA = (2.0 * 2) ** 0.25
LN_EPS, RMS_EPS = 1e-5, 1e-6
SCALE = HD ** -0.5
GRID_W = 64
ROPE_THETA = 10000.0

RING = 4
AHEAD = RING - 1

TURN, JOBS0 = 2 * KC, 6
START = 4 * TURN + 3 * JOBS0
START_RING = 16
NATIVE = (3, 6, 9, 12, KC - 1, 2 * KC - 1)
TURN0 = [("mod", _k) for _k in range(TURN)]
TURN1 = []
for _k in range(TURN):
    TURN1.append(("mod", _k))
    if _k in (18, 25):
        TURN1.append(("job", (_k - 18) // 7))
TURN1 += [("job", _n) for _n in range(2, JOBS0)]
UNITS0, UNITS1 = ([_e for _e in _t if _e[0] == "job" or _e[1] not in NATIVE] for _t in (TURN0, TURN1))

STEP = []
for _m in range(6 * 4):
    STEP.append((_m // 4, _m % 4))
    if 3 <= _m < 3 + KC:
        STEP.append(("mod", _m - 3))
MIX = len(STEP)
BOTH_STEPS = 12
MOD_BY_VECTOR = KC // 2
OUT0_FIRST = []
for _m in range(16):
    OUT0_FIRST.append(("job", _m))
    if 5 <= _m < 15:
        for _ in range(2 if _m % 2 or _m == 12 else 1):
            OUT0_FIRST.append(("mod", len(OUT0_FIRST) - 1 - _m))

SPLIT_AT = (0, 3, 6, 9, 12, 14, KC)

S_MIX = JOBS0 - MIX
S_AGATE = S_MIX + KC * MIX
S_OUT0 = S_AGATE + KC * 4
S_OUT0B = S_OUT0 + KC
S_K = S_OUT0B + KC * 8
S_Q0 = S_K + KC
S_V = S_Q0 + KC
S_ATT = S_V + KC
ATT = KC + GROUP * 4
S_ATTL = S_ATT + (KV - 1) * ATT
S_OUT1 = S_ATTL + GROUP * 4
SLABS = S_OUT1 + KC * 4

_sizes = [("conv_a_w", KC * TAPS_A), ("conv_a_b", KC), ("norm_a_g", KC), ("norm_a_b", KC),
          ("conv_b_w", KC * TAPS_B), ("ln_g", 2 * KC), ("ln_b", 2 * KC), ("b_mod", 96), ("cond", 2 * KC)]
COL, _at = {}, 0
for _n, _s in _sizes:
    COL[_n] = (_at, _at + _s)
    _at += _s
PARAMS = _at
CONSTS = P + P + 2 + 3
ROPE = 2 * 2 * HD + 2 * HD


def by_vector(pos, latent_only, order=STEP):
    return order[pos][0] == "mod" and (latent_only or order[pos][1] < MOD_BY_VECTOR)


def counts(pos, latent_only, order=STEP):
    n = 1
    while pos + n < len(order) and by_vector(pos + n, latent_only, order):
        n += 1
    return n


def unit(t, j):
    if isinstance(t, int) and t == 0:
        return j, j % RING
    return len(UNITS1) * t + len(UNITS0) - len(UNITS1) + j, (len(UNITS0) + j) % RING


def span(at, n=1):
    return slice(at, at + n) if isinstance(at, int) else bass.ds(at, n)


def lin(c, per=0, i=None):
    return c if i is None else i * per + c


def build(nc, weights, x_t, params, consts, rope, out_t):
    ctx = ExitStack()
    with ctx:
        def sb(name, shape, dt=F32):
            return ctx.enter_context(nc.sbuf_tensor(name, shape, dt))

        def sem(name):
            return ctx.enter_context(nc.semaphore(name))

        arena_at = -(-nc.sbuf_base // 32) * 32
        sb("arena", [P, KC * 2 * TOK])
        b_act = nc.alloc_sbuf_tensor_at("b_act", [P, KC, 2, TOK], F32R, offset=arena_at)
        att_at = arena_at + KC * TOK * 4
        k_t = nc.alloc_sbuf_tensor_at("k_t", [P, KV, TOK], F32, offset=att_at)
        v_tok = nc.alloc_sbuf_tensor_at("v_tok", [P, 4, KV * HD], F32, offset=att_at + 8192)
        q_tok = nc.alloc_sbuf_tensor_at("q_tok", [P, 2, GROUP * HD], F32, offset=att_at + 16384)
        q_t = nc.alloc_sbuf_tensor_at("q_t", [P, GROUP, LAT], F32, offset=att_at + 20480)
        prob = nc.alloc_sbuf_tensor_at("prob", [P, 2, TOK], F32, offset=att_at + 24576)
        prob_t = nc.alloc_sbuf_tensor_at("prob_t", [P, 4, LAT], F32, offset=att_at + 28672)
        k_tok = nc.alloc_sbuf_tensor_at("k_tok", [P, 4, KV * HD], F32, offset=att_at + 24576)
        start_raw = nc.alloc_sbuf_tensor_at("start_raw", [P, START_RING, TOK], F32, offset=arena_at)
        job_raw = nc.alloc_sbuf_tensor_at("job_raw", [P, JOBS0, TOK], F32, offset=att_at + 4096)
        c_row = nc.alloc_sbuf_tensor_at("c_row", [P, 4 * KC + P], F32, offset=att_at)
        b_flat = b_act[:, :, :, :].rearrange("p k s t -> p (k s t)")
        o_act = b_flat[:, 0:KC * 2 * LAT].rearrange("p (k s t) -> p k s t", k=KC, s=2)

        h = sb("h", [P, KC, 2, TOK], F32R)
        u = sb("u", [P, KC, TOK])
        w_raw = sb("w_raw", [P, RING, TOK])
        w_hi = sb("w_hi", [P, RING, TOK], F32R)
        w_lo = sb("w_lo", [P, RING, TOK], F32R)
        tmp = sb("tmp", [P, 4, TOK])
        x_in = sb("x_in", [P, 2, TOK])
        pads = sb("pads", [P, 2 * (LAT + 2 * PAD_A) + 2 * (LAT + 2 * PAD_B)])
        par = sb("par", [P, PARAMS])
        con = sb("con", [P, CONSTS])
        mod = sb("mod", [P, 96, 2])
        c4 = sb("c4", [P, 4 * KC + P], F32R)
        small = sb("small", [P, 98])
        v_stage = par[:, 0:4 * HD].rearrange("p (t d) -> p t d", t=4)

        t1, t2, t3, t4 = (tmp[:, n, :] for n in range(4))
        mod_row = t4
        mod_sum = x_in
        n_pad_a = 2 * (LAT + 2 * PAD_A)
        pad_a = pads[:, 0:n_pad_a].rearrange("p (s t) -> p s t", s=2)
        pad_b = pads[:, n_pad_a:n_pad_a + 2 * (LAT + 2 * PAD_B)].rearrange("p (s t) -> p s t", s=2)
        rope_cos = pads[:, 0:2 * HD].rearrange("p (t d) -> p t d", t=2)
        rope_sin = pads[:, 2 * HD:4 * HD].rearrange("p (t d) -> p t d", t=2)
        gains = pads[:, 4 * HD:6 * HD].rearrange("p (q d) -> p q d", q=2)
        squares = pads[:, 6 * HD:8 * HD].rearrange("p (n d) -> p n d", n=2)

        def column(name):
            a, b = COL[name]
            return par[:, a:b]

        conv_a_w, conv_a_b = column("conv_a_w"), column("conv_a_b")
        norm_a_g, norm_a_b = column("norm_a_g"), column("norm_a_b")
        conv_b_w, ln_g, ln_b = column("conv_b_w"), column("ln_g"), column("ln_b")
        b_mod = column("b_mod")
        cond = column("cond").rearrange("p (k c) -> p k c", c=2)
        ones, ident, sel = con[:, 0:P], con[:, P:2 * P], con[0:4, 2 * P:2 * P + 2]
        to_column = (con[:, 2 * P + 3:2 * P + 5], con[:, 2 * P + 2:2 * P + 4])
        cond_s = small[:, 0:2 * KC].rearrange("p (k c) -> p k c", c=2)
        neg_half = small[:, 32:40]
        alpha_g, alpha_b = small[:, 54:54 + KC], small[:, 70:70 + KC]
        ln_mean, ln_mean2, ln_var = (small[:, at:at + 4] for at in (86, 90, 94))
        sumsq = small[:, 40:48]
        negmax = small[:, 48:50]
        rowsum = small[:, 50:52]
        rowinv = small[:, 52:54]

        banks = ctx.enter_context(nc.psum_tensor("banks", [P, 8, TOK], F32))
        VAL, GLU, BX, BC, BB, MOD, SUM, SQS = range(8)
        BG = BX
        JOB0_BANK = (VAL, GLU, BX, BC, MOD, BB)
        G, Q, S, PT, PV = 0, 1, 3, 5, 7
        V_BANK = (6, 7, 0, 1)

        params_in = sem("params_in")
        consts_in = sem("consts_in")
        rope_in = sem("rope_in")
        xall_in = sem("xall_in")
        slab_landed = [sem(f"slab_landed{s}") for s in range(RING)]
        x_landed = [sem(f"x_landed{s}") for s in range(2)]
        start_landed = [sem(f"start_landed{n}") for n in range(START_RING // 4)]
        start_hi = sem("start_hi")
        start_lo = sem("start_lo")
        start_used = sem("start_used")
        job_landed = sem("job_landed")
        job_used = sem("job_used")
        hi_ready = sem("hi_ready")
        lo_ready = sem("lo_ready")
        slab_used = sem("slab_used")
        cleared = sem("cleared")
        cond_sig = sem("cond_sig")
        cond_mul = sem("cond_mul")
        cond_hi = sem("cond_hi")
        cond_lo = sem("cond_lo")
        mod_row_ready = sem("mod_row_ready")
        mod_cols_ready = sem("mod_cols_ready")
        mod_ready = sem("mod_ready")
        h_mod = sem("h_mod")
        h_hi = sem("h_hi")
        h_lo = sem("h_lo")
        glu_sig = sem("glu_sig")
        a_gated = sem("a_gated")
        bx_copied = sem("bx_copied")
        b_gated = sem("b_gated")
        conv_tap = sem("conv_tap")
        b_tap = sem("b_tap")
        b_mix = sem("b_mix")
        b_hi = sem("b_hi")
        conv_sq = sem("conv_sq")
        a_stats = sem("a_stats")
        ln_copy = sem("ln_copy")
        ln_sums = sem("ln_sums")
        ln_step = sem("ln_step")
        ln_diag = sem("ln_diag")
        ln_spread = sem("ln_spread")
        ln_sqrt = sem("ln_sqrt")
        an_step = sem("an_step")
        an_affine = sem("an_affine")
        ag_sig = sem("ag_sig")
        ag_mul = sem("ag_mul")
        act_hi = sem("act_hi")
        act_lo = sem("act_lo")
        x_scaled = sem("x_scaled")
        res_step = sem("res_step")
        res_sq = sem("res_sq")
        res_stats = sem("res_stats")
        n1_step = sem("n1_step")
        h1_mod_act = sem("h1_mod_act")
        h1_mod_dve = sem("h1_mod_dve")
        h1_hi = sem("h1_hi")
        h1_lo = sem("h1_lo")
        scale1 = sem("scale1")
        fold1 = sem("fold1")
        v_copied = sem("v_copied")
        head_squares = sem("head_squares")
        head_mean = sem("head_mean")
        head_power = sem("head_power")
        head_scaled = sem("head_scaled")
        rope_step = sem("rope_step")
        rope_done = sem("rope_done")
        k_transposed = sem("k_transposed")
        kt_ready = sem("kt_ready")
        q_transposed = sem("q_transposed")
        qt_ready = sem("qt_ready")
        v_staged = sem("v_staged")
        qk_done = sem("qk_done")
        max_step = sem("max_step")
        p_exp = sem("p_exp")
        p_norm_inv = sem("p_norm_inv")
        p_norm = sem("p_norm")
        pt_done = sem("pt_done")
        pt_copied = sem("pt_copied")
        pv_done = sem("pv_done")
        g_part = sem("g_part")
        g_sum = sem("g_sum")
        g_tanh = sem("g_tanh")
        g_silu = sem("g_silu")
        o_mul = sem("o_mul")
        o_hi = sem("o_hi")
        o_lo = sem("o_lo")
        y_part = sem("y_part")
        x1_scaled = sem("x1_scaled")
        y_step = sem("y_step")
        y_sq = sem("y_sq")
        y_stats = sem("y_stats")
        fin_step = sem("fin_step")
        fin_ready = sem("fin_ready")
        out_sem = sem("out_sem")

        def turn_landed(engine, k, i):
            q, slots = k // 4, START_RING // 4
            engine.wait_ge(start_landed[q % slots], lin(16 * (q // slots + 1), 16 * 8 // slots, i))

        ROPE_K, ROPE_T, ROPE_Q = 8, 3, 7
        ROPE_BASE = ROPE_K - 1 + ROPE_T

        def chunk(buf, j, jn):
            if j is None:
                return buf[:, jn, :]
            return buf[:, bass.ds(j[1] * j[0] + jn, 1), :].rearrange("p o t -> p (o t)")

        def per_chunk(col, j, jn):
            return col[:, jn:jn + 1] if j is None else col[:, bass.ds(j[1] * j[0] + jn, 1)]

        def rms_power(pool, n):
            pool.wait_ge(head_mean, n + 1)
            nc.gpsimd.tensor_tensor(sumsq, sumsq, neg_half, ALU.pow).then_inc(head_power, 1)

        def stage_v(pool, n):
            if n == 0:
                pool.wait_ge(v_copied, 4)
            else:
                pool.wait_ge(pv_done, GROUP * n)
            nc.gpsimd.tensor_copy(v_stage[:, :, :], v_tok[:, :, n * HD:(n + 1) * HD]).then_inc(v_staged, 1)

        block = ctx.enter_context(nc.Block())

        @block.sync
        def _(sp):
            def load_slab(base, k, per=0, i=None):
                p, slot = base + k, (base + k) % RING
                if i is not None or p >= RING:
                    sp.wait_ge(lo_ready, lin(p - RING + 1, per, i))
                at = START + p
                src = weights[at] if i is None else weights[bass.ds(i * per + at, 1)].rearrange("o p n -> p (o n)")
                sp.dma_start(w_raw[:, slot, :], src).then_inc(slab_landed[slot], 16)

            sp.dma_start(par[:, :], params).then_inc(params_in, 16)
            sp.dma_start(con[:, :], consts).then_inc(consts_in, 16)

            def load_four(t, q):
                if not isinstance(t, int) or t or q >= 4:
                    sp.wait_ge(start_used, t * TURN + 4 * q + 4)
                at = 4 * q if isinstance(t, int) and t == 0 else t * (TURN + JOBS0) - JOBS0 + 4 * q
                slot = q % (START_RING // 4)
                sp.dma_start(start_raw[:, 4 * slot:4 * slot + 4, :],
                             weights[span(at, 4)].rearrange("s p n -> p s n")).then_inc(start_landed[slot], 16)

            def load_jobs(t):
                if not isinstance(t, int):
                    sp.wait_ge(start_lo, unit(t, 0)[0])
                sp.dma_start(job_raw[:, :, :], weights[span(t * (TURN + JOBS0) + TURN - JOBS0, JOBS0)]
                             .rearrange("s p n -> p s n")).then_inc(job_landed, 16)

            def load_turn(t):
                for q in range(8):
                    load_four(t, q)
                    if isinstance(t, int) and t == 0:
                        continue
                    if q == 0:
                        load_x_chunks(t)
                    if q == 3:
                        load_jobs(t)

            def load_x_chunks(t):
                at = span(t * 4 - 4, 4)
                sp.dma_start(u[:, at, :], x_t[:, at, :]).then_inc(xall_in, 16)
            load_turn(0)
            load_turn(1)
            with sp.Fori(2, 4) as t:
                load_turn(t)
            load_x_chunks(4)
            for k in range(RING + 2):
                load_slab(0, k)
            with sp.Fori(0, (S_OUT0 - RING - 2) // RING) as i:
                for k in range(RING):
                    load_slab(RING + 2, k, RING, i)

            def load_x(j_slot, pair, i=None):
                if i is not None:
                    sp.wait_ge(x_scaled, i * 2 + j_slot - 1)
                    src = x_t[:, bass.ds(i * 2 + j_slot, 1), :].rearrange("p o n -> p (o n)")
                else:
                    src = x_t[:, 2 * pair + j_slot, :]
                sp.dma_start(x_in[:, j_slot, :], src).then_inc(x_landed[j_slot], 16)

            sp.wait_ge(mod_ready, 2 + 23)
            for s in range(2):
                load_x(s, 0)
                for k in range(KC):
                    load_slab(S_OUT0, KC * s + k)
            with sp.Fori(1, KC // 2) as i:
                for s in range(2):
                    load_x(s, 0, i)
                    for k in range(8):
                        load_slab(S_OUT0B, 8 * s + k, 16, i)
            sp.wait_ge(b_tap, TAPS_B * KC)
            sp.wait_ge(conv_tap, (TAPS_A + 1) * KC)
            sp.dma_start(pads[:, 0:ROPE], rope).then_inc(rope_in, 16)
            with sp.Fori(0, (SLABS - S_K) // RING) as i:
                for k in range(RING):
                    load_slab(S_K, k, RING, i)
            for j in range(KC):
                sp.wait_ge(fin_ready, j + 1)
                sp.dma_start(out_t[:, j, :], u[:, j, 0:LAT]).then_inc(out_sem, 16)
            sp.wait_ge(out_sem, 16 * KC)

        @block.gpsimd
        def _(pool):
            for n in range(3):
                rms_power(pool, n)
            stage_v(pool, 0)
            for n in range(1, KV):
                rms_power(pool, 2 + n)
                stage_v(pool, n)

        @block.tensor
        def _(pe):
            def slab(base, k, per=0, i=None):
                pe.wait_ge(lo_ready, lin(base + k + 1, per, i))
                return (base + k) % RING

            def job_slab(base, k, bank, act, first, last, per=0, i=None, count=1):
                s = slab(base, k, per, i)
                for kk in range(4):
                    blk = slice(kk * P, (kk + 1) * P)
                    for n, (w, half) in enumerate(((w_hi, 0), (w_hi, 1), (w_lo, 0))):
                        mm = nc.tensor.matmul(banks[:, bank, :], w[:, s, blk], act(kk, half),
                                              start=first and kk == 0 and n == 0,
                                              stop=last and kk == 3 and n == 2)
                mm.then_inc(slab_used, count)

            def job(base, bank, per=0, i=None, before=None):
                for k in range(4):
                    job_slab(base, k, bank, lambda kk, half: h[:, 4 * k + kk, half, :], k == 0, k == 3, per, i)

            def start_mod(t, k, j):
                bank, kc = (SUM, SQS)[k // KC], k % KC
                if k in NATIVE:
                    turn_landed(pe, k, t)
                    mm = nc.tensor.matmul(banks[:, bank, :], c_row[:, 4 * kc:4 * kc + P],
                                          start_raw[:, k % START_RING, :], start=False, stop=kc == KC - 1)
                else:
                    u_n, slot = unit(t, j)
                    pe.wait_ge(start_lo, u_n + 1)
                    for n, w in enumerate((w_hi, w_lo)):
                        mm = nc.tensor.matmul(banks[:, bank, :], c4[:, 4 * kc:4 * kc + P],
                                              w[:, slot, :], start=kc == 0 and n == 0, stop=False)
                mm.then_inc(start_used, 1)

            def start_job(t, job, j):
                if job == 0:
                    pe.wait_ge(h_lo, t * 4)
                u_n, slot = unit(t, j)
                pe.wait_ge(start_lo, u_n + 1)
                for kk in range(4):
                    blk = slice(kk * P, (kk + 1) * P)
                    for n, (w, half) in enumerate(((w_hi, 0), (w_hi, 1), (w_lo, 0))):
                        mm = nc.tensor.matmul(banks[:, JOB0_BANK[job], :], w[:, slot, blk],
                                              h[:, span(t * 4 - 4 + kk), half, :].rearrange("p o t -> p (o t)"),
                                              start=isinstance(t, int) and kk == 0 and n == 0, stop=False)
                mm.then_inc(job_used, 1)

            def start_turn(t):
                pe.wait_ge(mod_ready, t * 2 + 2)
                j = 0
                for kind, k in TURN0 if isinstance(t, int) and t == 0 else TURN1:
                    if kind == "job":
                        start_job(t, k, j)
                    else:
                        start_mod(t, k, j)
                    j += kind == "job" or k not in NATIVE
                    if (kind, k) == ("mod", 24):
                        mod_columns(SUM, t * 2 + 1)
                    if (kind, k) == ("job", 2):
                        mod_columns(SQS, t * 2 + 2)
                if isinstance(t, int) and t == 0:
                    mod_columns(SQS, t * 2 + 2)

            def mod_slab(base, k, kc, first, bank, per=0, i=None):
                s = slab(base, k, per, i)
                for n, w in enumerate((w_hi, w_lo)):
                    mm = nc.tensor.matmul(banks[:, bank, :], c4[:, 4 * kc:4 * kc + P], w[:, s, :],
                                          start=kc == first and n == 0, stop=kc == KC - 1 and n == 1)
                mm.then_inc(slab_used, 1)

            def mod_columns(bank, n):
                pe.wait_ge(mod_row_ready, n)
                for q in range(4):
                    mm = nc.tensor.matmul(banks[:, bank, 2 * q:2 * q + 2], mod_row[0:4, q * P:(q + 1) * P], sel,
                                          start=True, stop=True)
                mm.then_inc(mod_cols_ready, 1)

            def ln_columns(r, width):
                pe.wait_ge(ln_copy, 2 * r + 2)
                tiles = width // P
                for n, t in enumerate((t1, t2)):
                    for b in range(tiles):
                        at = n * tiles + b
                        mm = nc.tensor.matmul(banks[:, SQS, at:at + 1], t[:, b * P:(b + 1) * P], ones[:, 0:1],
                                              start=True, stop=True)
                mm.then_inc(ln_sums, 1)

            def ln_rows(r, n, width):
                pe.wait_ge(ln_diag, 2 * r + n + 1)
                nc.tensor.matmul(banks[:, (SUM, SQS)[n], 0:width], ones, (t1, t2)[n][:, 0:width],
                                 start=True, stop=True).then_inc(ln_spread, 1)

            pe.wait_ge(consts_in, 16)
            pe.wait_ge(cond_lo, 1)
            start_turn(0)
            start_turn(1)
            with pe.Fori(2, 4) as t:
                start_turn(t)
            pe.wait_ge(h_lo, KC)
            for n in range(JOBS0):
                job_slab(0, n, JOB0_BANK[n], lambda kk, half: h[:, KC - 4 + kk, half, :], False, True)
            def sum_columns(latent_only, n, sums=mod_sum):
                if not latent_only:
                    pe.wait_ge(mod_row_ready, n)
                for q in range(4):
                    blk = slice(q * P, (q + 1) * P)
                    if not latent_only:
                        nc.tensor.matmul(banks[:, MOD, 2 * q:2 * q + 2], mod_row[0:4, blk], sel,
                                         start=True, stop=False)
                    last = 0 if latent_only else 1
                    for c in range(last + 1):
                        mm = nc.tensor.matmul(banks[:, MOD, 2 * q:2 * q + 2], sums[:, c, blk], to_column[c],
                                              start=latent_only, stop=c == last)
                mm.then_inc(mod_cols_ready, 1)

            def mix_step(i, latent_only):
                for pos, (n, k) in enumerate(STEP):
                    if n == "mod":
                        if not by_vector(pos, latent_only):
                            mod_slab(S_MIX + pos, 0, k, MOD_BY_VECTOR, MOD, MIX, i)
                        continue
                    if pos == 0:
                        pe.wait_ge(a_gated, i + 1)
                        pe.wait_ge(mod_ready, i + 1 + 8)
                    elif k == 0 and n == 2:
                        pe.wait_ge(b_mix, i * 4 + 1)
                    elif k == 0 and n == 3:
                        pe.wait_ge(b_gated, i + 1)
                    elif k == 0 and n == 4:
                        pe.wait_ge(bx_copied, i + 1)
                    elif k == 0 and n == 5:
                        sum_columns(latent_only, i + 8)
                        pe.wait_ge(b_mix, i * 4 + 3)
                    job_slab(S_MIX + pos, 0, (VAL, GLU, BX, BC, BG, BB)[n],
                             lambda kk, half: h[:, 4 * k + kk, half, :], k == 0, k == 3, MIX, i,
                             counts(pos, latent_only))
            mix_step(1, False)
            with pe.Fori(2, BOTH_STEPS + 1) as i:
                mix_step(i, False)
            with pe.Fori(BOTH_STEPS + 1, KC) as i:
                mix_step(i, True)

            def agate_pair(base, per=0, i=None):
                for s in range(2):
                    if i is not None:
                        pe.wait_ge(ag_mul, i * 4 + 2 * s - 3)
                    elif s == 0:
                        pe.wait_ge(a_gated, KC + 1)
                    for k in range(4):
                        job_slab(base + 4 * s, k, s, lambda kk, half: h[:, 4 * k + kk, half, :],
                                 k == 0, k == 3, per, i)
                        if i is None and s == 0 and k == 2:
                            ln_columns(0, TOK)
                        if i is None and s == 0 and k == 3:
                            for n in range(2):
                                ln_rows(0, n, TOK)
            agate_pair(S_AGATE)
            with pe.Fori(1, KC // 2) as i:
                agate_pair(S_AGATE, 8, i)

            def out0_job_slab(base, k, s, count=1, per=0, i=None):
                act = (lambda kk, half: b_act[:, 4 * k + kk, half, :]) if k < 4 else \
                      (lambda kk, half: h[:, 4 * (k - 4) + kk, half, :])
                job_slab(base, 0, BX + s, act, k == 0, k == 7, per, i, count)

            pe.wait_ge(b_hi, KC)
            pe.wait_ge(b_mix, 4 * KC + 4)
            pe.wait_ge(b_gated, KC + 1)
            for pos, (kind, m) in enumerate(OUT0_FIRST):
                if kind == "job":
                    if 4 <= m < 8:
                        pe.wait_ge(act_lo, 4 * (m - 3))
                    out0_job_slab(S_OUT0 + pos, m % 8, m // 8, counts(pos, True, OUT0_FIRST))
            pe.wait_ge(lo_ready, S_OUT0 + len(OUT0_FIRST))
            sum_columns(True, 0, t1.unsqueeze(1))
            with pe.Fori(1, KC // 2) as i:
                for s in range(2):
                    pe.wait_ge(res_step, i * 4 + 2 * s - 2)
                    for k in range(8):
                        out0_job_slab(S_OUT0B + 8 * s + k, k, s, 1, 16, i)
            ln_columns(1, TOK)
            for n in range(2):
                ln_rows(1, n, TOK)

            def token_slab(base, k, kc, tile_banks, per=0, i=None):
                s = slab(base, k, per, i)
                for t, bank in enumerate(tile_banks):
                    tok = slice(t * P, (t + 1) * P)
                    for n, (half, w) in enumerate(((0, w_hi), (0, w_lo), (1, w_hi))):
                        mm = nc.tensor.matmul(banks[:, bank, :], h[:, kc, half, tok], w[:, s, :],
                                              start=kc == 0 and n == 0, stop=kc == KC - 1 and n == 2)
                mm.then_inc(slab_used, 1)

            pe.wait_ge(res_step, 2 * KC)
            for kc in range(KC):
                pe.wait_ge(h1_lo, kc + 1)
                token_slab(S_K, kc, kc, range(4))
            for kc in range(KC):
                token_slab(S_Q0, kc, kc, (4, 5))

            def transpose_k(n):
                pe.wait_ge(rope_done, n + 1)
                for t in range(2):
                    for kv in range(KV):
                        mm = nc.tensor.transpose(banks[:, 2 * n + 2 + t, kv * P:(kv + 1) * P],
                                                 k_tok[:, 2 * n + t, kv * HD:(kv + 1) * HD], ident)
                mm.then_inc(k_transposed, 1)

            def transpose_q(done, bank0):
                pe.wait_ge(rope_done, done)
                for t in range(2):
                    for g in range(GROUP):
                        mm = nc.tensor.transpose(banks[:, bank0 + t, g * P:(g + 1) * P],
                                                 q_tok[:, t, g * HD:(g + 1) * HD], ident)
                mm.then_inc(q_transposed, 1)

            pe.wait_ge(head_scaled, 8)
            for kc in range(KC):
                token_slab(S_V, kc, kc, V_BANK)
                if kc == 9:
                    pe.wait_ge(head_scaled, 16)
                    transpose_k(0)
                if kc == 10:
                    pe.wait_ge(head_scaled, 24)
                    transpose_k(1)
                if kc == 13:
                    pe.wait_ge(kt_ready, 2)
                    transpose_q(3, 2)
            pe.wait_ge(kt_ready, 4)
            pe.wait_ge(v_copied, 4)

            def scores(n, g):
                keys = k_t[:, n, :] if isinstance(n, int) else k_t[:, bass.ds(n, 1), :].rearrange("p o t -> p (o t)")
                for t in range(2):
                    mm = nc.tensor.matmul(banks[:, S + t, :], q_t[:, g, t * P:(t + 1) * P], keys,
                                          start=True, stop=True)
                mm.then_inc(qk_done, 1)

            def gate_slab(base, k, kk0, per, i):
                s = slab(base, k, per, i)
                for kk in range(4):
                    kc, blk = kk0 + kk, slice(kk * P, (kk + 1) * P)
                    nc.tensor.matmul(banks[:, G, :], w_hi[:, s, blk], h[:, kc, :, 0:LAT],
                                     start=kc == 0, stop=False)
                    mm = nc.tensor.matmul(banks[:, G, 0:LAT], w_lo[:, s, blk], h[:, kc, 0, 0:LAT],
                                          start=False, stop=kc == KC - 1)
                mm.then_inc(slab_used, 1)

            def attend(base, n, last, per=0, i=None):
                head = lambda c, k=1: lin(c, GROUP * k, i)
                pe.wait_ge(qt_ready, lin(2 if i is not None else 2 * KV, 2, i))
                scores(n, 0)
                k = 0
                for g in range(GROUP):
                    hd = g if i is not None else g + GROUP * (KV - 1)
                    if not last and g < 2:
                        for q in range(8):
                            token_slab(base, k, 8 * g + q, (Q, Q + 1), per, i)
                            k += 1
                    pe.wait_ge(g_sum, head(hd + 1))
                    for q in range(4):
                        gate_slab(base, k, 4 * q, per, i)
                        k += 1
                    pe.wait_ge(p_norm, head(2 * hd + 2, 2))
                    for t in range(2):
                        for c in range(4):
                            mm = nc.tensor.transpose(banks[:, PT + t, c * P:(c + 1) * P],
                                                     prob[:, t, c * P:(c + 1) * P], ident)
                    mm.then_inc(pt_done, 1)
                    if g + 1 < GROUP:
                        scores(n, g + 1)
                    elif not last:
                        transpose_q(lin(4, 1, i), Q)
                    pe.wait_ge(pt_copied, head(2 * hd + 2, 2))
                    pe.wait_ge(o_mul, head(hd + 1))
                    if g == 0:
                        pe.wait_ge(v_staged, lin(1 if i is not None else KV, 1, i))
                    for c in range(4):
                        mm = nc.tensor.matmul(banks[:, PV, 0:LAT], v_stage[:, c, :], prob_t[:, c, :],
                                              start=c == 0, stop=c == 3)
                    mm.then_inc(pv_done, 1)

            with pe.Fori(0, KV - 1) as i:
                attend(S_ATT, i, False, ATT, i)
            attend(S_ATTL, KV - 1, True)

            def out1_pair(base, per=0, i=None, first=False):
                for s in range(2):
                    if first and s == 0:
                        pe.wait_ge(o_lo, HEADS + 1)
                        pe.wait_ge(g_sum, HEADS + 1)
                    elif not first:
                        pe.wait_ge(y_step, i * 4 + 2 * s - 3 if not isinstance(i, int) else 4 * i + 2 * s - 3)
                    for k in range(4):
                        sl = slab(base + 4 * s, k, per, None if isinstance(i, int) else i)
                        for kk in range(4):
                            kc, blk = 4 * k + kk, slice(kk * P, (kk + 1) * P)
                            nc.tensor.matmul(banks[:, s, :], w_hi[:, sl, blk], o_act[:, kc, :, :],
                                             start=kc == 0, stop=False)
                            mm = nc.tensor.matmul(banks[:, s, 0:LAT], w_lo[:, sl, blk], o_act[:, kc, 0, :],
                                                  start=False, stop=kc == KC - 1)
                        mm.then_inc(slab_used, 1)
            out1_pair(S_OUT1, first=True)
            with pe.Fori(1, KC // 2 - 1) as i:
                out1_pair(S_OUT1, 8, i)
            out1_pair(S_OUT1 + 8 * (KC // 2 - 1), 0, KC // 2 - 1)
            ln_columns(2, LAT)
            for n in range(2):
                ln_rows(2, n, LAT)

        @block.scalar
        def _(act):
            def head_of(base, k, per=0, i=None, count=1):
                p = base + k + AHEAD
                if p >= SLABS:
                    return
                slot = p % RING
                act.wait_ge(slab_landed[slot], lin(16 * (p // RING + 1), 16 * per // RING, i))
                if i is not None or p >= RING:
                    act.wait_ge(slab_used, lin(p - RING + 1, per, i))
                nc.scalar.activation(w_hi[:, slot, :], w_raw[:, slot, :], ACT.Copy).then_inc(hi_ready, count)

            def copy_mod_row(bank, used, count, n):
                act.wait_ge(used, count)
                act.wait_ge(mod_cols_ready, n)
                nc.scalar.activation(mod_row[0:4, :], banks[0:4, bank, :], ACT.Copy).then_inc(mod_row_ready, 1)

            def ln_root(r, width):
                act.wait_ge(ln_step, 5 * r + 4)
                var = ln_var[:, 0:width // P]
                nc.scalar.activation(var, var, ACT.Sqrt).then_inc(ln_sqrt, 1)

            act.wait_ge(params_in, 16)
            nc.scalar.activation(cond_s, cond, ACT.Sigmoid).then_inc(cond_sig, 1)
            act.wait_ge(cond_mul, 1)
            c4v = c4[:, 0:4 * KC].rearrange("p (k c s) -> p k c s", c=2, s=2)
            nc.scalar.activation(c4v[:, :, :, 0], cond_s, ACT.Copy).then_inc(cond_hi, 1)

            def h_head(c):
                for half in range(2):
                    tok = slice(half * LAT, (half + 1) * LAT)
                    nc.scalar.activation(h[:, span(c), 0, tok].rearrange("p o t -> p (o t)"),
                                         u[:, span(c), tok].rearrange("p o t -> p (o t)"), ACT.Identity,
                                         scale=mod[:, span(c + KC), half], bias=mod[:, span(c), half]).then_inc(h_hi, 1)

            def slot_free(t, j):
                first = isinstance(t, int) and t == 0
                if j >= RING:
                    kind, k = (UNITS0 if first else UNITS1)[j - RING]
                elif first:
                    return
                else:
                    kind, k = (UNITS0 if isinstance(t, int) else UNITS1)[j - RING]
                    t = t - 1
                if kind == "job":
                    act.wait_ge(job_used, t * JOBS0 - JOBS0 + k + 1)
                else:
                    act.wait_ge(start_used, t * TURN + k + 1 + START_RING)

            def start_turn(t):
                first = isinstance(t, int) and t == 0
                for j, (kind, k) in enumerate(UNITS0 if first else UNITS1):
                    slot_free(t, j)
                    if kind == "job":
                        act.wait_ge(job_landed, t * 16)
                        raw = job_raw[:, k, :]
                    else:
                        turn_landed(act, k, t)
                        raw = start_raw[:, k % START_RING, :]
                    nc.scalar.activation(w_hi[:, unit(t, j)[1], :], raw, ACT.Copy).then_inc(start_hi, 1)
                    if (kind, k) == ("mod", 22):
                        copy_mod_row(SUM, start_used, t * TURN + KC + START_RING, t * 2 + 1)
                    if not first and j % 3 == 0 and 3 <= j <= 12:
                        if j == 3:
                            act.wait_ge(scale1, t)
                            act.wait_ge(xall_in, t * 16)
                        h_head(t * 4 - 4 + j // 3 - 1)
                copy_mod_row(SQS, start_used, t * TURN + TURN + START_RING, t * 2 + 2)

            start_turn(0)
            start_turn(1)
            with act.Fori(2, 4) as t:
                start_turn(t)
            act.wait_ge(scale1, 4)
            act.wait_ge(xall_in, 64)
            for c in range(KC - 4, KC):
                h_head(c)
            act.wait_ge(job_used, 3 * JOBS0)
            for k in range(-AHEAD, 0):
                head_of(0, k)

            for k in range(JOBS0):
                head_of(0, k)
                if k == 1:
                    act.wait_ge(slab_used, 2)
                    nc.scalar.activation(t2, banks[:, GLU, :], ACT.Sigmoid).then_inc(glu_sig, 1)
                if k == 2:
                    act.wait_ge(slab_used, 3)
                    act.wait_ge(h_lo, KC)
                    nc.scalar.activation(t1, banks[:, BX, :], ACT.Copy).then_inc(bx_copied, 1)
                if k == 4:
                    act.wait_ge(slab_used, 5)
                    act.wait_ge(a_gated, 2)
                    nc.scalar.activation(t2, banks[:, JOB0_BANK[4], :], ACT.Sigmoid).then_inc(glu_sig, 1)
            act.wait_ge(b_mix, 4 + 3)
            nc.scalar.activation(b_act[:, 0, 0, :], t1, ACT.Copy).then_inc(b_hi, 1)

            def conv_a_squares(i):
                act.wait_ge(conv_tap, i * (TAPS_A + 1) + TAPS_A + 1)
                nc.scalar.activation(t3, u[:, span(i), :].rearrange("p o t -> p (o t)"),
                                     ACT.Square).then_inc(conv_sq, 1)

            def mix_step(i, latent_only):
                for k in range(MIX):
                    pos = (k + AHEAD) % MIX
                    if not by_vector(pos, latent_only):
                        head_of(S_MIX, k, MIX, i, counts(pos, latent_only))
                    if k == 11 and isinstance(i, int):
                        conv_a_squares(i - 1)
                    if k == 11:
                        act.wait_ge(slab_used, i * MIX + S_MIX + 12)
                        act.wait_ge(b_mix, i * 4 + 2)
                        nc.scalar.activation(t2, banks[:, GLU, :], ACT.Sigmoid).then_inc(glu_sig, 1)
                    if k == 19:
                        act.wait_ge(slab_used, i * MIX + S_MIX + 20)
                        act.wait_ge(b_mix, i * 4 + 4)
                        nc.scalar.activation(t1, banks[:, BX, :], ACT.Copy).then_inc(bx_copied, 1)
                    if k == 34 and not latent_only:
                        copy_mod_row(MOD, slab_used, i * MIX + S_MIX + 35, i + 8)
                    if k == 35:
                        act.wait_ge(slab_used, i * MIX + S_MIX + 36)
                        act.wait_ge(a_gated, i + 2)
                        nc.scalar.activation(t2, banks[:, BG, :], ACT.Sigmoid).then_inc(glu_sig, 1)
                conv_a_squares(i)
                act.wait_ge(b_mix, i * 4 + 4 + 3)
                nc.scalar.activation(b_act[:, span(i), 0, :].rearrange("p o t -> p (o t)"), t1,
                                     ACT.Copy).then_inc(b_hi, 1)
            mix_step(1, False)
            with act.Fori(2, BOTH_STEPS + 1) as i:
                mix_step(i, False)
            with act.Fori(BOTH_STEPS + 1, KC) as i:
                mix_step(i, True)

            def norm_a_affine(j, jn):
                act.wait_ge(an_step, lin(3 * jn + 2, 6, None if j is None else j[1]))
                uj = chunk(u, j, jn)
                g = per_chunk(norm_a_g, j, jn)
                b = per_chunk(norm_a_b, j, jn)
                nc.scalar.activation(t3, uj, ACT.Sigmoid, scale=g, bias=b).then_inc(an_affine, 1)
                nc.scalar.activation(uj, uj, ACT.Identity, scale=g, bias=b).then_inc(an_affine, 1)

            def agate_act(base, per=0, i=None):
                for s in range(2):
                    for k in range(4):
                        head_of(base + 4 * s, k, per, i)
                        first = i is None and s == 0
                        if first and k == 1:
                            ln_root(0, TOK)
                        if k == (2 if first else 0):
                            norm_a_affine(None if i is None else (2, i), s)
                    act.wait_ge(slab_used, lin(base + 4 * s + 4, per, i))
                    if i is not None or s:
                        act.wait_ge(ag_mul, lin(2 * s, 4, i))
                    else:
                        act.wait_ge(mod_cols_ready, 24)
                    nc.scalar.activation(t4, banks[:, s, :], ACT.Sigmoid).then_inc(ag_sig, 1)

            agate_act(S_AGATE)
            with act.Fori(1, KC // 2) as i:
                agate_act(S_AGATE, 8, i)

            def out0_read(s, used, i=None):
                act.wait_ge(slab_used, used)
                act.wait_ge(x_landed[s], lin(16, 16, i))
                if i is not None or s:
                    act.wait_ge(res_step, lin(2 * s, 4, i))
                nc.scalar.activation(t3, x_in[:, s, :], ACT.Copy, scale=ALPHA).then_inc(x_scaled, 1)
                act.wait_ge(res_step, lin(2 * s + 2, 4, i))
                if i is not None or s:
                    act.wait_ge(res_stats, lin(2 * s, 4, i))
                nc.scalar.activation(t4, chunk(u, None if i is None else (2, i), s),
                                     ACT.Square).then_inc(res_sq, 1)

            for k, (kind, m) in enumerate(OUT0_FIRST):
                pos = k + AHEAD
                if pos >= len(OUT0_FIRST):
                    head_of(S_OUT0, k)
                elif not by_vector(pos, True, OUT0_FIRST):
                    head_of(S_OUT0, k, count=counts(pos, True, OUT0_FIRST))
                if kind == "job" and m < 6:
                    if m == 0:
                        act.wait_ge(slab_used, S_OUT0)
                        act.wait_ge(ag_mul, 2 * KC)
                    for c in range(SPLIT_AT[m], SPLIT_AT[m + 1]):
                        nc.scalar.activation(h[:, c, 0, :], u[:, c, :], ACT.Copy).then_inc(act_hi, 1)
                if kind == "job" and m % 8 == 7:
                    out0_read(m // 8, S_OUT0 + k + 1)
            with act.Fori(1, KC // 2) as i:
                for s in range(2):
                    for k in range(8):
                        head_of(S_OUT0B + 8 * s, k, 16, i)
                    out0_read(s, lin(S_OUT0B + 8 * s + 8, 16, i), i)
            ln_root(1, TOK)
            for c in range(KC):
                act.wait_ge(n1_step, 2 * c + 2)
                for out, ready in ((h[:, c, 0, :], h1_hi), (tmp[:, 2, :], h1_mod_act)):
                    if ready is h1_mod_act:
                        if c % 2:
                            continue
                        if c:
                            act.wait_ge(h1_lo, c - 1)
                    for half in range(2):
                        tok = slice(half * LAT, (half + 1) * LAT)
                        nc.scalar.activation(out[:, tok], u[:, c, tok], ACT.Identity,
                                             scale=mod[:, 48 + KC + c, half:half + 1],
                                             bias=mod[:, 48 + c, half:half + 1]).then_inc(ready, 1)
                if c:
                    head_of(S_K, c - 1)
            head_of(S_K, KC - 1)

            def head_sums(bank0, heads, batch, i=None):
                for n in heads:
                    if batch and n == 0:
                        act.wait_ge(head_scaled, lin(8 * batch, 8, i))
                    if batch or n > 1 or i is not None:
                        act.wait_ge(head_squares, lin(8 * batch + n - 1, 8, i))
                    nc.scalar.activation(squares[:, n % 2, :], banks[:, bank0 + n // 4, (n % 4) * HD:(n % 4 + 1) * HD],
                                         ACT.Square, accum_out=sumsq[:, n:n + 1]).then_inc(head_squares, 1)

            def head_scales(dst, bank0, heads, batch=None):
                if batch is not None:
                    act.wait_ge(head_power, batch)
                for n in heads:
                    d = slice((n % 4) * HD, (n % 4 + 1) * HD)
                    nc.scalar.activation(dst[:, n // 4, d], banks[:, bank0 + n // 4, d], ACT.Identity,
                                         scale=sumsq[:, n:n + 1]).then_inc(head_scaled, 1)

            for kc in range(KC):
                head_of(S_Q0, kc)
                if kc == 0:
                    act.wait_ge(slab_used, S_Q0)
                if kc in (0, 1):
                    head_sums(0, range(4 * kc, 4 * kc + 4), 0)
                if kc in (3, 4):
                    head_scales(k_tok[:, 0:2, :], 0, range(4 * kc - 12, 4 * kc - 8), 1)
                if kc in (6, 7):
                    head_sums(2, range(4 * kc - 24, 4 * kc - 20), 1)
                if kc in (9, 10):
                    head_scales(k_tok[:, 2:4, :], 2, range(4 * kc - 36, 4 * kc - 32), 2)

            def copy_transposed(dst, bank0, tile0, ready):
                for t in range(2):
                    tok = slice((tile0 + t) * P, (tile0 + t + 1) * P)
                    nc.scalar.activation(dst[:, :, tok], banks[:, bank0 + t, :].rearrange("p (g t) -> p g t", g=4),
                                         ACT.Copy).then_inc(ready, 1)

            for kc in range(KC):
                head_of(S_V, kc)
                if kc == 0:
                    act.wait_ge(slab_used, S_V)
                if kc in (0, 1):
                    head_sums(4, range(4 * kc, 4 * kc + 4), 2)
                if kc in (3, 4):
                    head_scales(q_tok, 4, range(4 * kc - 12, 4 * kc - 8), 3)
                if kc in (10, 11):
                    act.wait_ge(k_transposed, kc - 9)
                    copy_transposed(k_t, 2 * kc - 18, 2 * kc - 20, kt_ready)
                if kc == 14:
                    act.wait_ge(q_transposed, 1)
                    copy_transposed(q_t, 2, 0, qt_ready)
            act.wait_ge(slab_used, S_ATT)
            for t in (2, 3):
                nc.scalar.activation(v_tok[:, t, :], banks[:, V_BANK[t], :], ACT.Copy).then_inc(v_copied, 1)

            def attend_act(base, last, per=0, i=None):
                head = lambda c, k=1: lin(c, GROUP * k, i)
                k = 0
                for g in range(GROUP):
                    hd = g if i is not None else g + GROUP * (KV - 1)
                    slabs = 12 if not last and g < 2 else 4
                    for m in range(slabs):
                        head_of(base, k, per, i)
                        k += 1
                        if m == 0:
                            for t in range(2):
                                if t == 0:
                                    act.wait_ge(max_step, head(2 * hd + 2, 2))
                                nc.scalar.activation(prob[:, t, :], banks[:, S + t, :], ACT.Exp, scale=SCALE,
                                                     bias=negmax[:, t:t + 1],
                                                     accum_out=rowsum[:, t:t + 1]).then_inc(p_exp, 1)
                            if hd or i is not None:
                                if g:
                                    o_head(hd - 1, i)
                        if not last and g == 1 and m == 9:
                            act.wait_ge(slab_used, lin(base + 20, per, i))
                        if not last and g == 1 and m in (9, 10):
                            head_sums(Q, range(4 * m - 36, 4 * m - 32), 3, i)
                        if not last and g == 2 and m in (1, 2):
                            head_scales(q_tok, Q, range(4 * m - 4, 4 * m), lin(4, 1, i))
                    act.wait_ge(slab_used, lin(base + k, per, i))
                    act.wait_ge(o_lo, head(hd + 1))
                    nc.scalar.activation(t1[:, 0:LAT], banks[:, G, LAT:TOK], ACT.Copy).then_inc(g_part, 1)
                    act.wait_ge(pt_done, head(hd + 1))
                    for t in range(2):
                        nc.scalar.activation(prob_t[:, :, t * P:(t + 1) * P],
                                             banks[:, PT + t, :].rearrange("p (c t) -> p c t", c=4),
                                             ACT.Copy).then_inc(pt_copied, 1)
                    act.wait_ge(g_sum, head(hd + 2))
                    nc.scalar.activation(t2[:, 0:LAT], t1[:, 0:LAT], ACT.Tanh, scale=0.5).then_inc(g_tanh, 1)
                if not last:
                    act.wait_ge(q_transposed, lin(2, 1, i))
                    copy_transposed(q_t, Q, 0, qt_ready)
                o_head(GROUP - 1 if i is not None else HEADS - 1, i)

            def o_head(hd, i):
                act.wait_ge(o_mul, lin(hd + 2, GROUP, i))
                at = bass.ds(i * GROUP + hd, 1) if i is not None else slice(hd, hd + 1)
                nc.scalar.activation(o_act[:, at, 0, :].rearrange("p o t -> p (o t)"), t1[:, 0:LAT],
                                     ACT.Copy).then_inc(o_hi, 1)

            with act.Fori(0, KV - 1) as i:
                attend_act(S_ATT, False, ATT, i)
            attend_act(S_ATTL, True)

            def out1_read(s, jn, i=None):
                j = None if i is None else (2, i)
                at = lambda c, m: lin(m * jn + c, 2 * m, i)
                first = i is None and jn == 0
                if not first:
                    act.wait_ge(y_step, at(0, 2))
                act.wait_ge(slab_used, at(S_OUT1 + 4, 4))
                gate = mod[:, bass.ds(i * 2 + 80 + jn, 1), 0] if i is not None else mod[:, 80 + jn:81 + jn, 0]
                nc.scalar.activation(t1[:, 0:LAT], banks[:, s, LAT:TOK], ACT.Identity,
                                     scale=gate).then_inc(y_part, 1)
                uj = chunk(u, j, jn)[:, 0:LAT]
                nc.scalar.activation(t3[:, 0:LAT], uj, ACT.Identity, scale=per_chunk(alpha_g, j, jn),
                                     bias=per_chunk(alpha_b, j, jn)).then_inc(x1_scaled, 1)

            def out1_act(base, per=0, i=None, pair=0):
                for s in range(2):
                    jn = 2 * pair + s - 1
                    for k in range(4):
                        head_of(base + 4 * s, k, per, i)
                        if i is None and jn < 0:
                            continue
                        if k == 0:
                            out1_read(1 - s, jn, i)

            out1_act(S_OUT1)
            with act.Fori(1, KC // 2 - 1) as i:
                out1_act(S_OUT1, 8, i)
            out1_act(S_OUT1 + 8 * (KC // 2 - 1), pair=KC // 2 - 1)
            out1_read(1, KC - 1)
            ln_root(2, LAT)
            for c in range(KC):
                act.wait_ge(fin_step, 2 * c + 2)
                nc.scalar.activation(u[:, c, 0:LAT], u[:, c, 0:LAT], ACT.Identity, scale=ln_g[:, KC + c:KC + c + 1],
                                     bias=ln_b[:, KC + c:KC + c + 1]).then_inc(fin_ready, 1)

        @block.vector
        def _(dve):
            V = nc.vector

            def tail_of(base, k, per=0, i=None):
                p = base + k + AHEAD
                if p >= SLABS:
                    return
                slot = p % RING
                dve.wait_ge(hi_ready, lin(p + 1, per, i))
                V.tensor_tensor(w_lo[:, slot, :], w_raw[:, slot, :], w_hi[:, slot, :].bitcast(F32),
                                ALU.subtract).then_inc(lo_ready, 1)

            def mod_bias(bank, n, col, i_per=0, i=None):
                dve.wait_ge(mod_cols_ready, n)
                at = slice(col, col + 4) if i is None else span(i * i_per + col, 4)
                V.tensor_tensor(mod[:, at, :], banks[:, bank, 0:8].rearrange("p (q c) -> p q c", c=2),
                                b_mod[:, at].unsqueeze(2).to_broadcast([P, 4, 2]), ALU.add).then_inc(mod_ready, 1)

            def clear_stats():
                V.memset(banks[:, SUM, :], 0.0).then_inc(cleared, 1)
                V.memset(banks[:, SQS, :], 0.0).then_inc(cleared, 1)

            def ln_copies(r, width, stats_done):
                stats_done()
                V.tensor_copy(t1[:, 0:width], banks[:, SUM, 0:width]).then_inc(ln_copy, 1)
                V.tensor_copy(t2[:, 0:width], banks[:, SQS, 0:width]).then_inc(ln_copy, 1)

            def ln_moments(r, width):
                n = width // P
                mean, mean2, var = ln_mean[:, 0:n], ln_mean2[:, 0:n], ln_var[:, 0:n]

                def diagonals(t, col):
                    for b in range(n):
                        op = V.tensor_scalar(t[:, b * P:(b + 1) * P], ident, col[:, b:b + 1], None, ALU.mult)
                    op.then_inc(ln_diag, 1)

                dve.wait_ge(ln_sums, r + 1)
                V.tensor_scalar(mean, banks[:, SQS, 0:n], 1.0 / D, None, ALU.mult).then_inc(ln_step, 1)
                dve.wait_ge(ln_step, 5 * r + 1)
                V.tensor_tensor(mean2, mean, mean, ALU.mult).then_inc(ln_step, 1)
                dve.wait_ge(ln_step, 5 * r + 2)
                V.scalar_tensor_tensor(out=var, in0=banks[:, SQS, n:2 * n], scalar=1.0 / D, in1=mean2,
                                       op0=ALU.mult, op1=ALU.subtract).then_inc(ln_step, 1)
                dve.wait_ge(ln_step, 5 * r + 3)
                V.tensor_scalar(var, var, 0.0, LN_EPS, ALU.max, ALU.add).then_inc(ln_step, 1)
                diagonals(t1, mean)
                dve.wait_ge(ln_sqrt, r + 1)
                V.reciprocal(var, var).then_inc(ln_step, 1)
                dve.wait_ge(ln_step, 5 * r + 5)
                diagonals(t2, var)

            dve.sem_inc(start_used, START_RING)
            dve.sem_inc(mod_ready, 2)
            dve.sem_inc(a_gated, 1)
            dve.sem_inc(b_gated, 1)
            dve.sem_inc(b_mix, 4)
            dve.sem_inc(g_sum, 1)
            dve.sem_inc(o_mul, 1)
            dve.sem_inc(o_lo, 1)
            dve.sem_inc(mod_cols_ready, 1)
            V.memset(pads[:, :], 0.0).then_inc(cleared, 1)
            V.memset(c4[:, 4 * KC:].bitcast(F32), 0.0).then_inc(cleared, 1)
            V.memset(neg_half, -0.5).then_inc(cleared, 1)
            V.memset(c_row[:, :], 0.0).then_inc(cleared, 1)
            dve.wait_ge(params_in, 16)
            dve.wait_ge(cond_sig, 1)
            V.tensor_tensor(cond_s, cond_s, cond, ALU.mult).then_inc(cond_mul, 1)
            dve.wait_ge(cond_mul, 1)
            dve.wait_ge(cleared, 4)
            cr = c_row[:, 0:4 * KC].rearrange("p (k c s) -> p k c s", c=2, s=2)
            V.tensor_copy(cr[:, :, :, 0], cond_s).then_inc(cond_mul, 1)
            dve.wait_ge(cond_hi, 1)
            c4v = c4[:, 0:4 * KC].rearrange("p (k c s) -> p k c s", c=2, s=2)
            V.tensor_tensor(c4v[:, :, :, 1], cond_s, c4v[:, :, :, 0].bitcast(F32), ALU.subtract).then_inc(cond_lo, 1)

            def h_tail(c, q, t=None):
                buf = tmp[:, q % 2, :]
                for half in range(2):
                    tok = slice(half * LAT, (half + 1) * LAT)
                    V.tensor_scalar(buf[:, tok], u[:, span(c), tok].rearrange("p o t -> p (o t)"),
                                    mod[:, span(c + KC), half], mod[:, span(c), half],
                                    ALU.mult, ALU.add).then_inc(h_mod, 1)
                done = 2 * c + 2 if t is None else t * 8 - 8 + 2 * q + 2
                dve.wait_ge(h_mod, done)
                dve.wait_ge(h_hi, done)
                hq = lambda s: h[:, span(c), s, :].rearrange("p o t -> p (o t)")
                V.tensor_tensor(hq(1), buf, hq(0).bitcast(F32), ALU.subtract).then_inc(h_lo, 1)

            def start_turn(t):
                first = isinstance(t, int) and t == 0
                for j, (kind, k) in enumerate(UNITS0 if first else UNITS1):
                    u_n, slot = unit(t, j)
                    dve.wait_ge(start_hi, u_n + 1)
                    raw = job_raw[:, k, :] if kind == "job" else start_raw[:, k % START_RING, :]
                    V.tensor_tensor(w_lo[:, slot, :], raw, w_hi[:, slot, :].bitcast(F32),
                                    ALU.subtract).then_inc(start_lo, 1)
                    if (kind, k) == ("mod", 28):
                        mod_bias(SUM, t * 2 + 2, 0, 4, t)
                    if not first and j % 3 == 0 and 3 <= j <= 12:
                        if j == 3:
                            dve.wait_ge(xall_in, t * 16)
                        h_tail(t * 4 - 4 + j // 3 - 1, j // 3 - 1, t)
                mod_bias(SQS, t * 2 + 3, KC, 4, t)
                dve.wait_ge(mod_ready, t * 2 + 4)
                sc = mod[:, span(t * 4 + KC, 4), :]
                V.tensor_scalar(sc, sc, 1.0, None, ALU.add).then_inc(scale1, 1)
                dve.wait_ge(scale1, t + 1)

            start_turn(0)
            start_turn(1)
            with dve.Fori(2, 4) as t:
                start_turn(t)
            dve.wait_ge(xall_in, 64)
            for c in range(KC - 4, KC):
                h_tail(c, c % 4)
            clear_stats()
            for k in range(-AHEAD, 0):
                tail_of(0, k)

            def conv_a_tap(i, n):
                ui = u[:, span(i), :].rearrange("p o (s t) -> p (o s) t", s=2)
                src, w = pad_a[:, :, n:n + LAT], conv_a_w[:, span(i * TAPS_A + n)]
                acc = (ui, t3.rearrange("p (s t) -> p s t", s=2))[n % 2]
                if n == 0:
                    dve.wait_ge(a_gated, i + 2)
                    V.tensor_scalar(acc, src, w, conv_a_b[:, span(i)], ALU.mult, ALU.add).then_inc(conv_tap, 1)
                elif n == 1:
                    V.tensor_scalar(acc, src, w, None, ALU.mult).then_inc(conv_tap, 1)
                else:
                    dve.wait_ge(conv_tap, i * (TAPS_A + 1) + n - 1)
                    V.scalar_tensor_tensor(out=acc, in0=src, scalar=w, in1=acc, op0=ALU.mult,
                                           op1=ALU.add).then_inc(conv_tap, 1)

            def conv_a_close(i):
                ui = u[:, span(i), :].rearrange("p o t -> p (o t)")
                dve.wait_ge(conv_tap, i * (TAPS_A + 1) + TAPS_A)
                V.tensor_tensor(ui, ui, t3, ALU.add).then_inc(conv_tap, 1)

            def conv_a_sum(i):
                ui = u[:, span(i), :].rearrange("p o t -> p (o t)")
                dve.wait_ge(conv_tap, i * (TAPS_A + 1) + TAPS_A + 1)
                V.tensor_tensor(banks[:, SUM, :], banks[:, SUM, :], ui, ALU.add).then_inc(a_stats, 1)

            def conv_a_squares(i):
                dve.wait_ge(conv_sq, i + 1)
                V.tensor_tensor(banks[:, SQS, :], banks[:, SQS, :], t3, ALU.add).then_inc(a_stats, 1)

            def gate_value(i):
                dve.wait_ge(glu_sig, i * 2 + 1)
                V.tensor_tensor(pad_a[:, :, PAD_A:PAD_A + LAT], banks[:, VAL, :].rearrange("p (s t) -> p s t", s=2),
                                t2.rearrange("p (s t) -> p s t", s=2), ALU.mult).then_inc(a_gated, 1)

            t13 = t1.rearrange("p (s t) -> p s t", s=2)

            def gate_x(i):
                dve.wait_ge(bx_copied, i + 1)
                V.tensor_tensor(pad_b[:, :, PAD_B:PAD_B + LAT], banks[:, BC, :].rearrange("p (s t) -> p s t", s=2),
                                t13, ALU.mult).then_inc(b_gated, 1)

            def conv_b_tap(i, n):
                src, w = pad_b[:, :, n:n + LAT], conv_b_w[:, span(i * TAPS_B + n)]
                if n == 0:
                    dve.wait_ge(b_gated, i + 2)
                    V.tensor_scalar(t13, src, w, None, ALU.mult).then_inc(b_tap, 1)
                else:
                    dve.wait_ge(b_tap, i * TAPS_B + n)
                    V.scalar_tensor_tensor(out=t13, in0=src, scalar=w, in1=t13, op0=ALU.mult,
                                           op1=ALU.add).then_inc(b_tap, 1)

            def gate_silu(i, bank):
                dve.wait_ge(glu_sig, i * 2 + 2)
                V.tensor_tensor(t2, banks[:, bank, :], t2, ALU.mult).then_inc(b_mix, 1)

            def gate_conv_b(i):
                dve.wait_ge(b_tap, i * TAPS_B + TAPS_B)
                dve.wait_ge(b_mix, i * 4 + 4 + 1)
                V.tensor_tensor(t1, t1, t2, ALU.mult).then_inc(b_mix, 1)

            def b_output(i):
                dve.wait_ge(b_mix, i * 4 + 4 + 2)
                V.tensor_tensor(t1, banks[:, BB, :], t1, ALU.mult).then_inc(b_mix, 1)

            def b_tail(i):
                dve.wait_ge(b_hi, i + 1)
                bi = lambda s: b_act[:, span(i), s, :].rearrange("p o t -> p (o t)")
                V.tensor_tensor(bi(1), t1, bi(0).bitcast(F32), ALU.subtract).then_inc(b_mix, 1)

            for k in range(JOBS0):
                tail_of(0, k)
                if k == 2:
                    gate_value(0)
                if k == 4:
                    dve.wait_ge(slab_used, 4)
                    gate_x(0)
                for n in range((0, 0, 0, 3, 6, 8)[k], (0, 0, 3, 6, 8, 10)[k]):
                    conv_a_tap(0, n)
                if k == 5:
                    for n in range(TAPS_B):
                        conv_b_tap(0, n)
            gate_silu(0, JOB0_BANK[4])
            gate_conv_b(0)
            dve.wait_ge(slab_used, JOBS0)
            b_output(0)
            b_tail(0)
            TAPS0_AT = (10, 13, 16, 19, 21, 22, 24, 25, 27, 28, 30, 31)

            def add_mod_slab(kc, pos, latent_only, i, base=S_MIX, sums=mod_sum):
                slot = (base + pos) % RING
                dve.wait_ge(slab_landed[slot], lin(16 * ((base + pos) // RING + 1), 16 * MIX // RING, i))
                halves = 1 if latent_only else 2
                for c in range(halves):
                    if kc == 0:
                        op = V.tensor_scalar(sums[:, c, :], w_raw[:, slot, :], cond_s[:, kc, c:c + 1], None, ALU.mult)
                    else:
                        if c == 0:
                            dve.wait_ge(lo_ready, lin(base + pos - (1 if i is not None else 0), MIX, i))
                        op = V.scalar_tensor_tensor(out=sums[:, c, :], in0=w_raw[:, slot, :],
                                                    scalar=cond_s[:, kc, c:c + 1], in1=sums[:, c, :],
                                                    op0=ALU.mult, op1=ALU.add)
                op.then_inc(lo_ready, 1)

            def mix_step(i, latent_only):
                if latent_only:
                    taps_at = dict(enumerate([1, 1, 1] + [1, 1] * 6 + [0, 1, 0, 0] + [1, 1, 1, 3, 3, 2, 2, 2], 13))
                else:
                    taps_at = dict(enumerate([0, 1, 0] + [1, 2, 1, 1] * 3 + [0, 1, 1, 0] + [1, 1, 1, 2, 2, 2, 2, 2], 13))
                assert sum(taps_at.values()) == TAPS_A and max(taps_at) < MIX

                taps = iter(range(TAPS_A))
                for k in range(MIX):
                    pos = (k + AHEAD) % MIX
                    if by_vector(pos, latent_only):
                        add_mod_slab(STEP[pos][1], pos, latent_only, i)
                    else:
                        tail_of(S_MIX, k, MIX, i)
                    if k < 12 and isinstance(i, int):
                        for n in range(TAPS0_AT[k - 1] if k else 10, TAPS0_AT[k]):
                            conv_a_tap(0, n)
                    if k == 11 and isinstance(i, int):
                        conv_a_close(0)
                        conv_a_sum(0)
                    if k == 12:
                        gate_value(i)
                        if isinstance(i, int):
                            conv_a_squares(0)
                    for _ in range(taps_at.get(k, 0)):
                        conv_a_tap(i, next(taps))
                    if k == 28:
                        dve.wait_ge(slab_used, i * MIX + S_MIX + 28)
                        gate_x(i)
                    if k in (29, 30, 31):
                        conv_b_tap(i, k - 29)
                    if k == 37:
                        gate_silu(i, BG)
                    if k == 38:
                        gate_conv_b(i)
                        mod_bias(MOD, i + 9, 28, 4, i)
                conv_a_close(i)
                dve.wait_ge(slab_used, i * MIX + S_MIX + MIX)
                b_output(i)
                conv_a_sum(i)
                b_tail(i)
                conv_a_squares(i)
            mix_step(1, False)
            with dve.Fori(2, BOTH_STEPS + 1) as i:
                mix_step(i, False)
            with dve.Fori(BOTH_STEPS + 1, KC) as i:
                mix_step(i, True)

            def agate_dve(base, per=0, i=None):
                j = None if i is None else (2, i)
                for s in range(2):
                    uj = chunk(u, j, s)
                    first = i is None and s == 0
                    for k in range(4):
                        tail_of(base + 4 * s, k, per, i)
                        if first and k == 0:
                            dve.wait_ge(b_hi, KC)
                            dve.wait_ge(b_mix, 4 * KC + 4)
                            ln_copies(0, TOK, lambda: dve.wait_ge(a_stats, 2 * KC))
                        if first and k == 1:
                            ln_moments(0, TOK)
                        if k == (2 if first else 0):
                            if first:
                                dve.wait_ge(ln_spread, 2)
                            V.tensor_tensor(uj, uj, banks[:, SUM, :], ALU.subtract).then_inc(an_step, 1)
                            dve.wait_ge(an_step, lin(3 * s + 1, 6, i))
                            V.tensor_tensor(uj, uj, banks[:, SQS, :], ALU.mult).then_inc(an_step, 1)
                        if k == (3 if first else 2):
                            dve.wait_ge(an_affine, lin(2 * s + 2, 4, i))
                            V.tensor_tensor(uj, uj, t3, ALU.mult).then_inc(an_step, 1)
                    dve.wait_ge(ag_sig, lin(s + 1, 2, i))
                    V.tensor_tensor(t4, banks[:, s, :], t4, ALU.mult).then_inc(ag_mul, 1)
                    dve.wait_ge(ag_mul, lin(2 * s + 1, 4, i))
                    dve.wait_ge(an_step, lin(3 * s + 3, 6, i))
                    V.tensor_tensor(uj, uj, t4, ALU.mult).then_inc(ag_mul, 1)

            agate_dve(S_AGATE)
            with dve.Fori(1, KC // 2) as i:
                agate_dve(S_AGATE, 8, i)

            def out0_residual(s, used, i=None):
                uj = chunk(u, None if i is None else (2, i), s)
                dve.wait_ge(slab_used, used)
                dve.wait_ge(x_scaled, lin(s + 1, 2, i))
                for half in range(2):
                    tok = slice(half * LAT, (half + 1) * LAT)
                    gate = mod[:, 32 + s:33 + s, half] if i is None else mod[:, bass.ds(i * 2 + 32 + s, 1), half]
                    V.scalar_tensor_tensor(out=uj[:, tok], in0=banks[:, BX + s, tok], scalar=gate,
                                           in1=t3[:, tok], op0=ALU.mult, op1=ALU.add).then_inc(res_step, 1)
                dve.wait_ge(res_step, lin(2 * s + 2, 4, i))
                V.tensor_tensor(banks[:, SUM, :], banks[:, SUM, :], uj, ALU.add).then_inc(res_stats, 1)
                dve.wait_ge(res_sq, lin(s + 1, 2, i))
                V.tensor_tensor(banks[:, SQS, :], banks[:, SQS, :], t4, ALU.add).then_inc(res_stats, 1)

            dve.wait_ge(an_step, 3 * KC)
            clear_stats()
            dve.wait_ge(ag_mul, 2 * KC)
            for k, (kind, m) in enumerate(OUT0_FIRST):
                pos = k + AHEAD
                if pos < len(OUT0_FIRST) and by_vector(pos, True, OUT0_FIRST):
                    add_mod_slab(OUT0_FIRST[pos][1], pos, True, None, S_OUT0, t1.unsqueeze(1))
                else:
                    tail_of(S_OUT0, k)
                if kind == "job" and m < 6:
                    for c in range(SPLIT_AT[m], SPLIT_AT[m + 1]):
                        dve.wait_ge(act_hi, c + 1)
                        V.tensor_tensor(h[:, c, 1, :], u[:, c, :], h[:, c, 0, :].bitcast(F32),
                                        ALU.subtract).then_inc(act_lo, 1)
                if kind == "job" and m % 8 == 7:
                    out0_residual(m // 8, S_OUT0 + k + 1)
            mod_bias(MOD, 25, 92)
            sc1 = mod[:, 48 + KC:48 + 2 * KC, :]
            sh1 = mod[:, 48:48 + KC, :]
            dve.wait_ge(mod_ready, 2 + 24)
            V.tensor_scalar(sc1, sc1, 1.0, None, ALU.add).then_inc(scale1, 1)
            dve.wait_ge(scale1, 5)
            wide = lambda a: a.unsqueeze(2).to_broadcast([P, KC, 2])
            V.tensor_tensor(cond_s, sc1, wide(ln_b[:, 0:KC]), ALU.mult).then_inc(fold1, 1)
            V.tensor_scalar(alpha_g, ln_g[:, 0:KC], ALPHA, None, ALU.mult).then_inc(fold1, 1)
            dve.wait_ge(fold1, 2)
            V.tensor_tensor(sc1, sc1, wide(ln_g[:, 0:KC]), ALU.mult).then_inc(fold1, 1)
            V.tensor_tensor(sh1, sh1, cond_s, ALU.add).then_inc(fold1, 1)
            V.tensor_scalar(alpha_b, ln_b[:, 0:KC], ALPHA, None, ALU.mult).then_inc(fold1, 1)
            with dve.Fori(1, KC // 2) as i:
                for s in range(2):
                    for k in range(8):
                        tail_of(S_OUT0B + 8 * s, k, 16, i)
                    out0_residual(s, lin(S_OUT0B + 8 * s + 8, 16, i), i)
            ln_copies(1, TOK, lambda: dve.wait_ge(res_stats, 2 * KC))
            ln_moments(1, TOK)
            dve.wait_ge(fold1, 5)
            dve.wait_ge(ln_spread, 4)
            def h1_tail(c):
                dve.wait_ge((h1_mod_act, h1_mod_dve)[c % 2], 2 * (c // 2) + 2)
                dve.wait_ge(h1_hi, 2 * c + 2)
                V.tensor_tensor(h[:, c, 1, :], tmp[:, 2 + c % 2, :], h[:, c, 0, :].bitcast(F32),
                                ALU.subtract).then_inc(h1_lo, 1)

            for c in range(KC):
                V.tensor_tensor(u[:, c, :], u[:, c, :], banks[:, SUM, :], ALU.subtract).then_inc(n1_step, 1)
                dve.wait_ge(n1_step, 2 * c + 1)
                V.tensor_tensor(u[:, c, :], u[:, c, :], banks[:, SQS, :], ALU.mult).then_inc(n1_step, 1)
                if c:
                    h1_tail(c - 1)
                if c % 2:
                    dve.wait_ge(n1_step, 2 * c + 2)
                    for half in range(2):
                        tok = slice(half * LAT, (half + 1) * LAT)
                        V.tensor_scalar(tmp[:, 3, tok], u[:, c, tok], mod[:, 48 + KC + c, half:half + 1],
                                        mod[:, 48 + c, half:half + 1], ALU.mult, ALU.add).then_inc(h1_mod_dve, 1)
                if c > 1:
                    tail_of(S_K, c - 2)
            tail_of(S_K, KC - 2)
            h1_tail(KC - 1)
            tail_of(S_K, KC - 1)

            big, big2 = tmp[:, 2:4, :], x_in[:, :, :]
            by_head = lambda a: a.rearrange("p t (g d) -> p (t g) d", d=HD)

            def head_means(done):
                dve.wait_ge(head_squares, done)
                V.tensor_scalar(sumsq, sumsq, 1.0 / HD, RMS_EPS, ALU.mult, ALU.add).then_inc(head_mean, 1)

            def gain_k(x, done, sem_done):
                dve.wait_ge(head_scaled, done)
                V.tensor_tensor(by_head(x), by_head(x), gains[:, 1, :].unsqueeze(1).to_broadcast([P, 8, HD]),
                                ALU.mult).then_inc(sem_done, 1)

            def rotate_cos(x):
                for t in range(2):
                    per_head = lambda a: a[:, t, :].rearrange("p (g d) -> p g d", d=HD)
                    V.tensor_tensor(per_head(big), per_head(x), rope_cos[:, t, :].unsqueeze(1).to_broadcast([P, GROUP, HD]),
                                    ALU.mult).then_inc(rope_step, 1)

            def halves(a, t):
                return a[:, t, :].rearrange("p (g r f e) -> p g r f e", g=GROUP, r=2, f=2)

            def rotate_sin(x):
                for t in range(2):
                    sines = rope_sin[:, t, :].rearrange("p (r f e) -> p r f e", r=2, f=2)
                    for f in range(2):
                        V.tensor_tensor(halves(big2, t)[:, :, :, f, :], halves(x, t)[:, :, :, 1 - f, :],
                                        sines[:, :, f, :].unsqueeze(1).to_broadcast([P, GROUP, 2, 32]),
                                        ALU.mult).then_inc(rope_step, 1)

            def rotate_add(x, steps):
                dve.wait_ge(rope_step, steps)
                V.tensor_tensor(x, big, big2, ALU.add).then_inc(rope_done, 1)

            k_lat, k_ctx = k_tok[:, 0:2, :], k_tok[:, 2:4, :]
            dve.wait_ge(rope_in, 16)
            dve.wait_ge(h1_lo, KC)
            for kc in range(KC):
                tail_of(S_Q0, kc)
                if kc == 2:
                    head_means(8)
                if kc == 8:
                    head_means(16)
            for kc in range(KC):
                tail_of(S_V, kc)
                if kc == 0:
                    gain_k(k_lat, 8, rope_step)
                if kc == 1:
                    dve.wait_ge(rope_step, 1)
                    rotate_cos(k_lat)
                if kc == 2:
                    head_means(24)
                if kc == 3:
                    rotate_sin(k_lat)
                if kc == 4:
                    rotate_add(k_lat, ROPE_K - 1)
                if kc == 5:
                    gain_k(k_ctx, 16, rope_done)
                if kc == 7:
                    dve.wait_ge(rope_done, 2)
                    V.tensor_tensor(rope_cos, rope_cos, gains[:, 0, :].unsqueeze(1).to_broadcast([P, 2, HD]),
                                    ALU.mult).then_inc(rope_step, 1)
                    quarters = lambda a: a.rearrange("p t (r f e) -> p t r f e", r=2, f=2)
                    g4 = gains[:, 0, :].rearrange("p (r f e) -> p r f e", r=2, f=2)
                    for f in range(2):
                        sn = quarters(rope_sin)[:, :, :, f, :]
                        V.tensor_tensor(sn, sn, g4[:, :, 1 - f, :].unsqueeze(1).to_broadcast([P, 2, 2, 32]),
                                        ALU.mult).then_inc(rope_step, 1)
                if kc == 8:
                    dve.wait_ge(head_scaled, 24)
                    dve.wait_ge(rope_step, ROPE_BASE)
                    rotate_cos(q_tok)
                if kc == 9:
                    rotate_sin(q_tok)
                if kc == 10:
                    rotate_add(q_tok[:, :, :], ROPE_BASE + ROPE_Q - 1)
            dve.wait_ge(slab_used, S_ATT)
            for t in (0, 1):
                V.tensor_copy(v_tok[:, t, :], banks[:, V_BANK[t], :]).then_inc(v_copied, 1)

            def attend_dve(base, last, per=0, i=None):
                head = lambda c, k=1: lin(c, GROUP * k, i)
                k = 0
                for g in range(GROUP):
                    hd = g if i is not None else g + GROUP * (KV - 1)
                    slabs = 12 if not last and g < 2 else 4
                    for m in range(slabs):
                        tail_of(base, k, per, i)
                        k += 1
                        if m == 0:
                            dve.wait_ge(qk_done, head(hd + 1))
                            V.tensor_reduce(out=rowinv, in_=banks[:, S:S + 2, :], axis=AX_X,
                                            op=ALU.max).then_inc(max_step, 1)
                            dve.wait_ge(max_step, head(2 * hd + 1, 2))
                            V.tensor_scalar(negmax, rowinv, -SCALE, None, ALU.mult).then_inc(max_step, 1)
                            if g:
                                output(hd - 1, i)
                        if m == 2:
                            dve.wait_ge(p_exp, head(2 * hd + 2, 2))
                            V.reciprocal(rowinv, rowsum).then_inc(p_norm_inv, 1)
                            dve.wait_ge(p_norm_inv, head(hd + 1))
                            for t in range(2):
                                V.tensor_scalar(prob[:, t, :], prob[:, t, :], rowinv[:, t:t + 1], None,
                                                ALU.mult).then_inc(p_norm, 1)
                        if not last:
                            if g == 1 and m == 11:
                                head_means(lin(32, 8, i))
                            if g == 2 and m == 3:
                                dve.wait_ge(head_scaled, lin(32, 8, i))
                                rotate_cos(q_tok)
                            if g == 3 and m == 1:
                                rotate_sin(q_tok)
                            if g == 3 and m == 3:
                                rotate_add(q_tok[:, :, :], lin(ROPE_BASE + 2 * (ROPE_Q - 1), ROPE_Q - 1, i))
                    dve.wait_ge(g_part, head(hd + 1))
                    V.tensor_tensor(t1[:, 0:LAT], banks[:, G, 0:LAT], t1[:, 0:LAT], ALU.add).then_inc(g_sum, 1)
                output(GROUP - 1 if i is not None else HEADS - 1, i)

            def output(hd, i):
                dve.wait_ge(g_tanh, lin(hd + 1, GROUP, i))
                dve.wait_ge(g_sum, lin(hd + 2, GROUP, i))
                V.scalar_tensor_tensor(out=t1[:, 0:LAT], in0=t2[:, 0:LAT], scalar=1.0, in1=t1[:, 0:LAT],
                                       op0=ALU.add, op1=ALU.mult).then_inc(g_silu, 1)
                dve.wait_ge(pv_done, lin(hd + 1, GROUP, i))
                dve.wait_ge(g_silu, lin(hd + 1, GROUP, i))
                V.scalar_tensor_tensor(out=t1[:, 0:LAT], in0=banks[:, PV, 0:LAT], scalar=0.5, in1=t1[:, 0:LAT],
                                       op0=ALU.mult, op1=ALU.mult).then_inc(o_mul, 1)
                dve.wait_ge(o_hi, lin(hd + 1, GROUP, i))
                at = bass.ds(i * GROUP + hd, 1) if i is not None else slice(hd, hd + 1)
                part = lambda s: o_act[:, at, s, :].rearrange("p o t -> p (o t)")
                V.tensor_tensor(part(1), t1[:, 0:LAT], part(0).bitcast(F32), ALU.subtract).then_inc(o_lo, 1)

            with dve.Fori(0, KV - 1) as i:
                attend_dve(S_ATT, False, ATT, i)
            attend_dve(S_ATTL, True)

            def out1_residual(s, jn, i=None):
                j = None if i is None else (2, i)
                at = lambda c, m: lin(m * jn + c, 2 * m, i)
                gate = mod[:, bass.ds(i * 2 + 80 + jn, 1), 0] if i is not None else mod[:, 80 + jn:81 + jn, 0]
                dve.wait_ge(y_part, at(1, 1))
                V.scalar_tensor_tensor(out=t2[:, 0:LAT], in0=banks[:, s, 0:LAT], scalar=gate,
                                       in1=t1[:, 0:LAT], op0=ALU.mult, op1=ALU.add).then_inc(y_step, 1)
                dve.wait_ge(y_step, at(1, 2))
                dve.wait_ge(x1_scaled, at(1, 1))
                V.tensor_tensor(chunk(u, j, jn)[:, 0:LAT], t2[:, 0:LAT], t3[:, 0:LAT], ALU.add).then_inc(y_step, 1)

            def out1_square(jn, i=None):
                at = lambda c, m: lin(m * jn + c, 2 * m, i)
                uj = chunk(u, None if i is None else (2, i), jn)[:, 0:LAT]
                dve.wait_ge(y_step, at(2, 2))
                if i is not None or jn:
                    dve.wait_ge(y_stats, at(0, 2))
                V.tensor_tensor(t4[:, 0:LAT], uj, uj, ALU.mult).then_inc(y_sq, 1)

            def out1_stats(jn, i=None):
                at = lambda c, m: lin(m * jn + c, 2 * m, i)
                uj = chunk(u, None if i is None else (2, i), jn)[:, 0:LAT]
                V.tensor_tensor(banks[:, SUM, 0:LAT], banks[:, SUM, 0:LAT], uj, ALU.add).then_inc(y_stats, 1)
                dve.wait_ge(y_sq, at(1, 1))
                V.tensor_tensor(banks[:, SQS, 0:LAT], banks[:, SQS, 0:LAT], t4[:, 0:LAT],
                                ALU.add).then_inc(y_stats, 1)

            def out1_dve(base, per=0, i=None, pair=0):
                for s in range(2):
                    jn = 2 * pair + s - 1
                    for k in range(4):
                        tail_of(base + 4 * s, k, per, i)
                        if i is None and jn < 0:
                            continue
                        if k == 1:
                            out1_residual(1 - s, jn, i)
                        if k == 2:
                            out1_square(jn, i)
                        if k == 3:
                            out1_stats(jn, i)

            dve.wait_ge(v_copied, 4)
            clear_stats()
            out1_dve(S_OUT1)
            with dve.Fori(1, KC // 2 - 1) as i:
                out1_dve(S_OUT1, 8, i)
            out1_dve(S_OUT1 + 8 * (KC // 2 - 1), pair=KC // 2 - 1)
            out1_residual(1, KC - 1)
            out1_square(KC - 1)
            out1_stats(KC - 1)
            ln_copies(2, LAT, lambda: dve.wait_ge(y_stats, 2 * KC))
            ln_moments(2, LAT)
            dve.wait_ge(ln_spread, 6)
            for c in range(KC):
                V.tensor_tensor(u[:, c, 0:LAT], u[:, c, 0:LAT], banks[:, SUM, 0:LAT], ALU.subtract).then_inc(fin_step, 1)
                dve.wait_ge(fin_step, 2 * c + 1)
                V.tensor_tensor(u[:, c, 0:LAT], u[:, c, 0:LAT], banks[:, SQS, 0:LAT], ALU.mult).then_inc(fin_step, 1)


def weight_slabs(w_mod, w_in_e, w_out_e, w_in_o, w_out_o):
    mods = np.concatenate([w_mod[0], w_mod[1]], axis=1)

    def job(w, col, chunks):
        rows = w[chunks[0] * P:(chunks[-1] + 1) * P, col:col + P]
        return rows.reshape(len(chunks) // 4, 4, P, P).transpose(0, 2, 1, 3).reshape(-1, P, 4 * P)

    def group(w, col):
        return w[:, col:col + 512].reshape(KC, P, 512)

    all_in = range(KC)
    parts = [np.stack([job(w_in_e, at * D + j * P, all_in) for at in (0, 1, 3, 5, 6, 4)]) for j in range(KC)]
    mod_groups = [group(mods, 2 * D + j * 512) for j in range(KC)]
    out = []
    for q in range(4):
        out += [group(mods, q * 512), group(mods, D + q * 512)]
        if q:
            out.append(parts[0][:, q - 1])
    out.append(parts[0][:, 3])
    for j in range(1, KC):
        out.append(np.stack([mod_groups[j - 1][k] if n == "mod" else parts[j][n][k] for n, k in STEP]))
    for j in range(KC):
        out.append(job(w_in_e, 2 * D + j * P, all_in))
    out0 = [np.concatenate([job(w_out_e, j * P, range(KC, 2 * KC)), job(w_out_e, j * P, all_in)]) for j in range(KC)]
    out.append(np.stack([mod_groups[-1][m] if kind == "mod" else out0[m // 8][m % 8] for kind, m in OUT0_FIRST]))
    out += out0[2:]
    out += [group(w_in_o, 2 * D), group(w_in_o, 0), group(w_in_o, 2 * D + KV * HD)]
    for n in range(KV):
        for g in range(GROUP):
            if n + 1 < KV and g < 2:
                out.append(group(w_in_o, (n + 1) * 512)[8 * g:8 * g + 8])
            out.append(job(w_in_o, D + (n * GROUP + g) * P, all_in))
    for j in range(KC):
        out.append(job(w_out_o, j * P, all_in))
    slabs = np.concatenate(out, axis=0)
    assert slabs.shape == (START + SLABS, P, 512)
    return slabs


def rope_constants():
    tok = np.arange(LAT)
    row, col = (tok // GRID_W).astype(np.float32), (tok % GRID_W).astype(np.float32)
    axis = HD // 2
    freq = (ROPE_THETA ** (-np.arange(0, axis, 2, dtype=np.float32) / axis)).astype(np.float32)
    cos, sin = np.zeros((LAT, HD), np.float32), np.zeros((LAT, HD), np.float32)
    for n, pos in enumerate((row, col)):
        ang = pos[:, None] * freq[None, :]
        at = n * axis
        cos[:, at:at + axis] = np.concatenate([np.cos(ang), np.cos(ang)], axis=1)
        sin[:, at:at + axis] = np.concatenate([-np.sin(ang), np.sin(ang)], axis=1)
    return (t.reshape(2, P, HD).transpose(1, 0, 2).reshape(P, 2 * HD) for t in (cos, sin))


def kernel(x, c, ctx, c_ctx, w_mod, b_mod, post_ln_g, post_ln_b, w_in_e, conv_a_w, conv_a_b,
           norm_a_g, norm_a_b, conv_b_w, w_out_e, w_in_o, q_norm_g, k_norm_g, w_out_o):
    import numpy as np
    import concourse.bacc as bacc
    from concourse.bass_utils import run_bass_kernel_spmd

    def channels(a):
        a = np.asarray(a)
        return a.reshape(a.shape[0], -1, P).transpose(2, 1, 0)

    f = lambda a: channels(a).reshape(P, -1)
    tokens = np.concatenate([np.asarray(x)[0], np.asarray(ctx)[0]], axis=0)
    cond = np.concatenate([np.asarray(c), np.asarray(c_ctx)[None]], axis=0)
    params = np.concatenate([
        f(conv_a_w[0]), f(conv_a_b), f(norm_a_g), f(norm_a_b), f(conv_b_w[0]),
        channels(post_ln_g).transpose(0, 2, 1).reshape(P, -1), channels(post_ln_b).transpose(0, 2, 1).reshape(P, -1),
        channels(b_mod).transpose(0, 2, 1).reshape(P, -1), f(cond)], axis=1)
    sel = np.zeros((P, 2), np.float32)
    sel[0:2, 0] = 1
    sel[2:4, 1] = 1
    columns = np.broadcast_to(np.array([0, 1, 0], np.float32), (P, 3))
    consts = np.concatenate([np.ones((P, P), np.float32), np.eye(P, dtype=np.float32), sel, columns], axis=1)
    cos, sin = rope_constants()
    gains = [np.broadcast_to(np.asarray(g), (P, HD)) for g in (q_norm_g, k_norm_g)]
    rope = np.concatenate([cos, sin] + gains, axis=1)
    arrays = {
        "weights": weight_slabs(np.asarray(w_mod), np.asarray(w_in_e)[0], np.asarray(w_out_e)[0],
                                np.asarray(w_in_o)[0], np.asarray(w_out_o)[0]),
        "x_t": channels(tokens), "params": params, "consts": consts, "rope": rope,
    }
    arrays = {n: np.ascontiguousarray(a) for n, a in arrays.items()}
    nc = bacc.Bacc("TRN2", target_bir_lowering=False, num_devices=1)
    aps = [nc.dram_tensor(n, a.shape, F32, kind="ExternalInput").ap() for n, a in arrays.items()]
    out_t = nc.dram_tensor("out_t", (P, KC, LAT), F32, kind="ExternalOutput").ap()
    build(nc, *aps, out_t)
    r = run_bass_kernel_spmd(nc, [arrays], core_ids=[0])
    return r.results[0]["out_t"].transpose(2, 1, 0).reshape(1, LAT, D)
```
